# Optimizing a Trainium2 kernel written in Bass

```python
import jax, jax.numpy as jnp
from jax import lax
import numpy as np

D_MODEL = 1024
BATCH = 1
SEQ = 512
DEPTH = 2

HEAD_DIM = 64
N_HEADS_TOTAL = D_MODEL // HEAD_DIM
N_HEADS_SB = N_HEADS_TOTAL // 4
N_HEADS_MOBA = N_HEADS_TOTAL // 2
N_GROUPS_GMLP = N_HEADS_TOTAL - N_HEADS_SB - N_HEADS_MOBA
W_SB = N_HEADS_SB * HEAD_DIM
W_MOBA = N_HEADS_MOBA * HEAD_DIM
W_GMLP = N_GROUPS_GMLP * HEAD_DIM
D_MIX = W_SB + W_MOBA + W_GMLP
IN_COLS = 3 * W_SB + 3 * W_MOBA + 2 * W_GMLP

SB_Q_BLOCK = 128
MOBA_BLOCK = 256
MOBA_TOPK = 3
MOBA_Q_CHUNK = 16
GMLP_CHUNK = 128
ROPE_THETA = 500000.0
ROT_DIM = HEAD_DIM // 4

N_EXPERT_GROUPS = 4
EXPERTS_PER_GROUP = 8
N_EXPERTS = N_EXPERT_GROUPS * EXPERTS_PER_GROUP
D_EXPERT = D_MODEL // 2
MOE_TOP_K = 2
MOE_BLOCK = 256
NORM_EPS = 1e-6
OUT_SCALE = (2 * DEPTH) ** -0.5

kernel_name = "hybrid_stickbreak_moba_gmlp_hmoe"

def _rmsnorm(x, g):
    xf = x.astype(jnp.float32)
    y = xf * lax.rsqrt(jnp.mean(xf * xf, axis=-1, keepdims=True) + NORM_EPS)
    return y.astype(x.dtype) * g

def _partial_rope(x, positions):
    half = ROT_DIM // 2
    inv_freq = jnp.power(ROPE_THETA, -jnp.arange(half, dtype=jnp.float32) / half)
    ang = positions.astype(jnp.float32)[..., None] * inv_freq
    cos = jnp.cos(ang)[:, :, None, :]
    sin = jnp.sin(ang)[:, :, None, :]
    xr = x[..., :ROT_DIM].astype(jnp.float32)
    x1, x2 = xr[..., :half], xr[..., half:]
    rot = jnp.concatenate([x1 * cos - x2 * sin, x2 * cos + x1 * sin], axis=-1)
    return jnp.concatenate([rot.astype(x.dtype), x[..., ROT_DIM:]], axis=-1)

def _stick_breaking_attention(q, k, v):
    S = q.shape[1]
    scale = HEAD_DIM ** -0.5
    outs = []
    for i in range(S // SB_Q_BLOCK):
        t0 = i * SB_Q_BLOCK
        end = t0 + SB_Q_BLOCK
        z = jnp.einsum('bthd,bshd->bhts', q[:, t0:end], k[:, :end]).astype(jnp.float32) * scale
        t_pos = t0 + jnp.arange(SB_Q_BLOCK)
        s_pos = jnp.arange(end)
        causal = s_pos[None, :] < t_pos[:, None]
        log_rest = jnp.where(causal, jax.nn.log_sigmoid(-z), 0.0)
        log_after = lax.cumsum(log_rest, axis=3, reverse=True) - log_rest
        w = jnp.where(causal, jnp.exp(jax.nn.log_sigmoid(z) + log_after), 0.0)
        outs.append(jnp.einsum('bhts,bshd->bthd', w.astype(v.dtype), v[:, :end]))
    return jnp.concatenate(outs, axis=1)

def _moba_attention(q, k, v):
    B, S, H, d = q.shape
    n_blk = -(-S // MOBA_BLOCK)
    s_pad = n_blk * MOBA_BLOCK
    topk = min(MOBA_TOPK, max(n_blk - 1, 1))
    scale = HEAD_DIM ** -0.5
    neg = jnp.float32(-1e30)
    qt = q.transpose(0, 2, 1, 3)
    pad = ((0, 0), (0, 0), (0, s_pad - S), (0, 0))
    kt = jnp.pad(k.transpose(0, 2, 1, 3), pad).reshape(B, H, n_blk, MOBA_BLOCK, d)
    vt = jnp.pad(v.transpose(0, 2, 1, 3), pad).reshape(B, H, n_blk, MOBA_BLOCK, d)
    k_mean = jnp.mean(kt.astype(jnp.float32), axis=3)
    b_idx = jnp.arange(B)[:, None, None, None]
    h_idx = jnp.arange(H)[None, :, None, None]

    def chunk(c):
        t0 = c * MOBA_Q_CHUNK
        qc = lax.dynamic_slice_in_dim(qt, t0, MOBA_Q_CHUNK, axis=2)
        t_pos = t0 + jnp.arange(MOBA_Q_CHUNK)
        own = t0 // MOBA_BLOCK
        gate = jnp.einsum('bhqd,bhnd->bhqn', qc.astype(jnp.float32), k_mean)
        gate = jnp.where(jnp.arange(n_blk) < own, gate, neg)
        _, sel = lax.top_k(gate, topk)
        sel_ok = sel < own
        k_sel = kt[b_idx, h_idx, sel]
        v_sel = vt[b_idx, h_idx, sel]
        s_sel = jnp.einsum('bhqd,bhqnkd->bhqnk', qc, k_sel).astype(jnp.float32) * scale
        s_sel = jnp.where(sel_ok[..., None], s_sel, neg).reshape(B, H, MOBA_Q_CHUNK, topk * MOBA_BLOCK)
        k_own = lax.dynamic_index_in_dim(kt, own, axis=2, keepdims=False)
        v_own = lax.dynamic_index_in_dim(vt, own, axis=2, keepdims=False)
        s_own = jnp.einsum('bhqd,bhkd->bhqk', qc, k_own).astype(jnp.float32) * scale
        key_pos = own * MOBA_BLOCK + jnp.arange(MOBA_BLOCK)
        s_own = jnp.where(key_pos[None, :] <= t_pos[:, None], s_own, neg)
        p = jax.nn.softmax(jnp.concatenate([s_sel, s_own], axis=-1), axis=-1).astype(v.dtype)
        p_sel, p_own = p[..., :topk * MOBA_BLOCK], p[..., topk * MOBA_BLOCK:]
        v_sel = v_sel.reshape(B, H, MOBA_Q_CHUNK, topk * MOBA_BLOCK, d)
        return (jnp.einsum('bhqn,bhqnd->bhqd', p_sel, v_sel)
                + jnp.einsum('bhqk,bhkd->bhqd', p_own, v_own))

    o = lax.map(chunk, jnp.arange(S // MOBA_Q_CHUNK))
    return o.transpose(1, 0, 3, 2, 4).reshape(B, S, H, d)

def _gmlp_spatial_gating(u, v, g_vnorm, w_s, b_s):
    B, S, G, d = v.shape
    u = jax.nn.gelu(u)
    v = _rmsnorm(jax.nn.gelu(v), g_vnorm)
    mask = jnp.tril(jnp.ones((GMLP_CHUNK, GMLP_CHUNK), dtype=w_s.dtype))
    vc = v.reshape(B, S // GMLP_CHUNK, GMLP_CHUNK, G, d)
    mixed = jnp.einsum('gts,bcsgd->bctgd', w_s * mask, vc) + b_s.T[:, :, None]
    return u * mixed.reshape(B, S, G, d)

def _hierarchical_moe(h, w_rg, w_re, w_gate, w_up, w_down):
    T, D = h.shape
    hf = h.astype(jnp.float32)
    p_group = jax.nn.softmax(hf @ w_rg.astype(jnp.float32), axis=-1)
    g_sel = jnp.argmax(p_group, axis=-1)
    p_g = jnp.max(p_group, axis=-1)
    logit_e = (hf @ w_re.astype(jnp.float32)).reshape(T, N_EXPERT_GROUPS, EXPERTS_PER_GROUP)
    logit_e = jnp.take_along_axis(logit_e, g_sel[:, None, None], axis=1)[:, 0]
    top_p, top_i = lax.top_k(jax.nn.softmax(logit_e, axis=-1), MOE_TOP_K)
    top_p = top_p / jnp.sum(top_p, axis=-1, keepdims=True)
    expert_id = (g_sel[:, None] * EXPERTS_PER_GROUP + top_i).reshape(-1).astype(jnp.int32)
    gate_w = (p_g[:, None] * top_p).reshape(-1).astype(h.dtype)
    token_id = jnp.repeat(jnp.arange(T, dtype=jnp.int32), MOE_TOP_K)
    n_slots = T * MOE_TOP_K
    n_blocks = -(-n_slots // MOE_BLOCK) + N_EXPERTS
    order = jnp.argsort(expert_id)
    e_sorted = expert_id[order]
    counts = jnp.bincount(expert_id, length=N_EXPERTS)
    padded = (counts + MOE_BLOCK - 1) // MOE_BLOCK * MOE_BLOCK
    pad_end = jnp.cumsum(padded)
    pad_start = pad_end - padded
    start = jnp.cumsum(counts) - counts
    dest = pad_start[e_sorted] + jnp.arange(n_slots) - start[e_sorted]
    buf_tok = jnp.full((n_blocks * MOE_BLOCK,), T, dtype=jnp.int32).at[dest].set(token_id[order])
    buf_w = jnp.zeros((n_blocks * MOE_BLOCK,), h.dtype).at[dest].set(gate_w[order])
    blk_expert = jnp.minimum(
        jnp.searchsorted(pad_end, jnp.arange(n_blocks) * MOE_BLOCK, side='right'), N_EXPERTS - 1)
    h_pad = jnp.concatenate([h, jnp.zeros((1, D), h.dtype)], axis=0)

    def expert_block(args):
        tok, e = args
        xb = h_pad[tok]
        a = jax.nn.silu(xb @ w_gate[e]) * (xb @ w_up[e])
        return a @ w_down[e]

    y = lax.map(expert_block, (buf_tok.reshape(n_blocks, MOE_BLOCK), blk_expert))
    out = jnp.zeros((T + 1, D), h.dtype).at[buf_tok].add(y.reshape(-1, D) * buf_w[:, None])
    return out[:T]

def setup_inputs(seed: int = 0) -> dict:
    key = jax.random.key(seed)
    ks = jax.random.split(key, 16)
    f32 = jnp.float32
    x = jax.random.normal(ks[0], (BATCH, SEQ, D_MODEL), f32)
    start = jax.random.randint(ks[1], (BATCH, 1), 0, 4096, dtype=jnp.int32)
    positions = (start + jnp.arange(SEQ, dtype=jnp.int32)[None, :]).astype(jnp.int32)
    w_in = jax.random.normal(ks[2], (DEPTH, D_MODEL, IN_COLS), f32) * D_MODEL ** -0.5
    w_out = jax.random.normal(ks[3], (DEPTH, D_MIX, D_MODEL), f32) * D_MIX ** -0.5 * OUT_SCALE
    g_mix_norm = 1.0 + 0.02 * jax.random.normal(ks[4], (DEPTH, D_MODEL), f32)
    g_head_norm = 1.0 + 0.02 * jax.random.normal(ks[5], (DEPTH, N_HEADS_TOTAL, HEAD_DIM), f32)
    g_gmlp_vnorm = 1.0 + 0.02 * jax.random.normal(ks[6], (DEPTH, N_GROUPS_GMLP, HEAD_DIM), f32)
    w_spatial = jax.random.normal(ks[7], (DEPTH, N_GROUPS_GMLP, GMLP_CHUNK, GMLP_CHUNK), f32) * GMLP_CHUNK ** -0.5
    b_spatial = 1.0 + 0.1 * jax.random.normal(ks[8], (DEPTH, N_GROUPS_GMLP, GMLP_CHUNK), f32)
    g_ffn_norm = 1.0 + 0.02 * jax.random.normal(ks[9], (DEPTH, D_MODEL), f32)
    w_router_group = jax.random.normal(ks[10], (DEPTH, D_MODEL, N_EXPERT_GROUPS), f32) * D_MODEL ** -0.5
    w_router_expert = jax.random.normal(ks[11], (DEPTH, D_MODEL, N_EXPERTS), f32) * D_MODEL ** -0.5
    w_expert_gate = jax.random.normal(ks[12], (DEPTH, N_EXPERTS, D_MODEL, D_EXPERT), f32) * D_MODEL ** -0.5
    w_expert_up = jax.random.normal(ks[13], (DEPTH, N_EXPERTS, D_MODEL, D_EXPERT), f32) * D_MODEL ** -0.5
    w_expert_down = jax.random.normal(ks[14], (DEPTH, N_EXPERTS, D_EXPERT, D_MODEL), f32) * D_EXPERT ** -0.5 * OUT_SCALE
    g_final = 1.0 + 0.02 * jax.random.normal(ks[15], (D_MODEL,), f32)
    return {"x": x, "positions": positions, "w_in": w_in, "w_out": w_out,
            "g_mix_norm": g_mix_norm, "g_head_norm": g_head_norm, "g_gmlp_vnorm": g_gmlp_vnorm,
            "w_spatial": w_spatial, "b_spatial": b_spatial, "g_ffn_norm": g_ffn_norm,
            "w_router_group": w_router_group, "w_router_expert": w_router_expert,
            "w_expert_gate": w_expert_gate, "w_expert_up": w_expert_up,
            "w_expert_down": w_expert_down, "g_final": g_final}

def reference(x, positions, w_in, w_out, g_mix_norm, g_head_norm, g_gmlp_vnorm, w_spatial,
              b_spatial, g_ffn_norm, w_router_group, w_router_expert, w_expert_gate,
              w_expert_up, w_expert_down, g_final):
    B, S, _ = x.shape
    widths = [W_SB] * 3 + [W_MOBA] * 3 + [W_GMLP] * 2
    split_points = [int(p) for p in np.cumsum(widths)[:-1]]
    for l in range(DEPTH):
        h = _rmsnorm(x, g_mix_norm[l])
        proj = h @ w_in[l]
        qa, ka, va, qb, kb, vb, uc, vc = jnp.split(proj, split_points, axis=-1)
        o_sb = _stick_breaking_attention(qa.reshape(B, S, N_HEADS_SB, HEAD_DIM),
                                         ka.reshape(B, S, N_HEADS_SB, HEAD_DIM),
                                         va.reshape(B, S, N_HEADS_SB, HEAD_DIM))
        qb = _partial_rope(qb.reshape(B, S, N_HEADS_MOBA, HEAD_DIM), positions)
        kb = _partial_rope(kb.reshape(B, S, N_HEADS_MOBA, HEAD_DIM), positions)
        o_moba = _moba_attention(qb, kb, vb.reshape(B, S, N_HEADS_MOBA, HEAD_DIM))
        o_gmlp = _gmlp_spatial_gating(uc.reshape(B, S, N_GROUPS_GMLP, HEAD_DIM),
                                      vc.reshape(B, S, N_GROUPS_GMLP, HEAD_DIM),
                                      g_gmlp_vnorm[l], w_spatial[l], b_spatial[l])
        o = jnp.concatenate([o_sb, o_moba, o_gmlp], axis=2)
        o = _rmsnorm(o, g_head_norm[l]).reshape(B, S, D_MIX)
        x = x + o @ w_out[l]
        h = _rmsnorm(x, g_ffn_norm[l]).reshape(B * S, D_MODEL)
        y = _hierarchical_moe(h, w_router_group[l], w_router_expert[l], w_expert_gate[l],
                              w_expert_up[l], w_expert_down[l])
        x = x + y.reshape(B, S, D_MODEL)
    return _rmsnorm(x, g_final)


_drawn_inputs = setup_inputs


def setup_inputs(seed=0):
    import zlib

    import numpy as np

    out = dict(_drawn_inputs(seed))
    spreads = {}
    factors = {'g_gmlp_vnorm': 190.465,
     'b_spatial': 23.131,
     'g_final': 23.356,
     'g_head_norm': 2.797,
     'g_ffn_norm': 4.793}
    for name, (base, spread) in spreads.items():
        noise = np.random.default_rng([zlib.crc32(name.encode()), seed]).standard_normal(out[name].shape)
        drawn = base * np.exp(spread * noise) if base else spread * noise
        out[name] = __import__('jax').numpy.asarray(drawn.astype(out[name].dtype))
    for name, factor in factors.items():
        out[name] = (out[name] * factor).astype(out[name].dtype)
    return out
```

```python
import contextlib

import numpy as np
import concourse.bass as bass
from concourse import mybir

F32 = mybir.dt.float32
F32R = mybir.dt.float32r
I32 = mybir.dt.int32
U32 = mybir.dt.uint32
ACT = mybir.ActivationFunctionType
ALU = mybir.AluOpType
AX = mybir.AxisListType

P = 128
DEPTH, SEQ, D = 2, 512, 1024
NT = SEQ // P
KD = D // P
HD = 64
N_HEADS = D // HD
H_SB, H_MOBA, H_GMLP = 4, 8, 4
ROT = HD // 4
THETA = 500000.0
EPS = 1e-6
SCALE = HD ** -0.5
NEG = -1e30

CHUNK = 2048
TM_CHUNKS = 5
QK_CHUNKS = 6
OUT_CHUNKS = 4
MIX_CHUNKS = TM_CHUNKS + QK_CHUNKS + OUT_CHUNKS
RAW_SLOTS = 6

NE, NG, EPG = 32, 4, 8
FE = D // 2
KF = FE // P
ROWS_T = 96
MORE = (2 * SEQ - 2) // ROWS_T
TILES = NE + MORE
OWN_CHUNKS = 6
XS_ROWS = -(-(TILES + 1) * ROWS_T // P) * P
MAX_R = -(-SEQ // ROWS_T)

C_IDENT, C_ROT, C_NEG, C_TRI8, C_ONE8, C_LOW, C_BEFORE, C_ONES = (P * n for n in range(8))
C_FREQ = 8 * P
C_IOTA = C_FREQ + 1
C_GROUP = C_IOTA + NE
C_LIMIT = C_GROUP + NE
C_COLS = C_LIMIT + MAX_R - 1
L_GMIX, L_GHEAD, L_BS = 0, KD, 2 * KD
L_WS = L_BS + H_GMLP
L_WR = L_WS + H_GMLP * P
NR = NG + NE
L_COLS = L_WR + KD * NR

TWO_PI = (6.28125, float(np.float32(1.9350051879882812e-3)), float(np.float32(3.0199157663725e-7)))
ROUND = 12582912.0


def build(nc, x_d, pos_d, mix_d, lay_d, gv_d, gffn_d, wg_d, wu_d, wd_d, gfin_d, const_d, out_d):
    xs_d = nc.dram_tensor("expert_rows_in", (XS_ROWS, D), F32).ap()
    ys_d = nc.dram_tensor("expert_rows_out", (XS_ROWS, D), F32).ap()
    wg_v = wg_d.rearrange("l e (p k) n -> (l e) p (k n)", k=KD)
    wu_v = wu_d.rearrange("l e (p k) n -> (l e) p (k n)", k=KD)
    wd_v = wd_d.rearrange("l e (p k) n -> (l e) p (k n)", k=KF)

    with contextlib.ExitStack() as ctx:
        def sb(name, shape, dt=F32):
            return ctx.enter_context(nc.sbuf_tensor(name, shape, dt))

        def sem(name):
            return ctx.enter_context(nc.semaphore(name))

        X = sb("X", [P, NT, D])
        ROWS = sb("ROWS", [P, NT, D])
        HT_HI = sb("HT_HI", [P, KD, SEQ], F32R)
        HT_LO = sb("HT_LO", [P, KD, SEQ], F32R)
        TM = sb("TM", [P, NT, TM_CHUNKS * 256])
        RAW = sb("RAW", [P, RAW_SLOTS, CHUNK])
        W_HI = sb("W_HI", [P, 2, CHUNK], F32R)
        W_LO = sb("W_LO", [P, 2, CHUNK], F32R)
        ROPE = sb("ROPE", [P, 2, SEQ])
        QK = sb("QK", [P, 2, SEQ])
        A = sb("A", [P, NT, SEQ])
        B = sb("B", [P, NT, SEQ])
        LP = sb("LP", [P, L_COLS])
        GV = sb("GV", [P, H_GMLP * HD])
        GROW = sb("GROW", [P, D])
        C = sb("C", [P, C_COLS])
        WR_HI = sb("WR_HI", [P, KD, NR], F32R)
        WR_LO = sb("WR_LO", [P, KD, NR], F32R)
        SS = sb("SS", [P, NT * N_HEADS])
        MINUS_HALF = sb("MINUS_HALF", [P, NT * N_HEADS])
        NMAX = sb("NMAX", [P, 2, NT])
        RSUM = sb("RSUM", [P, 2, NT])
        SLOT = sb("SLOT", [P, 2, NT], U32)
        GATE = sb("GATE", [P, 2, NT])
        TILE_TAB = sb("TILE_TAB", [1, MORE + 1], I32)

        PS = ctx.enter_context(nc.psum_tensor("PS", [P, 8, 512], F32))

        XS = TM[0:ROWS_T, 0, 0:D]
        YB = TM[0:ROWS_T, 1, 0:D]
        SIL = TM[0:ROWS_T, 2, 0:FE]
        ACTED = TM[0:ROWS_T, 2, FE:2 * FE]
        XT_HI = HT_HI[:, 0:2, :].rearrange("p a n -> p (a n)")[:, 0:KD * ROWS_T].rearrange("p (k t) -> p k t", k=KD)
        XT_LO = HT_LO[:, 0:2, :].rearrange("p a n -> p (a n)")[:, 0:KD * ROWS_T].rearrange("p (k t) -> p k t", k=KD)
        AT_HI = HT_HI[:, 2, 0:KF * ROWS_T].rearrange("p (k t) -> p k t", k=KF)
        AT_LO = HT_LO[:, 2, 0:KF * ROWS_T].rearrange("p (k t) -> p k t", k=KF)
        GATHER = RAW[:, 0:4, :].rearrange("p a (b d) -> p (a b) d", d=D)
        IDENT = C[:, C_IDENT:C_IDENT + P]
        XT_PS = PS[:, 4:6, 0:KD * ROWS_T // 2].rearrange("p b (k t) -> p b k t", t=ROWS_T)
        AT_PS = PS[:, 6, 0:KF * ROWS_T].rearrange("p (k t) -> p k t", k=KF)

        def two(x):
            return x.rearrange("p (b k) t -> p b k t", b=2)


        first = sem("lay_loaded")
        lay_loaded = first
        raw_in = [sem(f"raw_in{s}") for s in range(RAW_SLOTS)]
        grow_in = sem("grow_in")
        hi_done, lo_done, mm_done = sem("hi_done"), sem("lo_done"), sem("mm_done")
        ss_done, ms_done, rstd_done = sem("ss_done"), sem("ms_done"), sem("rstd_done")
        sq_done, sq_used = sem("sq_done"), sem("sq_used")
        rows_done, tr_done, ht_hi, ht_lo = sem("rows_done"), sem("tr_done"), sem("ht_hi"), sem("ht_lo")
        tm_out = sem("tm_out")
        gelu_done, gv_ready, spatial_done, spatial_out = (
            sem("gelu_done"), sem("gv_ready"), sem("spatial_done"), sem("spatial_out"))
        qk_out, rot_done, qk_ready = sem("qk_out"), sem("rot_done"), sem("qk_ready")
        sb_z, sb_abs, sb_ln, sb_sum, sb_masked, sb_r, sb_w, sb_wm = (
            sem("sb_z"), sem("sb_abs"), sem("sb_ln"), sem("sb_sum"), sem("sb_masked"), sem("sb_r"), sem("sb_w"),
            sem("sb_wm"))
        mo_z, mo_max, mo_p, mo_t, mo_pt = sem("mo_z"), sem("mo_max"), sem("mo_p"), sem("mo_t"), sem("mo_pt")
        av_done, head_out = sem("av_done"), sem("head_out")
        x_added = sem("x_added")
        wr_hi, wr_lo, logits = sem("wr_hi"), sem("wr_lo"), sem("logits")
        gexp_in, gexp, ranks_in, ranks, slots, table = (
            sem("gexp_in"), sem("gexp"), sem("ranks_in"), sem("ranks"), sem("slots"), sem("table"))
        scattered = sem("scattered")
        xs_in, xs_t, xt_ready = sem("xs_in"), sem("xs_t"), sem("xt_ready")
        sil_done, act_done, at_t, at_hi, at_lo, xt_hi = (
            sem("sil_done"), sem("act_done"), sem("at_t"), sem("at_hi"), sem("at_lo"), sem("xt_hi"))
        y_copied, y_stored = sem("y_copied"), sem("y_stored")
        act_own, dve_own = sem("act_own"), sem("dve_own")
        last = sem("layer_sems_end")
        zeroed = sem("zeroed")
        scatter_in = sem("scatter_in")
        gather_in = sem("gather_in")
        consts_in, setup, out_stored, gfin_in = sem("consts_in"), sem("setup"), sem("out_stored"), sem("gfin_in")
        fin_ss, fin_ms, fin_rstd, fin_rows = sem("fin_ss"), sem("fin_ms"), sem("fin_rstd"), sem("fin_rows")

        class Own:

            def __init__(self, eng, s):
                self.eng, self.s, self.base, self.n = eng, s, 0, 0

            def __call__(self, ins):
                self.n += 1
                ins.then_inc(self.s, 1)
                self.eng.wait_ge(self.s, self.base + self.n)

            def at(self, start, i, per):
                self.base, self.n = start + i * per, 0

        def product3(pe, out, a_hi, a_lo, b_hi, b_lo, start, stop):
            pe.matmul(out, a_hi, b_hi, start=start, stop=False)
            pe.matmul(out, a_hi, b_lo, start=False, stop=False)
            return pe.matmul(out, a_lo, b_hi, start=False, stop=stop)

        with nc.Block() as block:
            @block.sync
            def _(sp):
                sp.dma_start(A[:, 0, :].bitcast(I32), pos_d.partition_broadcast(P)).then_inc(consts_in, 16)
                sp.dma_start(C[:], const_d).then_inc(consts_in, 16)
                sp.dma_start(X[:], x_d.rearrange("(i p) d -> p i d", p=P)).then_inc(consts_in, 16)
                sp.wait_ge(setup, 1)
                for n in range(XS_ROWS // P):
                    sp.dma_start(xs_d[n * P:(n + 1) * P, :], GROW[:]).then_inc(zeroed, 16)
                for n in range(NE * ROWS_T // P, XS_ROWS // P):
                    sp.dma_start(ys_d[n * P:(n + 1) * P, :], GROW[:]).then_inc(zeroed, 16)
                sp.wait_ge(consts_in, 48)
                sp.wait_ge(zeroed, (2 * XS_ROWS - NE * ROWS_T) // P * 16)

            @block.gpsimd
            def _(pool):
                pool.memset(GROW[:], 0.0).then_inc(setup, 1)
                pool.memset(MINUS_HALF[:], -0.5)

            @block.vector
            def _(dve):
                n = [1]

                def own(ins):
                    n[0] += 1
                    ins.then_inc(setup, 1)
                    dve.wait_ge(setup, n[0])

                ang, turns, cosx = A[:, 1, :], A[:, 2, :], A[:, 3, :]
                dve.wait_ge(consts_in, 48)
                dve.wait_ge(setup, 1)
                own(dve.tensor_copy(B[:, 0, :], A[:, 0, :].bitcast(I32)))
                own(dve.tensor_scalar(ang, B[:, 0, :], C[:, C_FREQ:C_FREQ + 1], None, ALU.mult))
                own(dve.tensor_scalar(turns, ang, float(1 / (2 * np.pi)), ROUND, ALU.mult, ALU.add))
                own(dve.tensor_scalar(turns, turns, -ROUND, None, ALU.add))
                for part in TWO_PI:
                    own(dve.scalar_tensor_tensor(ang, turns, -part, ang, ALU.mult, ALU.add))
                own(dve.tensor_scalar(ang, ang, float(np.float32(3.1415925)), float(np.float32(-3.1415925)), ALU.min,
                                      ALU.max))
                own(dve.tensor_scalar(cosx, ang, -1.0, None, ALU.mult))
                own(dve.tensor_tensor(cosx, cosx, ang, ALU.max))
                own(dve.tensor_scalar(cosx, cosx, -1.0, float(np.pi / 2), ALU.mult, ALU.add))

            @block.scalar
            def _(act):
                act.wait_ge(setup, 12)
                act.activation(ROPE[:, 0, :], A[:, 3, :], ACT.Sin)
                act.activation(ROPE[:, 1, :], A[:, 1, :], ACT.Sin)

        with nc.Fori(0, DEPTH) as l:
            with nc.Block() as block:
                @block.sync
                def _(sp):
                    sp.dma_start(LP[:], lay_d[bass.ds(l, 1), :, :].rearrange("l p n -> (l p) n")).then_inc(lay_loaded, 16)
                    sp.dma_start(GV[:], gv_d[bass.ds(l, 1), :].rearrange("l n -> (l n)").partition_broadcast(P)) \
                      .then_inc(lay_loaded, 16)
                    sp.dma_start(GROW[:], gffn_d[bass.ds(l, 1), :].rearrange("l n -> (l n)").partition_broadcast(P)) \
                      .then_inc(grow_in, 16)
                    for c in range(MIX_CHUNKS):
                        if c >= RAW_SLOTS:
                            sp.wait_ge(lo_done, c - RAW_SLOTS + 1)
                        sp.dma_start(RAW[:, c % RAW_SLOTS, :],
                                     mix_d[bass.ds(l * MIX_CHUNKS + c, 1), :, :].rearrange("c p n -> (c p) n")) \
                          .then_inc(raw_in[c % RAW_SLOTS], 16)

                    def expert(j, e):
                        w = (wg_v, wg_v, wu_v, wu_v, wd_v, wd_v)[j]
                        return w[bass.ds(e, 1), :, (j % 2) * CHUNK:(j % 2 + 1) * CHUNK].rearrange("e p n -> (e p) n")

                    def load_rows(t):
                        sp.dma_start(XS, xs_d[bass.ds(t * ROWS_T, ROWS_T), :]).then_inc(xs_in, 16)

                    def load_tile(t, e, at_start=False):
                        for j in range(OWN_CHUNKS):
                            if at_start:
                                sp.wait_ge(lo_done, min(MIX_CHUNKS - 3 + j + 1, MIX_CHUNKS))
                            else:
                                sp.wait_ge(lo_done, t * OWN_CHUNKS + (MIX_CHUNKS + j + 1 - OWN_CHUNKS))
                            sp.dma_start(RAW[:, j, :], expert(j, e)).then_inc(raw_in[j], 16)

                    load_tile(0, l * NE, at_start=True)
                    sp.wait_ge(scatter_in, l * (2 * NT * 16) + 2 * NT * 16)
                    sp.wait_ge(logits, 1)
                    load_rows(0)
                    sp.wait_ge(xs_t, 1)
                    load_rows(1)
                    with sp.Fori(1, NE) as t:
                        load_tile(t, l * NE + t)
                        sp.wait_ge(xs_t, t + 1)
                        load_rows(t + 1)
                    sp.wait_ge(table, 1)
                    n_more = sp.value_load(TILE_TAB[0:1, MORE:MORE + 1], min_val=0, max_val=MORE)
                    with sp.If(n_more > 0):
                        with sp.Fori(NE, TILES) as t:
                            e = sp.value_load(TILE_TAB[0:1, bass.ds(t - NE, 1)], min_val=0, max_val=NE - 1)
                            load_tile(t, l * NE + e)
                            sp.wait_ge(xs_t, t + 1)
                            load_rows(t + 1)
                        sp.wait_ge(xs_in, 16 * (TILES + 1))
                    sp.wait_ge(xs_in, 16 * (NE + 1))

                @block.gpsimd
                def _(pool):
                    def root(n, cols):
                        pool.wait_ge(ms_done, n)
                        pool.tensor_tensor(SS[:, 0:cols], SS[:, 0:cols], MINUS_HALF[:, 0:cols], ALU.pow) \
                            .then_inc(rstd_done, 1)

                    root(1, NT)
                    root(2, NT * H_GMLP)
                    for h in range(H_SB):
                        for n, j in enumerate(reversed(range(NT))):
                            pool.wait_ge(sb_sum, NT * h + n + 1)
                            pool.affine_select(out=A[:, j, 0:P], in_=A[:, j, 0:P], compare_op=ALU.is_gt, fill=0.0,
                                               base=0, pattern=[[1, P]], channel_multiplier=-1).then_inc(sb_masked, 1)
                        for n, j in enumerate(reversed(range(NT))):
                            pool.wait_ge(sb_w, NT * h + n + 1)
                            pool.affine_select(out=B[:, j, 0:P], in_=B[:, j, 0:P], compare_op=ALU.is_gt, fill=0.0,
                                               base=0, pattern=[[1, P]], channel_multiplier=-1).then_inc(sb_wm, 1)
                    root(3, NT * N_HEADS)
                    root(4, NT)
                    pool.wait_ge(rows_done, 3 * NT)
                    pool.wait_ge(slots, 1)
                    for s in range(2):
                        for i in range(NT):
                            pool.indirect_dma_start(
                                out=xs_d, out_offset=bass.IndirectOffsetOnAxis(SLOT[:, s, i:i + 1], 0),
                                in_=ROWS[:, i, :], in_offset=None).then_inc(scatter_in, 16)
                    pool.wait_ge(y_stored, 16 * (NE + 1))
                    pool.wait_ge(table, 1)
                    n_more = pool.value_load(TILE_TAB[0:1, MORE:MORE + 1], min_val=0, max_val=MORE)
                    with pool.If(n_more > 0):
                        pool.wait_ge(y_stored, 16 * (TILES + 1))
                    for i in range(NT):
                        for s in range(2):
                            pool.indirect_dma_start(
                                out=GATHER[:, 2 * i + s, :], out_offset=None, in_=ys_d,
                                in_offset=bass.IndirectOffsetOnAxis(SLOT[:, s, i:i + 1], 0)).then_inc(gather_in, 16)

                @block.scalar
                def _(act):
                    own = Own(act, act_own)

                    def copy(out, in_, **kw):
                        return act.activation(out, in_, ACT.Copy, **kw)

                    def split_hi(c):
                        act.wait_ge(raw_in[c % RAW_SLOTS], 16 * (c // RAW_SLOTS + 1))
                        if c >= 2:
                            act.wait_ge(mm_done, c - 1)
                        copy(W_HI[:, c % 2, :], RAW[:, c % RAW_SLOTS, :]).then_inc(hi_done, 1)

                    def squares():
                        for i in range(NT):
                            act.activation(ROWS[:, i, :], X[:, i, :], ACT.Square, accum_out=SS[:, i:i + 1]) \
                               .then_inc(ss_done, 1)

                    def transposed_hi(s, gains):
                        for k in range(KD):
                            act.wait_ge(tr_done, KD * s + k + 1)
                            kw = {} if gains is None else {"scale": LP[:, gains + k:gains + k + 1]}
                            copy(HT_HI[:, k, :], PS[:, k % 2, :], **kw).then_inc(ht_hi, 1)

                    squares()
                    act.wait_ge(lay_loaded, 32)
                    split_hi(0)
                    split_hi(1)
                    transposed_hi(0, L_GMIX)
                    for c in range(TM_CHUNKS):
                        act.wait_ge(mm_done, c + 1)
                        b = 2 * (c % 2)
                        copy(TM[:, :, c * 256:(c + 1) * 256],
                             PS[:, b:b + 2, :].rearrange("p b (i n) -> p (b i) n", n=256)).then_inc(tm_out, 1)
                        split_hi(c + 2)
                    act.wait_ge(tm_out, TM_CHUNKS)
                    act.activation(TM[:, :, 768:1280], TM[:, :, 768:1280], ACT.Gelu_apprx_tanh).then_inc(gelu_done, 1)

                    def q_and_k(pair, mm, dest):
                        act.wait_ge(mm_done, mm)
                        copy(dest, PS[:, 0:2, :]).then_inc(qk_out, 1)

                    for pair in range(2):
                        q_and_k(pair, TM_CHUNKS + pair + 1, QK[:])
                        if not pair:
                            split_hi(TM_CHUNKS + 2)
                        for h in (2 * pair, 2 * pair + 1):
                            if h:
                                act.wait_ge(av_done, h)
                            else:
                                act.wait_ge(gv_ready, 1)
                            for n, j in enumerate(reversed(range(NT))):
                                w = SEQ - P * j
                                act.wait_ge(sb_z, NT * h + n + 1)
                                act.activation(B[:, j, 0:w], PS[:, 2 + j, 0:w], ACT.Abs, scale=SCALE).then_inc(sb_abs, 1)
                            for n, j in enumerate(reversed(range(NT))):
                                w = SEQ - P * j
                                act.wait_ge(sb_abs, NT * h + n + 1)
                                own(act.activation(B[:, j, 0:w], B[:, j, 0:w], ACT.Exp, scale=-1.0))
                                act.activation(B[:, j, 0:w], B[:, j, 0:w], ACT.Ln, bias=1.0).then_inc(sb_ln, 1)
                            for n, j in enumerate(reversed(range(NT))):
                                w = SEQ - P * j
                                act.wait_ge(sb_r, NT * h + n + 1)
                                act.wait_ge(sb_sum, NT * h + n + 1)
                                act.activation(B[:, j, 0:w], PS[:, 2 + j, 0:w], ACT.Exp, scale=SCALE).then_inc(sb_w, 1)

                    for slot in range(2, RAW_SLOTS):
                        act.wait_ge(raw_in[slot], 32)
                    with act.Fori(0, 2) as r:
                        for half in range(2):
                            c = TM_CHUNKS + 2 + half
                            act.wait_ge(mm_done, 2 * r + c + 1)
                            act.wait_ge(av_done, 4 * r + H_SB + 2 * half)
                            copy(B[:, 0:2, :], PS[:, 0:2, :]).then_inc(qk_out, 1)
                            act.wait_ge(mm_done, 2 * r + c)
                            copy(W_HI[:, (c + 1) % 2, :], RAW[:, bass.ds(2 * r + 2 + half, 1), :]
                                 .rearrange("p a n -> p (a n)")).then_inc(hi_done, 1)
                            for h in range(2):
                                n = 4 * r + 2 * half + h
                                act.wait_ge(mo_max, n + 1)
                                act.wait_ge(av_done, n + H_SB)
                                for i in range(NT):
                                    w = P * (i + 1)
                                    act.activation(A[:, i, 0:w], PS[:, 2 + i, 0:w], ACT.Exp, bias=NMAX[:, 1, i:i + 1],
                                                   scale=SCALE, accum_out=RSUM[:, 0, i:i + 1]).then_inc(mo_p, 1)
                    split_hi(MIX_CHUNKS - 3)
                    act.wait_ge(av_done, H_SB + H_MOBA)
                    act.wait_ge(head_out, H_SB + H_MOBA)
                    act.wait_ge(spatial_out, H_GMLP)
                    for i in range(NT):
                        if i >= 2:
                            act.wait_ge(sq_used, i - 1)
                        act.activation(A[:, 2 * (i % 2):2 * (i % 2) + 2, :].rearrange("p a n -> p (a n)"), ROWS[:, i, :],
                                       ACT.Square).then_inc(sq_done, 1)
                    transposed_hi(1, L_GHEAD)
                    split_hi(MIX_CHUNKS - 2)
                    split_hi(MIX_CHUNKS - 1)
                    act.wait_ge(x_added, OUT_CHUNKS)
                    squares()
                    copy(WR_HI[:], LP[:, L_WR:L_COLS].rearrange("p (k n) -> p k n", n=NR)).then_inc(wr_hi, 1)

                    def split_own(t, j, begin=False):
                        act.wait_ge(raw_in[j], 16 * (t + (4 if j < 3 else 3)))
                        act.wait_ge(mm_done, MIX_CHUNKS if begin else t * OWN_CHUNKS + (MIX_CHUNKS + j - 1))
                        copy(W_HI[:, j % 2, :], RAW[:, j, :]).then_inc(hi_done, 1)

                    transposed_hi(2, None)
                    act.wait_ge(gexp_in, 1)
                    act.activation(A[:, 0, 0:NT * NG], A[:, 0, 0:NT * NG], ACT.Exp).then_inc(gexp, 1)
                    act.wait_ge(gexp_in, 2)
                    act.activation(GATE[:, 1, :], GATE[:, 1, :], ACT.Exp).then_inc(gexp, 1)

                    act.sem_inc(y_stored, 16)

                    def rows_hi(t):
                        act.wait_ge(xs_t, t + 1)
                        act.wait_ge(mm_done, t * OWN_CHUNKS + (MIX_CHUNKS - 2))
                        copy(two(XT_HI), XT_PS).then_inc(xt_hi, 1)

                    def tile(t, more):
                        split_own(t, 2)
                        act.wait_ge(mm_done, t * OWN_CHUNKS + (MIX_CHUNKS + 2))
                        act.activation(SIL, PS[0:ROWS_T, 0, :], ACT.Silu).then_inc(sil_done, 1)
                        split_own(t, 3)
                        split_own(t, 4)
                        act.wait_ge(at_t, t + 1)
                        copy(AT_HI, AT_PS).then_inc(at_hi, 1)
                        split_own(t, 5)
                        rows_hi(t + 1)
                        if more:
                            split_own(t + 1, 0)
                            split_own(t + 1, 1)
                        act.wait_ge(mm_done, t * OWN_CHUNKS + (MIX_CHUNKS + OWN_CHUNKS))
                        act.wait_ge(y_stored, 16 * t + 16)
                        copy(YB, PS[0:ROWS_T, 2:4, :].rearrange("p a n -> p (a n)")).then_inc(y_copied, 1)
                        act.wait_ge(y_copied, t + 1)
                        act.dma_start(ys_d[bass.ds(t * ROWS_T, ROWS_T), :], YB).then_inc(y_stored, 16)

                    split_own(0, 0, begin=True)
                    split_own(0, 1, begin=True)
                    rows_hi(0)
                    with act.Fori(0, NE - 1) as t:
                        tile(t, True)
                    tile(NE - 1, False)
                    act.wait_ge(table, 1)
                    n_more = act.value_load(TILE_TAB[0:1, MORE:MORE + 1], min_val=0, max_val=MORE)
                    with act.If(n_more > 0):
                        split_own(NE, 0)
                        split_own(NE, 1)
                        with act.Fori(NE, TILES - 1) as t:
                            tile(t, True)
                        tile(TILES - 1, False)

                @block.vector
                def _(dve):
                    own = Own(dve, dve_own)
                    tt, ts, stt = dve.tensor_tensor, dve.tensor_scalar, dve.scalar_tensor_tensor

                    def split_lo(c):
                        dve.wait_ge(hi_done, c + 1)
                        tt(W_LO[:, c % 2, :], RAW[:, c % RAW_SLOTS, :], W_HI[:, c % 2, :].bitcast(F32), ALU.subtract) \
                            .then_inc(lo_done, 1)

                    def mean(cols, count, n, waits):
                        for s, v in waits:
                            dve.wait_ge(s, v)
                        ts(SS[:, 0:cols], SS[:, 0:cols], 1.0 / count, EPS, ALU.mult, ALU.add).then_inc(ms_done, 1)
                        dve.wait_ge(rstd_done, n)

                    def transposed_lo(s, gains):
                        for k in range(KD):
                            dve.wait_ge(ht_hi, KD * s + k + 1)
                            gain = 1.0 if gains is None else LP[:, gains + k:gains + k + 1]
                            stt(HT_LO[:, k, :], PS[:, k % 2, :], gain, HT_HI[:, k, :].bitcast(F32), ALU.mult,
                                ALU.subtract).then_inc(ht_lo, 1)

                    def heads_of(x):
                        return x.rearrange("p i (g d) -> p i g d", d=HD)

                    mean(NT, D, 1, [(ss_done, NT)])
                    for i in range(NT):
                        ts(ROWS[:, i, :], X[:, i, :], SS[:, i:i + 1], None, ALU.mult).then_inc(rows_done, 1)
                    split_lo(0)
                    split_lo(1)
                    transposed_lo(0, L_GMIX)
                    for c in range(2, TM_CHUNKS + 2):
                        split_lo(c)
                    dve.wait_ge(gelu_done, 1)
                    V = heads_of(TM[:, :, 1024:1280])
                    sq = B[:, :, 0:256]
                    own(tt(sq, TM[:, :, 1024:1280], TM[:, :, 1024:1280], ALU.mult))
                    own(dve.tensor_reduce(SS[:, 0:NT * H_GMLP].rearrange("p (i g) -> p i g", i=NT), heads_of(sq), AX.X,
                                          ALU.add))
                    mean(NT * H_GMLP, HD, 2, [])
                    own(tt(V, V, SS[:, 0:NT * H_GMLP].rearrange("p (i g) -> p i g", i=NT).unsqueeze(3)
                           .broadcast_to([P, NT, H_GMLP, HD]), ALU.mult))
                    own(tt(TM[:, :, 1024:1280], TM[:, :, 1024:1280], GV[:].unsqueeze(1).broadcast_to([P, NT, 256]),
                           ALU.mult))
                    WS = LP[:, L_WS:L_WR].rearrange("p (g t) -> p g t", g=H_GMLP)
                    tt(WS, WS, C[:, C_LOW:C_LOW + P].unsqueeze(1).broadcast_to([P, H_GMLP, P]), ALU.mult) \
                        .then_inc(gv_ready, 1)
                    for pair in range(2):
                        if not pair:
                            split_lo(TM_CHUNKS + 2)
                        for h in (2 * pair, 2 * pair + 1):
                            if h:
                                dve.wait_ge(av_done, h)
                            for n, j in enumerate(reversed(range(NT))):
                                w = SEQ - P * j
                                dve.wait_ge(sb_abs, NT * h + n + 1)
                                own(ts(A[:, j, 0:w], PS[:, 2 + j, 0:w], SCALE, 0.0, ALU.mult, ALU.max))
                            for n, j in enumerate(reversed(range(NT))):
                                w = SEQ - P * j
                                dve.wait_ge(sb_ln, NT * h + n + 1)
                                tt(A[:, j, 0:w], A[:, j, 0:w], B[:, j, 0:w], ALU.add).then_inc(sb_sum, 1)
                            dve.wait_ge(av_done, h + 1)
                            dve.tensor_copy(ROWS[:, :, HD * h:HD * (h + 1)],
                                            PS[:, 0, 0:NT * HD].rearrange("p (i d) -> p i d", d=HD)).then_inc(head_out, 1)
                    n_own = own.n
                    with dve.Fori(0, 2) as r:
                        own.at(n_own, r, 10)
                        for half in range(2):
                            c = TM_CHUNKS + 2 + half
                            dve.wait_ge(rot_done, 2 * r + half + 1)
                            cos = ROPE[:, 0, :].unsqueeze(1).broadcast_to([P, 2, SEQ])
                            sin = ROPE[:, 1, :].unsqueeze(1).broadcast_to([P, 2, SEQ])
                            tt(QK[:], PS[:, 0:2, :], sin, ALU.mult)
                            own(tt(B[:, 0:2, :], B[:, 0:2, :], cos, ALU.mult))
                            tt(QK[:], QK[:], B[:, 0:2, :], ALU.add).then_inc(qk_ready, 1)
                            dve.wait_ge(hi_done, 2 * r + c + 2)
                            tt(W_LO[:, (c + 1) % 2, :],
                               RAW[:, bass.ds(2 * r + 2 + half, 1), :].rearrange("p a n -> p (a n)"),
                               W_HI[:, (c + 1) % 2, :].bitcast(F32), ALU.subtract).then_inc(lo_done, 1)
                            for h in range(2):
                                n = 4 * r + 2 * half + h
                                dve.wait_ge(mo_z, n + 1)
                                for i in range(NT):
                                    ins = dve.tensor_reduce(NMAX[:, 0, i:i + 1], PS[:, 2 + i, 0:P * (i + 1)], AX.X, ALU.max,
                                                            negate=True)
                                own(ins)
                                ts(NMAX[:, 1, :], NMAX[:, 0, :], SCALE, None, ALU.mult).then_inc(mo_max, 1)
                                dve.wait_ge(av_done, n + H_SB)
                                for i in range(NT):
                                    dve.wait_ge(mo_t, NT * n + i + 1)
                                    dve.tensor_copy(B[:, i, 0:P * (i + 1)], PS[:, 6 + i % 2, 0:P * (i + 1)]) \
                                        .then_inc(mo_pt, 1)
                                dve.wait_ge(mo_p, NT * n + NT)
                                own(dve.reciprocal(RSUM[:, 1, :], RSUM[:, 0, :]))
                                dve.wait_ge(av_done, n + H_SB + 1)
                                tt(ROWS[:, :, bass.ds(n * HD + HD * H_SB, HD)],
                                   PS[:, 0, 0:NT * HD].rearrange("p (i d) -> p i d", d=HD),
                                   RSUM[:, 1, :].unsqueeze(2).broadcast_to([P, NT, HD]), ALU.mult).then_inc(head_out, 1)
                    assert own.n == 10
                    own.at(n_own, 2, 10)
                    split_lo(MIX_CHUNKS - 3)
                    for g in range(H_GMLP):
                        dve.wait_ge(spatial_done, g + 1)
                        stt(ROWS[:, :, HD * (12 + g):HD * (13 + g)],
                            PS[:, 6 + g % 2, 0:NT * HD].rearrange("p (i d) -> p i d", d=HD),
                            LP[:, L_BS + g:L_BS + g + 1], TM[:, :, 768 + HD * g:768 + HD * (g + 1)], ALU.add,
                            ALU.mult).then_inc(spatial_out, 1)
                    for i in range(NT):
                        dve.wait_ge(sq_done, i + 1)
                        dve.tensor_reduce(SS[:, N_HEADS * i:N_HEADS * (i + 1)],
                                          A[:, 2 * (i % 2):2 * (i % 2) + 2, :].rearrange("p a (g d) -> p (a g) d", d=HD),
                                          AX.X, ALU.add).then_inc(sq_used, 1)
                    mean(NT * N_HEADS, HD, 3, [(sq_used, NT)])
                    for i in range(NT):
                        r4 = ROWS[:, i, :].rearrange("p (g d) -> p g d", d=HD)
                        tt(r4, r4, SS[:, N_HEADS * i:N_HEADS * (i + 1)].unsqueeze(2).broadcast_to([P, N_HEADS, HD]),
                           ALU.mult).then_inc(rows_done, 1)
                    transposed_lo(1, L_GHEAD)
                    for q in range(OUT_CHUNKS):
                        c = MIX_CHUNKS - OUT_CHUNKS + q
                        if q in (0, 1):
                            split_lo(c + 2)
                        dve.wait_ge(mm_done, c + 1)
                        b = 2 * (q % 2)
                        xq = X[:, :, q * 256:(q + 1) * 256]
                        tt(xq, xq, PS[:, b:b + 2, :].rearrange("p b (i n) -> p (b i) n", n=256), ALU.add) \
                            .then_inc(x_added, 1)
                    mean(NT, D, 4, [(ss_done, 2 * NT), (grow_in, 16)])
                    for i in range(NT):
                        stt(ROWS[:, i, :], X[:, i, :], SS[:, i:i + 1], GROW[:], ALU.mult, ALU.mult).then_inc(rows_done, 1)
                    dve.wait_ge(wr_hi, 1)
                    tt(WR_LO[:], LP[:, L_WR:L_COLS].rearrange("p (k n) -> p k n", n=NR), WR_HI[:].bitcast(F32),
                       ALU.subtract).then_inc(wr_lo, 1)
                    transposed_lo(2, None)
                    def bc(x, n):
                        return x.unsqueeze(2).broadcast_to([P, NT, n])

                    def area(a, b, cols):
                        return B[:, a, b * 128:b * 128 + NT * cols].rearrange("p (i n) -> p i n", n=cols)

                    def over(col, n):
                        return C[:, col:col + n].unsqueeze(1).broadcast_to([P, NT, n])

                    GE = A[:, 0, 0:NT * NG].rearrange("p (i n) -> p i n", n=NG)
                    G4, L, M1, M2 = area(0, 0, NG), area(0, 1, NE), area(0, 2, NE), area(0, 3, NE)
                    T1, T2, MB, POS = area(1, 0, NE), area(1, 1, NE), area(1, 2, NE), area(1, 3, NE)
                    SM = A[:, 1, 0:64].rearrange("p (a i) -> p a i", i=NT)
                    MAXG, SUMG, GSEL, TOP1, IDX1, TOP2, IDX2, PGRP = (SM[:, a, :] for a in range(8))
                    dve.wait_ge(logits, 1)
                    LG = PS[:, 2, 0:NT * 64].rearrange("p (i n) -> p i n", n=64)
                    own(dve.tensor_copy(G4, LG[:, :, 0:NG]))
                    own(dve.tensor_copy(L, LG[:, :, NG:NR]))
                    own(dve.tensor_reduce(MAXG, G4, AX.X, ALU.max))
                    tt(GE, G4, bc(MAXG, NG), ALU.subtract).then_inc(gexp_in, 1)

                    def argmax(x, top, idx, n, tmp):
                        own(tt(tmp, x, bc(top, n), ALU.is_lt))
                        own(stt(tmp, tmp, 64.0, over(C_IOTA, n), ALU.mult, ALU.add))
                        own(dve.tensor_reduce(idx, tmp, AX.X, ALU.min))

                    argmax(G4, MAXG, GSEL, NG, area(2, 0, NG))
                    own(tt(T1, over(C_GROUP, NE), bc(GSEL, NE), ALU.is_equal))
                    own(tt(L, L, T1, ALU.mult))
                    own(ts(T1, T1, -1.0, -NEG, ALU.add, ALU.mult))
                    own(tt(L, L, T1, ALU.add))
                    own(dve.tensor_reduce(TOP1, L, AX.X, ALU.max))
                    argmax(L, TOP1, IDX1, NE, T2)
                    own(tt(M1, over(C_IOTA, NE), bc(IDX1, NE), ALU.is_equal))
                    own(stt(L, M1, 2 * NEG, L, ALU.mult, ALU.add))
                    own(dve.tensor_reduce(TOP2, L, AX.X, ALU.max))
                    argmax(L, TOP2, IDX2, NE, T2)
                    own(tt(M2, over(C_IOTA, NE), bc(IDX2, NE), ALU.is_equal))
                    tt(MB, M1, M2, ALU.add).then_inc(ranks_in, 1)
                    tt(GATE[:, 1, :], TOP2, TOP1, ALU.subtract).then_inc(gexp_in, 1)
                    dve.wait_ge(gexp, 2)
                    own(dve.tensor_reduce(SUMG, GE, AX.X, ALU.add))
                    own(ts(T1[:, 0:1, 0:NT].rearrange("p a i -> p (a i)"), GATE[:, 1, :], 1.0, None, ALU.add))
                    own(tt(SUMG, SUMG, T1[:, 0:1, 0:NT].rearrange("p a i -> p (a i)"), ALU.mult))
                    own(dve.reciprocal(GATE[:, 0, :], SUMG))
                    own(tt(GATE[:, 1, :], GATE[:, 1, :], GATE[:, 0, :], ALU.mult))
                    dve.wait_ge(ranks, 1)
                    own(dve.tensor_copy(T1, PS[:, 3, 0:NT * NE].rearrange("p (i n) -> p i n", n=NE)))
                    CNT = area(3, 0, NE)[:, 0, :]
                    NV, INC, DIF, ONES = (area(3, 0, NE)[:, 1, :], area(3, 0, NE)[:, 2, :], area(3, 0, NE)[:, 3, :],
                                          C[:, C_ONES:C_ONES + NE])
                    own(dve.tensor_copy(CNT, PS[:, 3, NT * NE:NT * NE + NE]))
                    TH = A[:, 2, 0:NE * (MAX_R - 1)].rearrange("p (n r) -> p n r", r=MAX_R - 1)
                    own(tt(TH, CNT.unsqueeze(2).broadcast_to([P, NE, MAX_R - 1]),
                           C[:, C_LIMIT:C_LIMIT + MAX_R - 1].unsqueeze(1).broadcast_to([P, NE, MAX_R - 1]), ALU.is_gt))
                    own(dve.tensor_reduce(NV, TH, AX.X, ALU.add))
                    own(dve.tensor_tensor_scan(INC, ONES, NV, 0.0, ALU.mult, ALU.add))
                    own(tt(DIF, INC, NV, ALU.subtract))
                    own(ts(DIF, DIF, float(NE - 1), None, ALU.add))
                    own(tt(DIF, DIF, C[:, C_IOTA:C_IOTA + NE], ALU.subtract))
                    own(ts(T2, T1, float(ROWS_T), None, ALU.is_ge))
                    own(tt(T2, T2, DIF.unsqueeze(1).broadcast_to([P, NT, NE]), ALU.mult))
                    own(tt(T2, T2, over(C_IOTA, NE), ALU.add))
                    own(stt(POS, T2, float(ROWS_T), T1, ALU.mult, ALU.add))
                    own(tt(T2, POS, M1, ALU.mult))
                    own(dve.tensor_reduce(IDX1, T2, AX.X, ALU.add))
                    own(tt(T2, POS, M2, ALU.mult))
                    own(dve.tensor_reduce(IDX2, T2, AX.X, ALU.add))
                    own(dve.tensor_copy(SLOT[:, 0, :], IDX1))
                    dve.tensor_copy(SLOT[:, 1, :], IDX2).then_inc(slots, 1)
                    TJ = A[0:1, 3, 0:MORE * NE].rearrange("p (j n) -> p j n", n=NE)
                    EJ = A[0:1, 1, 64:64 + MORE + 1]
                    own(tt(TJ, INC[0:1, :].unsqueeze(1).broadcast_to([1, MORE, NE]),
                           C[0:1, C_IOTA:C_IOTA + MORE].unsqueeze(2).broadcast_to([1, MORE, NE]), ALU.is_le))
                    own(dve.tensor_reduce(EJ[:, 0:MORE], TJ, AX.X, ALU.add))
                    own(ts(EJ[:, 0:MORE], EJ[:, 0:MORE], float(NE - 1), None, ALU.min))
                    own(dve.tensor_copy(EJ[:, MORE:MORE + 1], INC[0:1, NE - 1:NE]))
                    dve.tensor_copy(TILE_TAB[:], EJ).then_inc(table, 1)

                    def lo_own(t, j):
                        dve.wait_ge(hi_done, t * OWN_CHUNKS + (MIX_CHUNKS + j + 1))
                        tt(W_LO[:, j % 2, :], RAW[:, j, :], W_HI[:, j % 2, :].bitcast(F32), ALU.subtract) \
                            .then_inc(lo_done, 1)

                    def rows_lo(t):
                        dve.wait_ge(xt_hi, t + 1)
                        tt(two(XT_LO), XT_PS, two(XT_HI).bitcast(F32), ALU.subtract) \
                            .then_inc(xt_ready, 1)

                    def tile(t, more):
                        lo_own(t, 2)
                        lo_own(t, 3)
                        dve.wait_ge(mm_done, t * OWN_CHUNKS + (MIX_CHUNKS + 4))
                        dve.wait_ge(sil_done, t + 1)
                        tt(ACTED, SIL, PS[0:ROWS_T, 1, :], ALU.mult).then_inc(act_done, 1)
                        lo_own(t, 4)
                        dve.wait_ge(at_hi, t + 1)
                        tt(AT_LO, AT_PS, AT_HI.bitcast(F32),
                           ALU.subtract).then_inc(at_lo, 1)
                        lo_own(t, 5)
                        rows_lo(t + 1)
                        if more:
                            lo_own(t + 1, 0)
                            lo_own(t + 1, 1)

                    lo_own(0, 0)
                    lo_own(0, 1)
                    rows_lo(0)
                    with dve.Fori(0, NE - 1) as t:
                        tile(t, True)
                    tile(NE - 1, False)
                    n_more = dve.value_load(TILE_TAB[0:1, MORE:MORE + 1], min_val=0, max_val=MORE)
                    with dve.If(n_more > 0):
                        lo_own(NE, 0)
                        lo_own(NE, 1)
                        with dve.Fori(NE, TILES - 1) as t:
                            tile(t, True)
                        tile(TILES - 1, False)
                    for i in range(NT):
                        dve.wait_ge(gather_in, l * (2 * NT * 16) + 2 * NT * 16)
                        for s in range(2):
                            own(stt(X[:, i, :], GATHER[:, 2 * i + s, :], GATE[:, s, i:i + 1], X[:, i, :], ALU.mult,
                                    ALU.add))

                @block.tensor
                def _(pe):
                    def transpose_rows(s):
                        pe.wait_ge(rows_done, NT * (s + 1))
                        for k in range(KD):
                            if k >= 2:
                                pe.wait_ge(ht_lo, KD * s + k - 1)
                            for i in range(NT):
                                ins = pe.transpose(PS[:, k % 2, P * i:P * (i + 1)],
                                                   ROWS[:, i, :].rearrange("p (m k) -> p m k", k=KD)[:, :, k], IDENT)
                            ins.then_inc(tr_done, 1)

                    def by_tokens(c, bank):
                        s = c % 2
                        pe.wait_ge(lo_done, c + 1)
                        w_hi = W_HI[:, s, :].rearrange("p (k n) -> p k n", k=KD)
                        w_lo = W_LO[:, s, :].rearrange("p (k n) -> p k n", k=KD)
                        for i in range(NT):
                            out = PS[:, bank + i // 2, 256 * (i % 2):256 * (i % 2) + 256]
                            for k in range(KD):
                                ins = product3(pe, out, HT_HI[:, k, P * i:P * (i + 1)], HT_LO[:, k, P * i:P * (i + 1)],
                                               w_hi[:, k, :], w_lo[:, k, :], k == 0, k == KD - 1)
                        ins.then_inc(mm_done, 1)

                    def project_pair(s):
                        w_hi = W_HI[:, s, :].rearrange("p (q k n) -> p q k n", q=2, k=KD)
                        w_lo = W_LO[:, s, :].rearrange("p (q k n) -> p q k n", q=2, k=KD)
                        for q in range(2):
                            for k in range(KD):
                                ins = product3(pe, PS[:, q, :], w_hi[:, q, k, :], w_lo[:, q, k, :], HT_HI[:, k, :],
                                               HT_LO[:, k, :], k == 0, k == KD - 1)
                        ins.then_inc(mm_done, 1)

                    transpose_rows(0)
                    pe.wait_ge(ht_lo, KD)
                    for c in range(TM_CHUNKS):
                        if c >= 2:
                            pe.wait_ge(tm_out, c - 1)
                        by_tokens(c, 2 * (c % 2))
                    for pair in range(2):
                        c = TM_CHUNKS + pair
                        pe.wait_ge(tm_out, TM_CHUNKS)
                        if pair:
                            pe.wait_ge(head_out, 2 * pair)
                        pe.wait_ge(lo_done, c + 1)
                        project_pair(c % 2)
                        pe.wait_ge(qk_out, pair + 1)
                        for hh in range(2):
                            h = 2 * pair + hh
                            part = slice(HD * hh, HD * (hh + 1))
                            if h:
                                pe.wait_ge(sb_w, NT * h)
                            for j in reversed(range(NT)):
                                pe.matmul(PS[:, 2 + j, 0:SEQ - P * j], QK[part, 1, P * j:P * (j + 1)],
                                          QK[part, 0, P * j:SEQ], start=True, stop=True).then_inc(sb_z, 1)
                            for n, j in enumerate(reversed(range(NT))):
                                pe.wait_ge(sb_masked, NT * h + n + 1)
                                for jj in reversed(range(j + 1, NT)):
                                    pe.matmul(PS[:, 2 + j, P * (jj - j):SEQ - P * j], C[:, C_ONE8:C_ONE8 + P],
                                              A[:, jj, 0:SEQ - P * jj], start=False, stop=False, skip_group_check=True)
                                pe.matmul(PS[:, 2 + j, 0:SEQ - P * j], C[:, C_TRI8:C_TRI8 + P], A[:, j, 0:SEQ - P * j],
                                          start=False, stop=True, skip_group_check=True).then_inc(sb_r, 1)
                            pe.wait_ge(sb_wm, NT * (h + 1))
                            if hh:
                                pe.wait_ge(head_out, h)
                            for i in range(NT):
                                for j in range(i + 1):
                                    ins = pe.matmul(PS[:, 0, HD * i:HD * (i + 1)], B[:, j, P * (i - j):P * (i - j + 1)],
                                                    TM[:, j, HD * h:HD * (h + 1)], start=(j == 0), stop=(j == i))
                            ins.then_inc(av_done, 1)
                    pe.wait_ge(sb_w, NT * H_SB)
                    with pe.Fori(0, 2) as r:
                        for half in range(2):
                            c = TM_CHUNKS + 2 + half
                            pe.wait_ge(head_out, 4 * r + H_SB + 2 * half)
                            pe.wait_ge(lo_done, 2 * r + c + 1)
                            project_pair(c % 2)
                            pe.wait_ge(qk_out, 2 * r + 3 + half)
                            for q in range(2):
                                ins = pe.matmul(PS[:, q, :], C[:, C_ROT:C_ROT + P], B[:, q, :], start=True, stop=True)
                            ins.then_inc(rot_done, 1)
                            pe.wait_ge(qk_ready, 2 * r + half + 1)
                            for hh in range(2):
                                n = 4 * r + 2 * half + hh
                                part = slice(HD * hh, HD * (hh + 1))
                                for i in range(NT):
                                    q = QK[part, 0, P * i:P * (i + 1)]
                                    if i:
                                        pe.matmul(PS[:, 2 + i, 0:P * i], q, QK[part, 1, 0:P * i], start=True, stop=True)
                                    own_keys = PS[:, 2 + i, P * i:P * (i + 1)]
                                    pe.matmul(own_keys, q, QK[part, 1, P * i:P * (i + 1)], start=True, stop=False)
                                    ins = pe.matmul(own_keys, IDENT, C[:, C_NEG:C_NEG + P], start=False, stop=True)
                                ins.then_inc(mo_z, 1)
                                for i in range(NT):
                                    pe.wait_ge(mo_p, NT * n + i + 1)
                                    if i >= 2:
                                        pe.wait_ge(mo_pt, NT * n + i - 1)
                                    for j in range(i + 1):
                                        ins = pe.transpose(PS[:, 6 + i % 2, P * j:P * (j + 1)],
                                                           A[:, i, P * j:P * (j + 1)], IDENT)
                                    ins.then_inc(mo_t, 1)
                                pe.wait_ge(mo_pt, NT * n + NT)
                                if hh:
                                    pe.wait_ge(head_out, n + H_SB)
                                for i in range(NT):
                                    for j in range(i + 1):
                                        ins = pe.matmul(PS[:, 0, HD * i:HD * (i + 1)], B[:, i, P * j:P * (j + 1)],
                                                        TM[:, j, bass.ds(n * HD + HD * H_SB, HD)], start=(j == 0),
                                                        stop=(j == i))
                                ins.then_inc(av_done, 1)
                    pe.wait_ge(gv_ready, 1)
                    for g in range(H_GMLP):
                        if g >= 2:
                            pe.wait_ge(spatial_out, g - 1)
                        pe.matmul(PS[:, 6 + g % 2, 0:NT * HD], LP[:, L_WS + P * g:L_WS + P * (g + 1)],
                                  TM[:, :, 1024 + HD * g:1024 + HD * (g + 1)], start=True, stop=True) \
                            .then_inc(spatial_done, 1)
                    pe.wait_ge(head_out, H_SB + H_MOBA)
                    transpose_rows(1)
                    pe.wait_ge(ht_lo, 2 * KD)
                    for q in range(OUT_CHUNKS):
                        if q >= 2:
                            pe.wait_ge(x_added, q - 1)
                        by_tokens(MIX_CHUNKS - OUT_CHUNKS + q, 2 * (q % 2))
                    pe.wait_ge(x_added, OUT_CHUNKS)
                    transpose_rows(2)
                    pe.wait_ge(ht_lo, 3 * KD)
                    pe.wait_ge(wr_lo, 1)
                    for i in range(NT):
                        for k in range(KD):
                            ins = product3(pe, PS[:, 2, 64 * i:64 * i + NR], HT_HI[:, k, P * i:P * (i + 1)],
                                           HT_LO[:, k, P * i:P * (i + 1)], WR_HI[:, k, :], WR_LO[:, k, :], k == 0,
                                           k == KD - 1)
                    ins.then_inc(logits, 1)
                    pe.wait_ge(ranks_in, 1)
                    chosen = [B[:, 1, 256 + NE * i:256 + NE * (i + 1)] for i in range(NT)]
                    for i in range(NT):
                        for b in range(i):
                            pe.matmul(PS[:, 3, NE * i:NE * (i + 1)], C[:, C_ONES:C_ONES + P], chosen[b], start=(b == 0),
                                      stop=False)
                        pe.matmul(PS[:, 3, NE * i:NE * (i + 1)], C[:, C_BEFORE:C_BEFORE + P], chosen[i], start=(i == 0),
                                  stop=True)
                    for b in range(NT):
                        ins = pe.matmul(PS[:, 3, NE * NT:NE * (NT + 1)], C[:, C_ONES:C_ONES + P], chosen[b],
                                        start=(b == 0), stop=(b == NT - 1))
                    ins.then_inc(ranks, 1)

                    def transpose_tile(t):
                        pe.wait_ge(xs_in, 16 * (t + 1))
                        pe.wait_ge(xt_ready, t)
                        for k in range(KD):
                            ins = pe.transpose(XT_PS[:, k // 4, k % 4, :],
                                               XS.rearrange("p (m k) -> p m k", k=KD)[:, :, k],
                                               C[0:ROWS_T, C_IDENT:C_IDENT + ROWS_T])
                        ins.then_inc(xs_t, 1)

                    def tile(t):
                        n = MIX_CHUNKS + 1
                        for j in range(4):
                            pe.wait_ge(lo_done, t * OWN_CHUNKS + (n + j))
                            if j == 0:
                                pe.wait_ge(xt_ready, t + 1)
                            w_hi = W_HI[:, j % 2, :].rearrange("p (k n) -> p k n", n=FE)
                            w_lo = W_LO[:, j % 2, :].rearrange("p (k n) -> p k n", n=FE)
                            for kk in range(4):
                                k = 4 * (j % 2) + kk
                                ins = product3(pe, PS[0:ROWS_T, j // 2, :], XT_HI[:, k, :], XT_LO[:, k, :],
                                               w_hi[:, kk, :], w_lo[:, kk, :], k == 0, k == KD - 1)
                            ins.then_inc(mm_done, 1)
                        transpose_tile(t + 1)
                        pe.wait_ge(act_done, t + 1)
                        for k in range(KF):
                            ins = pe.transpose(AT_PS[:, k, :],
                                               ACTED.rearrange("p (m k) -> p m k", k=KF)[:, :, k],
                                               C[0:ROWS_T, C_IDENT:C_IDENT + ROWS_T])
                        ins.then_inc(at_t, 1)
                        pe.wait_ge(at_lo, t + 1)
                        for j in range(4, 6):
                            pe.wait_ge(lo_done, t * OWN_CHUNKS + (n + j))
                            w_hi = W_HI[:, j % 2, :].rearrange("p (k n) -> p k n", n=D)
                            w_lo = W_LO[:, j % 2, :].rearrange("p (k n) -> p k n", n=D)
                            for kk in range(2):
                                k = 2 * (j - 4) + kk
                                for half in range(2):
                                    cols = slice(512 * half, 512 * (half + 1))
                                    ins = product3(pe, PS[0:ROWS_T, 2 + half, :], AT_HI[:, k, :], AT_LO[:, k, :],
                                                   w_hi[:, kk, cols], w_lo[:, kk, cols], k == 0, k == KF - 1)
                            ins.then_inc(mm_done, 1)

                    transpose_tile(0)
                    with pe.Fori(0, NE) as t:
                        tile(t)
                    pe.wait_ge(table, 1)
                    n_more = pe.value_load(TILE_TAB[0:1, MORE:MORE + 1], min_val=0, max_val=MORE)
                    with pe.If(n_more > 0):
                        with pe.Fori(NE, TILES) as t:
                            tile(t)

            nc.all_engine_barrier(sems_to_clear=range(first.num, last.num + 1))

        with nc.Block() as block:
            @block.scalar
            def _(act):
                for i in range(NT):
                    act.activation(ROWS[:, i, :], X[:, i, :], ACT.Square, accum_out=SS[:, i:i + 1]).then_inc(fin_ss, 1)

            @block.gpsimd
            def _(pool):
                pool.wait_ge(fin_ms, 1)
                pool.tensor_tensor(SS[:, 0:NT], SS[:, 0:NT], MINUS_HALF[:, 0:NT], ALU.pow).then_inc(fin_rstd, 1)

            @block.vector
            def _(dve):
                dve.wait_ge(fin_ss, NT)
                dve.tensor_scalar(SS[:, 0:NT], SS[:, 0:NT], 1.0 / D, EPS, ALU.mult, ALU.add).then_inc(fin_ms, 1)
                dve.wait_ge(fin_rstd, 1)
                dve.wait_ge(gfin_in, 16)
                for i in range(NT):
                    dve.scalar_tensor_tensor(ROWS[:, i, :], X[:, i, :], SS[:, i:i + 1], GROW[:], ALU.mult, ALU.mult) \
                       .then_inc(fin_rows, 1)

            @block.sync
            def _(sp):
                sp.dma_start(GROW[:], gfin_d.partition_broadcast(P)).then_inc(gfin_in, 16)
                for i in range(NT):
                    sp.wait_ge(fin_rows, i + 1)
                    sp.dma_start(out_d[i * P:(i + 1) * P, :], ROWS[:, i, :]).then_inc(out_stored, 16)
                sp.wait_ge(out_stored, 16 * NT)


def constants():
    c = np.zeros((P, C_COLS), np.float32)
    row, col = np.arange(P)[:, None], np.arange(P)[None, :]
    c[:, C_IDENT:C_IDENT + P] = row == col
    half = ROT // 2
    d_in, d_out, same = row % HD, col % HD, row // HD == col // HD
    c[:, C_ROT:C_ROT + P] = np.where(same & (d_out < half) & (d_in == d_out + half), -1.0, 0.0) + np.where(
        same & (d_out >= half) & (d_out < ROT) & (d_in == d_out - half), 1.0, 0.0)
    c[:, C_NEG:C_NEG + P] = np.where(col > row, NEG, 0.0)
    c[:, C_TRI8:C_TRI8 + P] = np.where(row >= col, -1.0 / SCALE, 0.0)
    c[:, C_ONE8:C_ONE8 + P] = -1.0 / SCALE
    c[:, C_LOW:C_LOW + P] = col >= row
    c[:, C_BEFORE:C_BEFORE + P] = row < col
    c[:, C_ONES:C_ONES + P] = 1.0
    freq = np.power(np.float32(THETA), -np.arange(half, dtype=np.float32) / np.float32(half)).astype(np.float32)
    d = np.arange(P) % HD
    c[:, C_FREQ] = np.where(d < ROT, freq[d % half], 0.0)
    c[:, C_IOTA:C_IOTA + NE] = np.arange(NE)
    c[:, C_GROUP:C_GROUP + NE] = np.arange(NE) // EPG
    c[:, C_LIMIT:C_LIMIT + MAX_R - 1] = ROWS_T * np.arange(1, MAX_R)
    return c


def kernel(x, positions, w_in, w_out, g_mix_norm, g_head_norm, g_gmlp_vnorm, w_spatial, b_spatial, g_ffn_norm,
           w_router_group, w_router_expert, w_expert_gate, w_expert_up, w_expert_down, g_final):
    import concourse.bacc as bacc
    from concourse.bass_utils import run_bass_kernel_spmd

    w_in, w_out = np.asarray(w_in), np.asarray(w_out)
    wsb, wmo = H_SB * HD, H_MOBA * HD
    rows = w_in.reshape(DEPTH, P, KD, -1)
    qa, ka, va, qb, kb, vb, uv = np.split(rows, np.cumsum([wsb] * 3 + [wmo] * 3), axis=-1)
    tm = np.concatenate([va, vb, uv], axis=-1)
    chunks = [tm[..., 256 * c:256 * (c + 1)].reshape(DEPTH, P, CHUNK) for c in range(TM_CHUNKS)]
    for q, k in ((qa, ka), (qb, kb)):
        for c in range(q.shape[-1] // P):
            pair = np.stack([q[..., P * c:P * (c + 1)], k[..., P * c:P * (c + 1)]], axis=2)
            chunks.append(pair.reshape(DEPTH, P, CHUNK))
    out_rows = w_out.reshape(DEPTH, P, KD, D)
    chunks += [out_rows[..., 256 * c:256 * (c + 1)].reshape(DEPTH, P, CHUNK) for c in range(OUT_CHUNKS)]
    mix = np.ascontiguousarray(np.stack(chunks, axis=1)).reshape(DEPTH * MIX_CHUNKS, P, CHUNK)

    router = np.concatenate([np.asarray(w_router_group), np.asarray(w_router_expert)], axis=-1)
    lay = np.concatenate([
        np.asarray(g_mix_norm).reshape(DEPTH, P, KD),
        np.asarray(g_head_norm).reshape(DEPTH, P, KD),
        np.asarray(b_spatial).transpose(0, 2, 1),
        np.asarray(w_spatial).transpose(0, 3, 1, 2).reshape(DEPTH, P, H_GMLP * P),
        router.reshape(DEPTH, P, KD * NR),
    ], axis=-1)
    arrays = {
        "x": np.asarray(x).reshape(SEQ, D),
        "positions": np.asarray(positions).reshape(SEQ),
        "mix": mix,
        "lay": np.ascontiguousarray(lay),
        "g_vnorm": np.asarray(g_gmlp_vnorm).reshape(DEPTH, H_GMLP * HD),
        "g_ffn": np.asarray(g_ffn_norm),
        "w_gate": np.asarray(w_expert_gate),
        "w_up": np.asarray(w_expert_up),
        "w_down": np.asarray(w_expert_down),
        "g_final": np.asarray(g_final),
        "constants": constants(),
    }
    nc = bacc.Bacc("TRN2", target_bir_lowering=False, num_devices=1)
    ins = [nc.dram_tensor(n, a.shape, mybir.dt.from_np(a.dtype), kind="ExternalInput").ap() for n, a in arrays.items()]
    out = nc.dram_tensor("out", (SEQ, D), F32, kind="ExternalOutput").ap()
    build(nc, *ins, out)
    r = run_bass_kernel_spmd(nc, [arrays], core_ids=[0])
    return r.results[0]["out"].reshape(1, SEQ, D)
```

```python
import contextlib

import numpy as np
import concourse.bass as bass
from concourse import mybir

F32 = mybir.dt.float32
F32R = mybir.dt.float32r
I32 = mybir.dt.int32
U32 = mybir.dt.uint32
ACT = mybir.ActivationFunctionType
ALU = mybir.AluOpType
AX = mybir.AxisListType

P = 128
DEPTH, SEQ, D = 2, 512, 1024
NT = SEQ // P
KD = D // P
HD = 64
N_HEADS = D // HD
H_SB, H_MOBA, H_GMLP = 4, 8, 4
ROT = HD // 4
THETA = 500000.0
EPS = 1e-6
SCALE = HD ** -0.5
NEG = -1e30

CHUNK = 2048
UNIT = CHUNK // 2
W_SLOTS = 4
TM_GROUPS = ((768, 512, 2), (256, 512, 2), (0, 256, 1))
TM_CHUNKS = 5
QK_CHUNKS = 6
OUT_CHUNKS = 4
MIX_CHUNKS = TM_CHUNKS + QK_CHUNKS + OUT_CHUNKS
MIX_UNITS = 2 * MIX_CHUNKS
QK_UNIT = 2 * TM_CHUNKS
OUT_UNIT = QK_UNIT + 2 * QK_CHUNKS
RAW_SLOTS = 6

NE, NG, EPG = 32, 4, 8
FE = D // 2
KF = FE // P
ROWS_T = 96
MORE = (2 * SEQ - 2) // ROWS_T
TILES = NE + MORE
OWN_CHUNKS = 6
OWN_UNITS = 2 * OWN_CHUNKS
XS_ROWS = -(-(TILES + 1) * ROWS_T // P) * P
MAX_R = -(-SEQ // ROWS_T)

C_IDENT, C_ROT, C_NEG, C_TRI8, C_ONE8, C_LOW, C_BEFORE, C_ONES = (P * n for n in range(8))
C_FREQ = 8 * P
C_IOTA = C_FREQ + 1
C_GROUP = C_IOTA + NE
C_LIMIT = C_GROUP + NE
C_COLS = C_LIMIT + MAX_R - 1
L_GMIX, L_GHEAD, L_BS = 0, KD, 2 * KD
L_WS = L_BS + H_GMLP
L_WR = L_WS + H_GMLP * P
NR = NG + NE
L_COLS = L_WR + KD * NR

TWO_PI = (6.28125, float(np.float32(1.9350051879882812e-3)), float(np.float32(3.0199157663725e-7)))
ROUND = 12582912.0


def build(nc, x_d, pos_d, mix_d, lay_d, gv_d, gffn_d, wg_d, wu_d, wd_d, gfin_d, const_d, out_d):
    xs_d = nc.dram_tensor("expert_rows_in", (XS_ROWS, D), F32).ap()
    ys_d = nc.dram_tensor("expert_rows_out", (XS_ROWS, D), F32).ap()
    wg_v = wg_d.rearrange("l e (p k) n -> (l e) p (k n)", k=KD)
    wu_v = wu_d.rearrange("l e (p k) n -> (l e) p (k n)", k=KD)
    wd_v = wd_d.rearrange("l e (p k) n -> (l e) p (k n)", k=KF)

    with contextlib.ExitStack() as ctx:
        def sb(name, shape, dt=F32):
            return ctx.enter_context(nc.sbuf_tensor(name, shape, dt))

        def sem(name):
            return ctx.enter_context(nc.semaphore(name))

        X = sb("X", [P, NT, D])
        ROWS = sb("ROWS", [P, NT, D])
        HT_HI = sb("HT_HI", [P, KD, SEQ], F32R)
        HT_LO = sb("HT_LO", [P, KD, SEQ], F32R)
        TM = sb("TM", [P, NT, TM_CHUNKS * 256])
        RAW = sb("RAW", [P, RAW_SLOTS, CHUNK])
        W_HI = sb("W_HI", [P, W_SLOTS, UNIT], F32R)
        W_LO = sb("W_LO", [P, W_SLOTS, UNIT], F32R)
        ROPE = sb("ROPE", [P, 2, SEQ])
        QK = sb("QK", [P, 2, SEQ])
        A = sb("A", [P, NT, SEQ])
        B = sb("B", [P, NT, SEQ])
        LP = sb("LP", [P, L_COLS])
        GV = sb("GV", [P, H_GMLP * HD])
        GROW = sb("GROW", [P, D])
        C = sb("C", [P, C_COLS])
        WR_HI = sb("WR_HI", [P, KD, NR], F32R)
        WR_LO = sb("WR_LO", [P, KD, NR], F32R)
        ROOT = sb("ROOT", [P, 2, NT * N_HEADS])
        SS = sb("SS", [P, NT * N_HEADS])
        MINUS_HALF = sb("MINUS_HALF", [P, NT * N_HEADS])
        NMAX = sb("NMAX", [P, 2, NT])
        RSUM = sb("RSUM", [P, 2, NT])
        SLOT = sb("SLOT", [P, 2, NT], U32)
        GATE = sb("GATE", [P, 2, NT])
        TILE_TAB = sb("TILE_TAB", [1, MORE + 1], I32)

        PS = ctx.enter_context(nc.psum_tensor("PS", [P, 8, 512], F32))

        QK_OF = [QK, TM[:, 0:2, 768:1280]]
        QK_RAW = TM[:, 2:4, 768:1280]
        XS = TM[0:ROWS_T, 0, 0:D]
        YB = TM[0:ROWS_T, 1, 0:D]
        SIL = TM[0:ROWS_T, 2, 0:FE]
        ACTED = TM[0:ROWS_T, 2, FE:2 * FE]
        XT_HI = HT_HI[:, 0:2, :].rearrange("p a n -> p (a n)")[:, 0:KD * ROWS_T].rearrange("p (k t) -> p k t", k=KD)
        XT_LO = HT_LO[:, 0:2, :].rearrange("p a n -> p (a n)")[:, 0:KD * ROWS_T].rearrange("p (k t) -> p k t", k=KD)
        AT_HI = HT_HI[:, 2, 0:KF * ROWS_T].rearrange("p (k t) -> p k t", k=KF)
        AT_LO = HT_LO[:, 2, 0:KF * ROWS_T].rearrange("p (k t) -> p k t", k=KF)
        GATHER = RAW[:, 0:4, :].rearrange("p a (b d) -> p (a b) d", d=D)
        IDENT = C[:, C_IDENT:C_IDENT + P]
        XT_PS = PS[:, 4:6, 0:KD * ROWS_T // 2].rearrange("p b (k t) -> p b k t", t=ROWS_T)
        AT_PS = PS[:, 6, 0:KF * ROWS_T].rearrange("p (k t) -> p k t", k=KF)

        def two(x):
            return x.rearrange("p (b k) t -> p b k t", b=2)


        first = sem("lay_loaded")
        lay_loaded = first
        raw_in = [sem(f"raw_in{s}") for s in range(RAW_SLOTS)]
        grow_in = sem("grow_in")
        hi_done, lo_done, mm_done = sem("hi_done"), sem("lo_done"), sem("mm_done")
        ss_done, ms_done, rstd_done = sem("ss_done"), sem("ms_done"), sem("rstd_done")
        sq_done, sq_used = sem("sq_done"), sem("sq_used")
        root_done = sem("root_done")
        rows_done, tr_done, ht_hi, ht_lo = sem("rows_done"), sem("tr_done"), sem("ht_hi"), sem("ht_lo")
        tm_out = sem("tm_out")
        gelu_done, gv_ready, spatial_done, spatial_out = (
            sem("gelu_done"), sem("gv_ready"), sem("spatial_done"), sem("spatial_out"))
        qk_out, rot_done, qk_ready = sem("qk_out"), sem("rot_done"), sem("qk_ready")
        exp_tables = "natural_log_exp_and_others"
        sb_z, sb_abs, sb_ln, sb_sum, sb_masked, sb_r, sb_w, sb_wm = (
            sem("sb_z"), sem("sb_abs"), sem("sb_ln"), sem("sb_sum"), sem("sb_masked"), sem("sb_r"), sem("sb_w"),
            sem("sb_wm"))
        mo_z, mo_max, mo_p, mo_t, mo_pt = sem("mo_z"), sem("mo_max"), sem("mo_p"), sem("mo_t"), sem("mo_pt")
        av_done, head_out = sem("av_done"), sem("head_out")
        x_added = sem("x_added")
        wr_hi, wr_lo, logits = sem("wr_hi"), sem("wr_lo"), sem("logits")
        dve_ss = sem("dve_ss")
        gexp_in, gexp, ranks_in, ranks, slots, table = (
            sem("gexp_in"), sem("gexp"), sem("ranks_in"), sem("ranks"), sem("slots"), sem("table"))
        scattered = sem("scattered")
        xs_in, xs_t, xt_ready = sem("xs_in"), sem("xs_t"), sem("xt_ready")
        sil_done, act_done, at_t, at_hi, at_lo, xt_hi = (
            sem("sil_done"), sem("act_done"), sem("at_t"), sem("at_hi"), sem("at_lo"), sem("xt_hi"))
        y_copied, y_stored = sem("y_copied"), sem("y_stored")
        act_own, dve_own = sem("act_own"), sem("dve_own")
        last = sem("layer_sems_end")
        zeroed = sem("zeroed")
        scatter_in = sem("scatter_in")
        gather_in = [sem(f"gather_in{i}") for i in range(NT)]
        consts_in, setup, out_stored, gfin_in = sem("consts_in"), sem("setup"), sem("out_stored"), sem("gfin_in")
        fin_ss, fin_ms, fin_rstd, fin_rows = sem("fin_ss"), sem("fin_ms"), sem("fin_rstd"), sem("fin_rows")

        zero_count = []

        class Own:

            def __init__(self, eng, s):
                self.eng, self.s, self.base, self.n = eng, s, 0, 0

            def __call__(self, ins):
                self.n += 1
                ins.then_inc(self.s, 1)
                self.eng.wait_ge(self.s, self.base + self.n)

            def at(self, start, i, per):
                self.base, self.n = start + i * per, 0

        def product3(pe, out, a_hi, a_lo, b_hi, b_lo, start, stop):
            pe.matmul(out, a_hi, b_hi, start=start, stop=False)
            pe.matmul(out, a_hi, b_lo, start=False, stop=False)
            return pe.matmul(out, a_lo, b_hi, start=False, stop=stop)

        with nc.Block() as block:
            @block.sync
            def _(sp):
                sp.dma_start(A[:, 0, :].bitcast(I32), pos_d.partition_broadcast(P)).then_inc(consts_in, 16)
                sp.dma_start(C[:], const_d).then_inc(consts_in, 16)
                sp.dma_start(X[:], x_d.rearrange("(i p) d -> p i d", p=P)).then_inc(consts_in, 16)
                sp.wait_ge(consts_in, 48)

            @block.gpsimd
            def _(pool):
                pool.memset(GROW[:], 0.0).then_inc(setup, 1)
                pool.memset(MINUS_HALF[:], -0.5)

            @block.vector
            def _(dve):
                n = [1]

                def own(ins):
                    n[0] += 1
                    ins.then_inc(setup, 1)
                    dve.wait_ge(setup, n[0])

                ang, turns, cosx = A[:, 1, :], A[:, 2, :], A[:, 3, :]
                dve.wait_ge(consts_in, 48)
                dve.wait_ge(setup, 1)
                own(dve.tensor_copy(B[:, 0, :], A[:, 0, :].bitcast(I32)))
                own(dve.tensor_scalar(ang, B[:, 0, :], C[:, C_FREQ:C_FREQ + 1], None, ALU.mult))
                own(dve.tensor_scalar(turns, ang, float(1 / (2 * np.pi)), ROUND, ALU.mult, ALU.add))
                own(dve.tensor_scalar(turns, turns, -ROUND, None, ALU.add))
                for part in TWO_PI:
                    own(dve.scalar_tensor_tensor(ang, turns, -part, ang, ALU.mult, ALU.add))
                own(dve.tensor_scalar(ang, ang, float(np.float32(3.1415925)), float(np.float32(-3.1415925)), ALU.min,
                                      ALU.max))
                own(dve.tensor_scalar(cosx, ang, -1.0, None, ALU.mult))
                own(dve.tensor_tensor(cosx, cosx, ang, ALU.max))
                own(dve.tensor_scalar(cosx, cosx, -1.0, float(np.pi / 2), ALU.mult, ALU.add))

            @block.scalar
            def _(act):
                act.wait_ge(setup, 12)
                act.activation(ROPE[:, 0, :], A[:, 3, :], ACT.Sin)
                act.activation(ROPE[:, 1, :], A[:, 1, :], ACT.Sin)

        with nc.Fori(0, DEPTH) as l:
            with nc.Block() as block:
                @block.sync
                def _(sp):
                    sp.dma_start(LP[:], lay_d[bass.ds(l, 1), :, :].rearrange("l p n -> (l p) n")).then_inc(lay_loaded, 16)
                    sp.dma_start(GV[:], gv_d[bass.ds(l, 1), :].rearrange("l n -> (l n)").partition_broadcast(P)) \
                      .then_inc(lay_loaded, 16)
                    fill = 4 * P
                    zeros = GROW[:].unsqueeze(1).broadcast_to([P, 4, D])
                    zero_rows = [xs_d[n:min(n + fill, XS_ROWS), :] for n in range(0, XS_ROWS, fill)]
                    zero_rows += [ys_d[n:min(n + fill, XS_ROWS), :] for n in range(NE * ROWS_T, XS_ROWS, fill)]

                    for c in range(MIX_CHUNKS):
                        if c >= RAW_SLOTS:
                            sp.wait_ge(lo_done, 2 * (c - RAW_SLOTS) + 2)
                        sp.dma_start(RAW[:, c % RAW_SLOTS, :],
                                     mix_d[bass.ds(l * MIX_CHUNKS + c, 1), :, :].rearrange("c p n -> (c p) n")) \
                          .then_inc(raw_in[c % RAW_SLOTS], 16)
                        if c >= 2 and zero_rows:
                            with sp.If(l < 1):
                                for rows in (zero_rows.pop(), zero_rows.pop() if zero_rows else None):
                                    if rows is not None:
                                        n = rows.shape[0] // P
                                        sp.dma_start(rows.rearrange("(n p) d -> p n d", p=P), zeros[:, 0:n, :]) \
                                          .then_inc(zeroed, 16)
                                        zero_count.append(1)
                    assert not zero_rows
                    sp.wait_ge(zeroed, 16 * len(zero_count))
                    sp.dma_start(GROW[:], gffn_d[bass.ds(l, 1), :].rearrange("l n -> (l n)").partition_broadcast(P)) \
                      .then_inc(grow_in, 16)

                    def expert(j, e):
                        w = (wg_v, wg_v, wu_v, wu_v, wd_v, wd_v)[j]
                        return w[bass.ds(e, 1), :, (j % 2) * CHUNK:(j % 2 + 1) * CHUNK].rearrange("e p n -> (e p) n")

                    def load_rows(t):
                        sp.dma_start(XS, xs_d[bass.ds(t * ROWS_T, ROWS_T), :]).then_inc(xs_in, 16)

                    def load_tile(t, e, at_start=False):
                        for j in range(OWN_CHUNKS):
                            if at_start:
                                sp.wait_ge(lo_done, min(MIX_UNITS - 6 + 2 * j + 2, MIX_UNITS))
                            else:
                                sp.wait_ge(lo_done, t * OWN_UNITS + (MIX_UNITS + 2 * j + 2 - OWN_UNITS))
                            sp.dma_start(RAW[:, j, :], expert(j, e)).then_inc(raw_in[j], 16)

                    load_tile(0, l * NE, at_start=True)
                    sp.wait_ge(scatter_in, l * (2 * NT * 16) + 2 * NT * 16)
                    sp.wait_ge(logits, 1)
                    load_rows(0)
                    sp.wait_ge(xs_t, 1)
                    load_rows(1)
                    with sp.Fori(1, NE) as t:
                        load_tile(t, l * NE + t)
                        sp.wait_ge(xs_t, t + 1)
                        load_rows(t + 1)
                    sp.wait_ge(table, 1)
                    n_more = sp.value_load(TILE_TAB[0:1, MORE:MORE + 1], min_val=0, max_val=MORE)
                    with sp.If(n_more > 0):
                        with sp.Fori(NE, TILES) as t:
                            e = sp.value_load(TILE_TAB[0:1, bass.ds(t - NE, 1)], min_val=0, max_val=NE - 1)
                            load_tile(t, l * NE + e)
                            sp.wait_ge(xs_t, t + 1)
                            load_rows(t + 1)
                        sp.wait_ge(xs_in, 16 * (TILES + 1))
                    sp.wait_ge(xs_in, 16 * (NE + 1))

                @block.gpsimd
                def _(pool):
                    def root(n, cols):
                        pool.wait_ge(ms_done, 2 * n - 1 if n == 1 else 4)
                        pool.tensor_tensor(SS[:, 0:cols], SS[:, 0:cols], MINUS_HALF[:, 0:cols], ALU.pow) \
                            .then_inc(rstd_done, 1)

                    root(1, NT)
                    for h in range(H_SB):
                        for n, j in enumerate(reversed(range(NT))):
                            pool.wait_ge(sb_sum, NT * h + n + 1)
                            pool.affine_select(out=A[:, j, 0:P], in_=A[:, j, 0:P], compare_op=ALU.is_gt, fill=0.0,
                                               base=0, pattern=[[1, P]], channel_multiplier=-1).then_inc(sb_masked, 1)
                        for n, j in enumerate(reversed(range(NT))):
                            pool.wait_ge(sb_w, NT * h + n + 1)
                            pool.affine_select(out=B[:, j, 0:P], in_=B[:, j, 0:P], compare_op=ALU.is_gt, fill=0.0,
                                               base=0, pattern=[[1, P]], channel_multiplier=-1).then_inc(sb_wm, 1)
                    root(2, NT)
                    pool.wait_ge(rows_done, 3 * NT)
                    pool.wait_ge(zeroed, 16 * len(zero_count))
                    pool.wait_ge(slots, 1)
                    for s in range(2):
                        for i in range(NT):
                            pool.indirect_dma_start(
                                out=xs_d, out_offset=bass.IndirectOffsetOnAxis(SLOT[:, s, i:i + 1], 0),
                                in_=ROWS[:, i, :], in_offset=None).then_inc(scatter_in, 16)
                    pool.wait_ge(y_stored, 16 * (NE + 1))
                    pool.wait_ge(table, 1)
                    n_more = pool.value_load(TILE_TAB[0:1, MORE:MORE + 1], min_val=0, max_val=MORE)
                    with pool.If(n_more > 0):
                        pool.wait_ge(y_stored, 16 * (TILES + 1))
                    for i in range(NT):
                        for s in range(2):
                            pool.indirect_dma_start(
                                out=GATHER[:, 2 * i + s, :], out_offset=None, in_=ys_d,
                                in_offset=bass.IndirectOffsetOnAxis(SLOT[:, s, i:i + 1], 0)).then_inc(gather_in[i], 16)

                @block.scalar
                def _(act):
                    own = Own(act, act_own)

                    def copy(out, in_, **kw):
                        return act.activation(out, in_, ACT.Copy, **kw)

                    def split_hi(u):
                        c = u // 2
                        act.wait_ge(raw_in[c % RAW_SLOTS], 16 * (c // RAW_SLOTS + 1))
                        if u >= W_SLOTS:
                            act.wait_ge(mm_done, u - W_SLOTS + 1)
                        copy(W_HI[:, u % W_SLOTS, :], RAW[:, c % RAW_SLOTS, UNIT * (u % 2):UNIT * (u % 2 + 1)]) \
                            .then_inc(hi_done, 1)

                    def squares():
                        for i in range(NT // 2):
                            act.activation(ROWS[:, i, :], X[:, i, :], ACT.Square, accum_out=SS[:, i:i + 1]) \
                               .then_inc(ss_done, 1)

                    def roots(n, cols):
                        act.wait_ge(ms_done, n)
                        act.activation(ROOT[:, 0, 0:cols], SS[:, 0:cols], ACT.Sqrt).then_inc(root_done, 1)

                    def transposed_hi(s, gains):
                        for k in range(KD):
                            act.wait_ge(tr_done, KD * s + k + 1)
                            kw = {} if gains is None else {"scale": LP[:, gains + k:gains + k + 1]}
                            copy(HT_HI[:, k, :], PS[:, k % 2, :], **kw).then_inc(ht_hi, 1)

                    act.preload_act_table_set(exp_tables)
                    squares()
                    act.wait_ge(lay_loaded, 32)
                    for u in range(2):
                        split_hi(u)
                    transposed_hi(0, L_GMIX)
                    for u in range(2, 4):
                        split_hi(u)
                    u = 0
                    for g, (col, width, chunks) in enumerate(TM_GROUPS):
                        for _ in range(2 * chunks):
                            split_hi(u + W_SLOTS)
                            u += 1
                        b = 4 * (g % 2)
                        act.wait_ge(mm_done, u)
                        copy(TM[:, :, col:col + width], PS[:, b:b + NT, 0:width]).then_inc(tm_out, 1)
                        if g == 0:
                            act.wait_ge(tm_out, 1)
                            act.activation(TM[:, :, 768:1280], TM[:, :, 768:1280], ACT.Gelu_apprx_tanh) \
                                .then_inc(gelu_done, 1)
                            roots(2, NT * H_GMLP)
                            act.preload_act_table_set(exp_tables)

                    act.wait_ge(mm_done, QK_UNIT + 2)
                    copy(QK_OF[0][:], PS[:, 0:2, :]).then_inc(qk_out, 1)
                    split_hi(QK_UNIT + W_SLOTS)
                    split_hi(QK_UNIT + W_SLOTS + 1)

                    def next_pair(pair, q):
                        if pair == QK_CHUNKS - 1:
                            return
                        u = QK_UNIT + 2 * pair + 2 + q
                        act.wait_ge(mm_done, u + 1)
                        if pair == 0 and q == 0:
                            act.wait_ge(spatial_out, H_GMLP)
                        dest = QK_OF[1] if pair == 0 else QK_RAW
                        if pair >= 2:
                            act.wait_ge(qk_ready, 2 * (pair - 1))
                        copy(dest[:, q, :], PS[:, q, :]).then_inc(qk_out, 1)
                        if u + W_SLOTS < MIX_UNITS - W_SLOTS:
                            split_hi(u + W_SLOTS)

                    for h in range(H_SB):
                        if h:
                            act.wait_ge(av_done, h)
                        else:
                            act.wait_ge(gv_ready, 1)
                        for n, j in enumerate(reversed(range(NT))):
                            w = SEQ - P * j
                            act.wait_ge(sb_z, NT * h + n + 1)
                            act.activation(B[:, j, 0:w], PS[:, 2 + j, 0:w], ACT.Abs, scale=SCALE).then_inc(sb_abs, 1)
                        for n, j in enumerate(reversed(range(NT))):
                            w = SEQ - P * j
                            act.wait_ge(sb_abs, NT * h + n + 1)
                            own(act.activation(B[:, j, 0:w], B[:, j, 0:w], ACT.Exp, scale=-1.0))
                            act.activation(B[:, j, 0:w], B[:, j, 0:w], ACT.Ln, bias=1.0).then_inc(sb_ln, 1)
                        next_pair(h // 2, h % 2)
                        for n, j in enumerate(reversed(range(NT))):
                            w = SEQ - P * j
                            act.wait_ge(sb_r, NT * h + n + 1)
                            act.wait_ge(sb_sum, NT * h + n + 1)
                            act.activation(B[:, j, 0:w], PS[:, 2 + j, 0:w], ACT.Exp, scale=SCALE).then_inc(sb_w, 1)

                    for n in range(H_MOBA):
                        act.wait_ge(mo_max, n + 1)
                        act.wait_ge(av_done, n + H_SB)
                        for i in range(NT):
                            w = P * (i + 1)
                            act.activation(A[:, i, 0:w], PS[:, 2 + i, 0:w], ACT.Exp, bias=NMAX[:, 1, i:i + 1],
                                           scale=SCALE, accum_out=RSUM[:, 0, i:i + 1]).then_inc(mo_p, 1)
                        next_pair(2 + n // 2, n % 2)
                    act.wait_ge(av_done, H_SB + H_MOBA)
                    act.wait_ge(head_out, H_SB + H_MOBA)
                    for i in range(NT):
                        if i >= 2:
                            act.wait_ge(sq_used, i - 1)
                        act.activation(A[:, 2 * (i % 2):2 * (i % 2) + 2, :].rearrange("p a n -> p (a n)"), ROWS[:, i, :],
                                       ACT.Square).then_inc(sq_done, 1)
                    roots(3, NT * N_HEADS)
                    transposed_hi(1, L_GHEAD)
                    for u in range(MIX_UNITS - W_SLOTS, MIX_UNITS):
                        split_hi(u)
                    act.wait_ge(x_added, 2)
                    squares()
                    copy(WR_HI[:], LP[:, L_WR:L_COLS].rearrange("p (k n) -> p k n", n=NR)).then_inc(wr_hi, 1)

                    def split_own(t, u):
                        j = u // 2
                        act.wait_ge(raw_in[j], 16 * (t + (4 if j < 3 else 3)))
                        act.wait_ge(mm_done, t * OWN_UNITS + (MIX_UNITS + u - W_SLOTS + 1))
                        copy(W_HI[:, (MIX_UNITS + u) % W_SLOTS, :], RAW[:, j, UNIT * (u % 2):UNIT * (u % 2 + 1)]) \
                            .then_inc(hi_done, 1)

                    transposed_hi(2, None)
                    act.wait_ge(gexp_in, 1)
                    act.activation(A[:, 0, 0:NT * NG], A[:, 0, 0:NT * NG], ACT.Exp).then_inc(gexp, 1)
                    act.wait_ge(gexp_in, 2)
                    act.activation(GATE[:, 1, :], GATE[:, 1, :], ACT.Exp).then_inc(gexp, 1)

                    act.sem_inc(y_stored, 16)

                    def rows_hi(t):
                        act.wait_ge(xs_t, t + 1)
                        act.wait_ge(mm_done, t * OWN_UNITS + (MIX_UNITS - 4))
                        copy(two(XT_HI), XT_PS).then_inc(xt_hi, 1)

                    def tile(t, more):
                        for u in range(4, 7):
                            split_own(t, u)
                        act.wait_ge(mm_done, t * OWN_UNITS + (MIX_UNITS + 4))
                        act.activation(SIL, PS[0:ROWS_T, 0, :], ACT.Silu).then_inc(sil_done, 1)
                        for u in range(7, 11):
                            split_own(t, u)
                        act.wait_ge(at_t, t + 1)
                        copy(AT_HI, AT_PS).then_inc(at_hi, 1)
                        split_own(t, 11)
                        rows_hi(t + 1)
                        if more:
                            for u in range(4):
                                split_own(t + 1, u)
                        act.wait_ge(mm_done, t * OWN_UNITS + (MIX_UNITS + OWN_UNITS))
                        act.wait_ge(y_stored, 16 * t + 16)
                        copy(YB, PS[0:ROWS_T, 2:4, :].rearrange("p a n -> p (a n)")).then_inc(y_copied, 1)
                        act.wait_ge(y_copied, t + 1)
                        act.dma_start(ys_d[bass.ds(t * ROWS_T, ROWS_T), :], YB).then_inc(y_stored, 16)

                    act.preload_act_table(ACT.Silu)
                    for u in range(4):
                        split_own(0, u)
                    rows_hi(0)
                    with act.Fori(0, NE - 1) as t:
                        tile(t, True)
                    tile(NE - 1, False)
                    act.wait_ge(table, 1)
                    n_more = act.value_load(TILE_TAB[0:1, MORE:MORE + 1], min_val=0, max_val=MORE)
                    with act.If(n_more > 0):
                        for u in range(4):
                            split_own(NE, u)
                        with act.Fori(NE, TILES - 1) as t:
                            tile(t, True)
                        tile(TILES - 1, False)

                @block.vector
                def _(dve):
                    own = Own(dve, dve_own)
                    tt, ts, stt = dve.tensor_tensor, dve.tensor_scalar, dve.scalar_tensor_tensor

                    def split_lo(u):
                        dve.wait_ge(hi_done, u + 1)
                        tt(W_LO[:, u % W_SLOTS, :], RAW[:, u // 2 % RAW_SLOTS, UNIT * (u % 2):UNIT * (u % 2 + 1)],
                           W_HI[:, u % W_SLOTS, :].bitcast(F32), ALU.subtract).then_inc(lo_done, 1)

                    def squares(n):
                        for i in range(NT // 2, NT):
                            dve.tensor_tensor_reduce(out=ROWS[:, i, :], in0=X[:, i, :], in1=X[:, i, :], scale=1.0,
                                                     scalar=0.0, op0=ALU.mult, op1=ALU.add,
                                                     accum_out=SS[:, i:i + 1]).then_inc(dve_ss, 1)
                        dve.wait_ge(dve_ss, 2 * n)
                        dve.wait_ge(ss_done, 2 * n)

                    def mean(cols, count):
                        ts(SS[:, 0:cols], SS[:, 0:cols], 1.0 / count, EPS, ALU.mult, ALU.add).then_inc(ms_done, 1)

                    def inverse_root(n, cols):
                        x, y, z = SS[:, 0:cols], ROOT[:, 1, 0:cols], ROOT[:, 0, 0:cols]
                        dve.wait_ge(root_done, n)
                        own(dve.reciprocal(y, z))
                        own(tt(z, y, y, ALU.mult))
                        own(tt(z, z, x, ALU.mult))
                        own(ts(z, z, -0.5, 1.5, ALU.mult, ALU.add))
                        own(tt(x, y, z, ALU.mult))

                    def transposed_lo(s, gains):
                        for k in range(KD):
                            dve.wait_ge(ht_hi, KD * s + k + 1)
                            gain = 1.0 if gains is None else LP[:, gains + k:gains + k + 1]
                            stt(HT_LO[:, k, :], PS[:, k % 2, :], gain, HT_HI[:, k, :].bitcast(F32), ALU.mult,
                                ALU.subtract).then_inc(ht_lo, 1)

                    def heads_of(x):
                        return x.rearrange("p i (g d) -> p i g d", d=HD)

                    squares(1)
                    mean(NT, D)
                    dve.wait_ge(rstd_done, 1)
                    for i in range(NT):
                        ts(ROWS[:, i, :], X[:, i, :], SS[:, i:i + 1], None, ALU.mult).then_inc(rows_done, 1)
                    for u in range(2):
                        split_lo(u)
                    transposed_lo(0, L_GMIX)
                    for u in range(2, 8):
                        split_lo(u)
                    dve.wait_ge(gelu_done, 1)
                    V = heads_of(TM[:, :, 1024:1280])
                    sq = B[:, :, 0:256]
                    own(tt(sq, TM[:, :, 1024:1280], TM[:, :, 1024:1280], ALU.mult))
                    own(dve.tensor_reduce(SS[:, 0:NT * H_GMLP].rearrange("p (i g) -> p i g", i=NT), heads_of(sq), AX.X,
                                          ALU.add))
                    mean(NT * H_GMLP, HD)
                    inverse_root(1, NT * H_GMLP)
                    own(tt(V, V, SS[:, 0:NT * H_GMLP].rearrange("p (i g) -> p i g", i=NT).unsqueeze(3)
                           .broadcast_to([P, NT, H_GMLP, HD]), ALU.mult))
                    own(tt(TM[:, :, 1024:1280], TM[:, :, 1024:1280], GV[:].unsqueeze(1).broadcast_to([P, NT, 256]),
                           ALU.mult))
                    WS = LP[:, L_WS:L_WR].rearrange("p (g t) -> p g t", g=H_GMLP)
                    tt(WS, WS, C[:, C_LOW:C_LOW + P].unsqueeze(1).broadcast_to([P, H_GMLP, P]), ALU.mult) \
                        .then_inc(gv_ready, 1)
                    for u in range(8, QK_UNIT + W_SLOTS + 1):
                        split_lo(u)
                    split_lo(QK_UNIT + W_SLOTS + 1)
                    for g in range(H_GMLP):
                        dve.wait_ge(spatial_done, g + 1)
                        stt(ROWS[:, :, HD * (12 + g):HD * (13 + g)],
                            PS[:, 6 + g % 2, 0:NT * HD].rearrange("p (i d) -> p i d", d=HD),
                            LP[:, L_BS + g:L_BS + g + 1], TM[:, :, 768 + HD * g:768 + HD * (g + 1)], ALU.add,
                            ALU.mult).then_inc(spatial_out, 1)

                    def next_pair(pair, q):
                        if pair == QK_CHUNKS - 1:
                            return
                        u = QK_UNIT + 2 * pair + 2 + q
                        if u + W_SLOTS < MIX_UNITS - W_SLOTS:
                            split_lo(u + W_SLOTS)

                    def rotate(pair, q):
                        x, y = QK_RAW[:, q, :], QK_OF[pair % 2][:, q, :]
                        dve.wait_ge(rot_done, 2 * (pair - 2) + q + 1)
                        own(tt(y, PS[:, q, :], ROPE[:, 1, :], ALU.mult))
                        own(tt(x, x, ROPE[:, 0, :], ALU.mult))
                        tt(y, y, x, ALU.add).then_inc(qk_ready, 1)

                    for h in range(H_SB):
                        if h:
                            dve.wait_ge(av_done, h)
                        for n, j in enumerate(reversed(range(NT))):
                            w = SEQ - P * j
                            dve.wait_ge(sb_abs, NT * h + n + 1)
                            own(ts(A[:, j, 0:w], PS[:, 2 + j, 0:w], SCALE, 0.0, ALU.mult, ALU.max))
                        for n, j in enumerate(reversed(range(NT))):
                            w = SEQ - P * j
                            dve.wait_ge(sb_ln, NT * h + n + 1)
                            tt(A[:, j, 0:w], A[:, j, 0:w], B[:, j, 0:w], ALU.add).then_inc(sb_sum, 1)
                        next_pair(h // 2, h % 2)
                        dve.wait_ge(av_done, h + 1)
                        dve.tensor_copy(ROWS[:, :, HD * h:HD * (h + 1)],
                                        PS[:, 6 + h % 2, 0:NT * HD].rearrange("p (i d) -> p i d", d=HD)) \
                            .then_inc(head_out, 1)
                    rotate(2, 0)
                    rotate(2, 1)
                    for n in range(H_MOBA):
                        pair = 2 + n // 2
                        dve.wait_ge(mo_z, n + 1)
                        for i in range(NT):
                            ins = dve.tensor_reduce(NMAX[:, 0, i:i + 1], PS[:, 2 + i, 0:P * (i + 1)], AX.X, ALU.max,
                                                    negate=True)
                        own(ins)
                        ts(NMAX[:, 1, :], NMAX[:, 0, :], SCALE, None, ALU.mult).then_inc(mo_max, 1)
                        if n % 2 and pair < QK_CHUNKS - 1:
                            rotate(pair + 1, 0)
                        dve.wait_ge(av_done, n + H_SB)
                        next_pair(pair, n % 2)
                        for i in range(NT):
                            dve.wait_ge(mo_t, NT * n + i + 1)
                            dve.tensor_copy(B[:, i, 0:P * (i + 1)], PS[:, 2 + i, 0:P * (i + 1)]).then_inc(mo_pt, 1)
                        dve.wait_ge(mo_p, NT * n + NT)
                        own(dve.reciprocal(RSUM[:, 1, :], RSUM[:, 0, :]))
                        dve.wait_ge(av_done, n + H_SB + 1)
                        tt(ROWS[:, :, HD * (n + H_SB):HD * (n + H_SB + 1)],
                           PS[:, 6 + n % 2, 0:NT * HD].rearrange("p (i d) -> p i d", d=HD),
                           RSUM[:, 1, :].unsqueeze(2).broadcast_to([P, NT, HD]), ALU.mult).then_inc(head_out, 1)
                        if n % 2 and pair < QK_CHUNKS - 1:
                            rotate(pair + 1, 1)
                    for i in range(NT):
                        dve.wait_ge(sq_done, i + 1)
                        dve.tensor_reduce(SS[:, N_HEADS * i:N_HEADS * (i + 1)],
                                          A[:, 2 * (i % 2):2 * (i % 2) + 2, :].rearrange("p a (g d) -> p (a g) d", d=HD),
                                          AX.X, ALU.add).then_inc(sq_used, 1)
                    dve.wait_ge(sq_used, NT)
                    mean(NT * N_HEADS, HD)
                    inverse_root(2, NT * N_HEADS)
                    for i in range(NT):
                        r4 = ROWS[:, i, :].rearrange("p (g d) -> p g d", d=HD)
                        tt(r4, r4, SS[:, N_HEADS * i:N_HEADS * (i + 1)].unsqueeze(2).broadcast_to([P, N_HEADS, HD]),
                           ALU.mult).then_inc(rows_done, 1)
                    transposed_lo(1, L_GHEAD)
                    for half in range(2):
                        if half == 0:
                            for u in range(MIX_UNITS - W_SLOTS, MIX_UNITS):
                                split_lo(u)
                        dve.wait_ge(mm_done, OUT_UNIT + 4 * (half + 1))
                        xq = X[:, :, 512 * half:512 * (half + 1)]
                        tt(xq, xq, PS[:, 4 * half:4 * half + NT, :], ALU.add).then_inc(x_added, 1)
                    dve.wait_ge(x_added, 2)
                    squares(2)
                    mean(NT, D)
                    dve.wait_ge(rstd_done, 2)
                    dve.wait_ge(grow_in, 16)
                    for i in range(NT):
                        stt(ROWS[:, i, :], X[:, i, :], SS[:, i:i + 1], GROW[:], ALU.mult, ALU.mult).then_inc(rows_done, 1)
                    dve.wait_ge(wr_hi, 1)
                    tt(WR_LO[:], LP[:, L_WR:L_COLS].rearrange("p (k n) -> p k n", n=NR), WR_HI[:].bitcast(F32),
                       ALU.subtract).then_inc(wr_lo, 1)
                    transposed_lo(2, None)
                    def bc(x, n):
                        return x.unsqueeze(2).broadcast_to([P, NT, n])

                    def area(a, b, cols):
                        return B[:, a, b * 128:b * 128 + NT * cols].rearrange("p (i n) -> p i n", n=cols)

                    def over(col, n):
                        return C[:, col:col + n].unsqueeze(1).broadcast_to([P, NT, n])

                    GE = A[:, 0, 0:NT * NG].rearrange("p (i n) -> p i n", n=NG)
                    G4, L, M1, M2 = area(0, 0, NG), area(0, 1, NE), area(0, 2, NE), area(0, 3, NE)
                    T1, T2, MB, POS = area(1, 0, NE), area(1, 1, NE), area(1, 2, NE), area(1, 3, NE)
                    SM = A[:, 1, 0:64].rearrange("p (a i) -> p a i", i=NT)
                    MAXG, SUMG, GSEL, TOP1, IDX1, TOP2, IDX2, PGRP = (SM[:, a, :] for a in range(8))
                    dve.wait_ge(logits, 1)
                    LG = PS[:, 2, 0:NT * 64].rearrange("p (i n) -> p i n", n=64)
                    own(dve.tensor_copy(G4, LG[:, :, 0:NG]))
                    own(dve.tensor_copy(L, LG[:, :, NG:NR]))
                    own(dve.tensor_reduce(MAXG, G4, AX.X, ALU.max))
                    tt(GE, G4, bc(MAXG, NG), ALU.subtract).then_inc(gexp_in, 1)

                    def argmax(x, top, idx, n, tmp):
                        own(tt(tmp, x, bc(top, n), ALU.is_lt))
                        own(stt(tmp, tmp, 64.0, over(C_IOTA, n), ALU.mult, ALU.add))
                        own(dve.tensor_reduce(idx, tmp, AX.X, ALU.min))

                    argmax(G4, MAXG, GSEL, NG, area(2, 0, NG))
                    own(tt(T1, over(C_GROUP, NE), bc(GSEL, NE), ALU.is_equal))
                    own(tt(L, L, T1, ALU.mult))
                    own(ts(T1, T1, -1.0, -NEG, ALU.add, ALU.mult))
                    own(tt(L, L, T1, ALU.add))
                    own(dve.tensor_reduce(TOP1, L, AX.X, ALU.max))
                    argmax(L, TOP1, IDX1, NE, T2)
                    own(tt(M1, over(C_IOTA, NE), bc(IDX1, NE), ALU.is_equal))
                    own(stt(L, M1, 2 * NEG, L, ALU.mult, ALU.add))
                    own(dve.tensor_reduce(TOP2, L, AX.X, ALU.max))
                    argmax(L, TOP2, IDX2, NE, T2)
                    own(tt(M2, over(C_IOTA, NE), bc(IDX2, NE), ALU.is_equal))
                    tt(MB, M1, M2, ALU.add).then_inc(ranks_in, 1)
                    tt(GATE[:, 1, :], TOP2, TOP1, ALU.subtract).then_inc(gexp_in, 1)
                    dve.wait_ge(gexp, 2)
                    own(dve.tensor_reduce(SUMG, GE, AX.X, ALU.add))
                    own(ts(T1[:, 0:1, 0:NT].rearrange("p a i -> p (a i)"), GATE[:, 1, :], 1.0, None, ALU.add))
                    own(tt(SUMG, SUMG, T1[:, 0:1, 0:NT].rearrange("p a i -> p (a i)"), ALU.mult))
                    own(dve.reciprocal(GATE[:, 0, :], SUMG))
                    own(tt(GATE[:, 1, :], GATE[:, 1, :], GATE[:, 0, :], ALU.mult))
                    dve.wait_ge(ranks, 1)
                    own(dve.tensor_copy(T1, PS[:, 3, 0:NT * NE].rearrange("p (i n) -> p i n", n=NE)))
                    CNT = area(3, 0, NE)[:, 0, :]
                    NV, INC, DIF, ONES = (area(3, 0, NE)[:, 1, :], area(3, 0, NE)[:, 2, :], area(3, 0, NE)[:, 3, :],
                                          C[:, C_ONES:C_ONES + NE])
                    own(dve.tensor_copy(CNT, PS[:, 3, NT * NE:NT * NE + NE]))
                    TH = A[:, 2, 0:NE * (MAX_R - 1)].rearrange("p (n r) -> p n r", r=MAX_R - 1)
                    own(tt(TH, CNT.unsqueeze(2).broadcast_to([P, NE, MAX_R - 1]),
                           C[:, C_LIMIT:C_LIMIT + MAX_R - 1].unsqueeze(1).broadcast_to([P, NE, MAX_R - 1]), ALU.is_gt))
                    own(dve.tensor_reduce(NV, TH, AX.X, ALU.add))
                    own(dve.tensor_tensor_scan(INC, ONES, NV, 0.0, ALU.mult, ALU.add))
                    own(tt(DIF, INC, NV, ALU.subtract))
                    own(ts(DIF, DIF, float(NE - 1), None, ALU.add))
                    own(tt(DIF, DIF, C[:, C_IOTA:C_IOTA + NE], ALU.subtract))
                    own(ts(T2, T1, float(ROWS_T), None, ALU.is_ge))
                    own(tt(T2, T2, DIF.unsqueeze(1).broadcast_to([P, NT, NE]), ALU.mult))
                    own(tt(T2, T2, over(C_IOTA, NE), ALU.add))
                    own(stt(POS, T2, float(ROWS_T), T1, ALU.mult, ALU.add))
                    own(tt(T2, POS, M1, ALU.mult))
                    own(dve.tensor_reduce(IDX1, T2, AX.X, ALU.add))
                    own(tt(T2, POS, M2, ALU.mult))
                    own(dve.tensor_reduce(IDX2, T2, AX.X, ALU.add))
                    own(dve.tensor_copy(SLOT[:, 0, :], IDX1))
                    dve.tensor_copy(SLOT[:, 1, :], IDX2).then_inc(slots, 1)
                    TJ = A[0:1, 3, 0:MORE * NE].rearrange("p (j n) -> p j n", n=NE)
                    EJ = A[0:1, 1, 64:64 + MORE + 1]
                    own(tt(TJ, INC[0:1, :].unsqueeze(1).broadcast_to([1, MORE, NE]),
                           C[0:1, C_IOTA:C_IOTA + MORE].unsqueeze(2).broadcast_to([1, MORE, NE]), ALU.is_le))
                    own(dve.tensor_reduce(EJ[:, 0:MORE], TJ, AX.X, ALU.add))
                    own(ts(EJ[:, 0:MORE], EJ[:, 0:MORE], float(NE - 1), None, ALU.min))
                    own(dve.tensor_copy(EJ[:, MORE:MORE + 1], INC[0:1, NE - 1:NE]))
                    dve.tensor_copy(TILE_TAB[:], EJ).then_inc(table, 1)

                    def lo_own(t, u):
                        slot = (MIX_UNITS + u) % W_SLOTS
                        dve.wait_ge(hi_done, t * OWN_UNITS + (MIX_UNITS + u + 1))
                        tt(W_LO[:, slot, :], RAW[:, u // 2, UNIT * (u % 2):UNIT * (u % 2 + 1)],
                           W_HI[:, slot, :].bitcast(F32), ALU.subtract).then_inc(lo_done, 1)

                    def rows_lo(t):
                        dve.wait_ge(xt_hi, t + 1)
                        tt(two(XT_LO), XT_PS, two(XT_HI).bitcast(F32), ALU.subtract) \
                            .then_inc(xt_ready, 1)

                    def tile(t, more):
                        for u in range(4, 11):
                            lo_own(t, u)
                        dve.wait_ge(mm_done, t * OWN_UNITS + (MIX_UNITS + 8))
                        dve.wait_ge(sil_done, t + 1)
                        tt(ACTED, SIL, PS[0:ROWS_T, 1, :], ALU.mult).then_inc(act_done, 1)
                        dve.wait_ge(at_hi, t + 1)
                        tt(AT_LO, AT_PS, AT_HI.bitcast(F32), ALU.subtract).then_inc(at_lo, 1)
                        lo_own(t, 11)
                        rows_lo(t + 1)
                        if more:
                            for u in range(4):
                                lo_own(t + 1, u)

                    for u in range(4):
                        lo_own(0, u)
                    rows_lo(0)
                    with dve.Fori(0, NE - 1) as t:
                        tile(t, True)
                    tile(NE - 1, False)
                    n_more = dve.value_load(TILE_TAB[0:1, MORE:MORE + 1], min_val=0, max_val=MORE)
                    with dve.If(n_more > 0):
                        for u in range(4):
                            lo_own(NE, u)
                        with dve.Fori(NE, TILES - 1) as t:
                            tile(t, True)
                        tile(TILES - 1, False)
                    for i in range(NT):
                        dve.wait_ge(gather_in[i], l * 32 + 32)
                        for s in range(2):
                            own(stt(X[:, i, :], GATHER[:, 2 * i + s, :], GATE[:, s, i:i + 1], X[:, i, :], ALU.mult,
                                    ALU.add))

                @block.tensor
                def _(pe):
                    def transpose_rows(s):
                        pe.wait_ge(rows_done, NT * (s + 1))
                        for k in range(KD):
                            if k >= 2:
                                pe.wait_ge(ht_lo, KD * s + k - 1)
                            for i in range(NT):
                                ins = pe.transpose(PS[:, k % 2, P * i:P * (i + 1)],
                                                   ROWS[:, i, :].rearrange("p (m k) -> p m k", k=KD)[:, :, k], IDENT)
                            ins.then_inc(tr_done, 1)

                    def by_tokens(u0, width, chunks, bank):
                        ks = KD // (2 * chunks)
                        for n in range(2 * chunks):
                            slot = (u0 + n) % W_SLOTS
                            pe.wait_ge(lo_done, u0 + n + 1)
                            w_hi = W_HI[:, slot, :].rearrange("p (k n) -> p k n", n=width)
                            w_lo = W_LO[:, slot, :].rearrange("p (k n) -> p k n", n=width)
                            for i in range(NT):
                                tokens = slice(P * i, P * (i + 1))
                                for kk in range(ks):
                                    k = ks * n + kk
                                    ins = product3(pe, PS[:, bank + i, 0:width], HT_HI[:, k, tokens], HT_LO[:, k, tokens],
                                                   w_hi[:, kk, :], w_lo[:, kk, :], k == 0, k == KD - 1)
                            ins.then_inc(mm_done, 1)

                    def project(pair, q):
                        if pair == QK_CHUNKS:
                            return
                        u = QK_UNIT + 2 * pair + q
                        pe.wait_ge(lo_done, u + 1)
                        w_hi = W_HI[:, u % W_SLOTS, :].rearrange("p (k n) -> p k n", k=KD)
                        w_lo = W_LO[:, u % W_SLOTS, :].rearrange("p (k n) -> p k n", k=KD)
                        for k in range(KD):
                            ins = product3(pe, PS[:, q, :], w_hi[:, k, :], w_lo[:, k, :], HT_HI[:, k, :], HT_LO[:, k, :],
                                           k == 0, k == KD - 1)
                        ins.then_inc(mm_done, 1)

                    def rotated(pair, q):
                        if pair == QK_CHUNKS:
                            return
                        pe.wait_ge(qk_out, 1 + 2 * (pair - 1) + q + 1)
                        pe.matmul(PS[:, q, :], C[:, C_ROT:C_ROT + P], QK_RAW[:, q, :], start=True, stop=True) \
                            .then_inc(rot_done, 1)

                    transpose_rows(0)
                    pe.wait_ge(ht_lo, KD)
                    u = 0
                    for g, (_, width, chunks) in enumerate(TM_GROUPS):
                        if g == 2:
                            pe.wait_ge(tm_out, 1)
                        by_tokens(u, width, chunks, 4 * (g % 2))
                        u += 2 * chunks
                    pe.wait_ge(tm_out, len(TM_GROUPS))
                    project(0, 0)
                    project(0, 1)
                    pe.wait_ge(gv_ready, 1)
                    for g in range(H_GMLP):
                        if g >= 2:
                            pe.wait_ge(spatial_out, g - 1)
                        pe.matmul(PS[:, 6 + g % 2, 0:NT * HD], LP[:, L_WS + P * g:L_WS + P * (g + 1)],
                                  TM[:, :, 1024 + HD * g:1024 + HD * (g + 1)], start=True, stop=True) \
                            .then_inc(spatial_done, 1)
                    for h in range(H_SB):
                        pair, hh = h // 2, h % 2
                        part = slice(HD * hh, HD * (hh + 1))
                        q_t, k_t = QK_OF[pair][:, 0, :], QK_OF[pair][:, 1, :]
                        pe.wait_ge(qk_out, 1 if h < 2 else 3)
                        if h:
                            pe.wait_ge(sb_w, NT * h)
                        for j in reversed(range(NT)):
                            pe.matmul(PS[:, 2 + j, 0:SEQ - P * j], k_t[part, P * j:P * (j + 1)], q_t[part, P * j:SEQ],
                                      start=True, stop=True).then_inc(sb_z, 1)
                        project(pair + 1, hh)
                        for n, j in enumerate(reversed(range(NT))):
                            pe.wait_ge(sb_masked, NT * h + n + 1)
                            for jj in reversed(range(j + 1, NT)):
                                pe.matmul(PS[:, 2 + j, P * (jj - j):SEQ - P * j], C[:, C_ONE8:C_ONE8 + P],
                                          A[:, jj, 0:SEQ - P * jj], start=False, stop=False, skip_group_check=True)
                            pe.matmul(PS[:, 2 + j, 0:SEQ - P * j], C[:, C_TRI8:C_TRI8 + P], A[:, j, 0:SEQ - P * j],
                                      start=False, stop=True, skip_group_check=True).then_inc(sb_r, 1)
                        if h == 3:
                            rotated(2, 0)
                        if h < 2:
                            pe.wait_ge(spatial_out, H_GMLP)
                        else:
                            pe.wait_ge(head_out, h - 1)
                        pe.wait_ge(sb_wm, NT * (h + 1))
                        for i in range(NT):
                            for j in range(i + 1):
                                ins = pe.matmul(PS[:, 6 + hh, HD * i:HD * (i + 1)], B[:, j, P * (i - j):P * (i - j + 1)],
                                                TM[:, j, HD * h:HD * (h + 1)], start=(j == 0), stop=(j == i))
                        ins.then_inc(av_done, 1)
                    rotated(2, 1)
                    pe.wait_ge(sb_w, NT * H_SB)
                    for n in range(H_MOBA):
                        pair, hh = 2 + n // 2, n % 2
                        part = slice(HD * hh, HD * (hh + 1))
                        q_t, k_t = QK_OF[pair % 2][:, 0, :], QK_OF[pair % 2][:, 1, :]
                        pe.wait_ge(qk_ready, 2 * (n // 2) + 2)
                        for i in range(NT):
                            q = q_t[part, P * i:P * (i + 1)]
                            if i:
                                pe.matmul(PS[:, 2 + i, 0:P * i], q, k_t[part, 0:P * i], start=True, stop=True)
                            own_keys = PS[:, 2 + i, P * i:P * (i + 1)]
                            pe.matmul(own_keys, q, k_t[part, P * i:P * (i + 1)], start=True, stop=False)
                            ins = pe.matmul(own_keys, IDENT, C[:, C_NEG:C_NEG + P], start=False, stop=True)
                        ins.then_inc(mo_z, 1)
                        if hh and pair < QK_CHUNKS - 1:
                            rotated(pair + 1, 0)
                        project(pair + 1, hh)
                        for i in range(NT):
                            pe.wait_ge(mo_p, NT * n + i + 1)
                            for j in range(i + 1):
                                ins = pe.transpose(PS[:, 2 + i, P * j:P * (j + 1)], A[:, i, P * j:P * (j + 1)], IDENT)
                            ins.then_inc(mo_t, 1)
                        pe.wait_ge(head_out, n + H_SB - 1)
                        for i in range(NT):
                            pe.wait_ge(mo_pt, NT * n + i + 1)
                            for j in range(i + 1):
                                ins = pe.matmul(PS[:, 6 + hh, HD * i:HD * (i + 1)], B[:, i, P * j:P * (j + 1)],
                                                TM[:, j, HD * (n + H_SB):HD * (n + H_SB + 1)], start=(j == 0),
                                                stop=(j == i))
                        ins.then_inc(av_done, 1)
                        if hh and pair < QK_CHUNKS - 1:
                            rotated(pair + 1, 1)
                    pe.wait_ge(head_out, H_SB + H_MOBA)
                    transpose_rows(1)
                    pe.wait_ge(ht_lo, 2 * KD)
                    for half in range(2):
                        by_tokens(OUT_UNIT + 4 * half, 512, 2, 4 * half)
                    pe.wait_ge(x_added, 2)
                    transpose_rows(2)
                    pe.wait_ge(ht_lo, 3 * KD)
                    pe.wait_ge(wr_lo, 1)
                    for i in range(NT):
                        for k in range(KD):
                            ins = product3(pe, PS[:, 2, 64 * i:64 * i + NR], HT_HI[:, k, P * i:P * (i + 1)],
                                           HT_LO[:, k, P * i:P * (i + 1)], WR_HI[:, k, :], WR_LO[:, k, :], k == 0,
                                           k == KD - 1)
                    ins.then_inc(logits, 1)
                    pe.wait_ge(ranks_in, 1)
                    chosen = [B[:, 1, 256 + NE * i:256 + NE * (i + 1)] for i in range(NT)]
                    for i in range(NT):
                        for b in range(i):
                            pe.matmul(PS[:, 3, NE * i:NE * (i + 1)], C[:, C_ONES:C_ONES + P], chosen[b], start=(b == 0),
                                      stop=False)
                        pe.matmul(PS[:, 3, NE * i:NE * (i + 1)], C[:, C_BEFORE:C_BEFORE + P], chosen[i], start=(i == 0),
                                  stop=True)
                    for b in range(NT):
                        ins = pe.matmul(PS[:, 3, NE * NT:NE * (NT + 1)], C[:, C_ONES:C_ONES + P], chosen[b],
                                        start=(b == 0), stop=(b == NT - 1))
                    ins.then_inc(ranks, 1)

                    def transpose_tile(t):
                        pe.wait_ge(xs_in, 16 * (t + 1))
                        pe.wait_ge(xt_ready, t)
                        for k in range(KD):
                            ins = pe.transpose(XT_PS[:, k // 4, k % 4, :],
                                               XS.rearrange("p (m k) -> p m k", k=KD)[:, :, k],
                                               C[0:ROWS_T, C_IDENT:C_IDENT + ROWS_T])
                        ins.then_inc(xs_t, 1)

                    def tile(t):
                        def parts(u, n):
                            pe.wait_ge(lo_done, t * OWN_UNITS + (MIX_UNITS + u + 1))
                            slot = (MIX_UNITS + u) % W_SLOTS
                            return (W_HI[:, slot, :].rearrange("p (k n) -> p k n", n=n),
                                    W_LO[:, slot, :].rearrange("p (k n) -> p k n", n=n))

                        pe.wait_ge(xt_ready, t + 1)
                        for u in range(8):
                            w_hi, w_lo = parts(u, FE)
                            for kk in range(2):
                                k = 2 * (u % 4) + kk
                                ins = product3(pe, PS[0:ROWS_T, u // 4, :], XT_HI[:, k, :], XT_LO[:, k, :],
                                               w_hi[:, kk, :], w_lo[:, kk, :], k == 0, k == KD - 1)
                            ins.then_inc(mm_done, 1)
                        transpose_tile(t + 1)
                        pe.wait_ge(act_done, t + 1)
                        for k in range(KF):
                            ins = pe.transpose(AT_PS[:, k, :], ACTED.rearrange("p (m k) -> p m k", k=KF)[:, :, k],
                                               C[0:ROWS_T, C_IDENT:C_IDENT + ROWS_T])
                        ins.then_inc(at_t, 1)
                        pe.wait_ge(at_lo, t + 1)
                        for k in range(KF):
                            w_hi, w_lo = parts(8 + k, D)
                            for half in range(2):
                                cols = slice(512 * half, 512 * (half + 1))
                                ins = product3(pe, PS[0:ROWS_T, 2 + half, :], AT_HI[:, k, :], AT_LO[:, k, :],
                                               w_hi[:, 0, cols], w_lo[:, 0, cols], k == 0, k == KF - 1)
                            ins.then_inc(mm_done, 1)

                    transpose_tile(0)
                    with pe.Fori(0, NE) as t:
                        tile(t)
                    pe.wait_ge(table, 1)
                    n_more = pe.value_load(TILE_TAB[0:1, MORE:MORE + 1], min_val=0, max_val=MORE)
                    with pe.If(n_more > 0):
                        with pe.Fori(NE, TILES) as t:
                            tile(t)

            nc.all_engine_barrier(sems_to_clear=range(first.num, last.num + 1))

        with nc.Block() as block:
            @block.scalar
            def _(act):
                for i in range(NT):
                    act.activation(ROWS[:, i, :], X[:, i, :], ACT.Square, accum_out=SS[:, i:i + 1]).then_inc(fin_ss, 1)

            @block.gpsimd
            def _(pool):
                pool.wait_ge(fin_ms, 1)
                pool.tensor_tensor(SS[:, 0:NT], SS[:, 0:NT], MINUS_HALF[:, 0:NT], ALU.pow).then_inc(fin_rstd, 1)

            @block.vector
            def _(dve):
                dve.wait_ge(fin_ss, NT)
                dve.tensor_scalar(SS[:, 0:NT], SS[:, 0:NT], 1.0 / D, EPS, ALU.mult, ALU.add).then_inc(fin_ms, 1)
                dve.wait_ge(fin_rstd, 1)
                dve.wait_ge(gfin_in, 16)
                for i in range(NT):
                    dve.scalar_tensor_tensor(ROWS[:, i, :], X[:, i, :], SS[:, i:i + 1], GROW[:], ALU.mult, ALU.mult) \
                       .then_inc(fin_rows, 1)

            @block.sync
            def _(sp):
                sp.dma_start(GROW[:], gfin_d.partition_broadcast(P)).then_inc(gfin_in, 16)
                for i in range(NT):
                    sp.wait_ge(fin_rows, i + 1)
                    sp.dma_start(out_d[i * P:(i + 1) * P, :], ROWS[:, i, :]).then_inc(out_stored, 16)
                sp.wait_ge(out_stored, 16 * NT)


def constants():
    c = np.zeros((P, C_COLS), np.float32)
    row, col = np.arange(P)[:, None], np.arange(P)[None, :]
    c[:, C_IDENT:C_IDENT + P] = row == col
    half = ROT // 2
    d_in, d_out, same = row % HD, col % HD, row // HD == col // HD
    c[:, C_ROT:C_ROT + P] = np.where(same & (d_out < half) & (d_in == d_out + half), -1.0, 0.0) + np.where(
        same & (d_out >= half) & (d_out < ROT) & (d_in == d_out - half), 1.0, 0.0)
    c[:, C_NEG:C_NEG + P] = np.where(col > row, NEG, 0.0)
    c[:, C_TRI8:C_TRI8 + P] = np.where(row >= col, -1.0 / SCALE, 0.0)
    c[:, C_ONE8:C_ONE8 + P] = -1.0 / SCALE
    c[:, C_LOW:C_LOW + P] = col >= row
    c[:, C_BEFORE:C_BEFORE + P] = row < col
    c[:, C_ONES:C_ONES + P] = 1.0
    freq = np.power(np.float32(THETA), -np.arange(half, dtype=np.float32) / np.float32(half)).astype(np.float32)
    d = np.arange(P) % HD
    c[:, C_FREQ] = np.where(d < ROT, freq[d % half], 0.0)
    c[:, C_IOTA:C_IOTA + NE] = np.arange(NE)
    c[:, C_GROUP:C_GROUP + NE] = np.arange(NE) // EPG
    c[:, C_LIMIT:C_LIMIT + MAX_R - 1] = ROWS_T * np.arange(1, MAX_R)
    return c


def kernel(x, positions, w_in, w_out, g_mix_norm, g_head_norm, g_gmlp_vnorm, w_spatial, b_spatial, g_ffn_norm,
           w_router_group, w_router_expert, w_expert_gate, w_expert_up, w_expert_down, g_final):
    import concourse.bacc as bacc
    from concourse.bass_utils import run_bass_kernel_spmd

    w_in, w_out = np.asarray(w_in), np.asarray(w_out)
    wsb, wmo = H_SB * HD, H_MOBA * HD
    rows = w_in.reshape(DEPTH, P, KD, -1)
    qa, ka, va, qb, kb, vb, uv = np.split(rows, np.cumsum([wsb] * 3 + [wmo] * 3), axis=-1)
    chunks = []
    for w in (uv, vb, va):
        n = w.shape[-1] * KD // CHUNK
        chunks += [w[:, :, c * (KD // n):(c + 1) * (KD // n)].reshape(DEPTH, P, CHUNK) for c in range(n)]
    for q, k in ((qa, ka), (qb, kb)):
        for c in range(q.shape[-1] // P):
            pair = np.stack([q[..., P * c:P * (c + 1)], k[..., P * c:P * (c + 1)]], axis=2)
            chunks.append(pair.reshape(DEPTH, P, CHUNK))
    out_rows = w_out.reshape(DEPTH, P, KD, D)
    for cols in (slice(0, 512), slice(512, D)):
        chunks += [out_rows[:, :, k:k + KD // 2, cols].reshape(DEPTH, P, CHUNK) for k in (0, KD // 2)]
    mix = np.ascontiguousarray(np.stack(chunks, axis=1)).reshape(DEPTH * MIX_CHUNKS, P, CHUNK)

    router = np.concatenate([np.asarray(w_router_group), np.asarray(w_router_expert)], axis=-1)
    lay = np.concatenate([
        np.asarray(g_mix_norm).reshape(DEPTH, P, KD),
        np.asarray(g_head_norm).reshape(DEPTH, P, KD),
        np.asarray(b_spatial).transpose(0, 2, 1),
        np.asarray(w_spatial).transpose(0, 3, 1, 2).reshape(DEPTH, P, H_GMLP * P),
        router.reshape(DEPTH, P, KD * NR),
    ], axis=-1)
    arrays = {
        "x": np.asarray(x).reshape(SEQ, D),
        "positions": np.asarray(positions).reshape(SEQ),
        "mix": mix,
        "lay": np.ascontiguousarray(lay),
        "g_vnorm": np.asarray(g_gmlp_vnorm).reshape(DEPTH, H_GMLP * HD),
        "g_ffn": np.asarray(g_ffn_norm),
        "w_gate": np.asarray(w_expert_gate),
        "w_up": np.asarray(w_expert_up),
        "w_down": np.asarray(w_expert_down),
        "g_final": np.asarray(g_final),
        "constants": constants(),
    }
    nc = bacc.Bacc("TRN2", target_bir_lowering=False, num_devices=1)
    ins = [nc.dram_tensor(n, a.shape, mybir.dt.from_np(a.dtype), kind="ExternalInput").ap() for n, a in arrays.items()]
    out = nc.dram_tensor("out", (SEQ, D), F32, kind="ExternalOutput").ap()
    build(nc, *ins, out)
    r = run_bass_kernel_spmd(nc, [arrays], core_ids=[0])
    return r.results[0]["out"].reshape(1, SEQ, D)
```

```python
import contextlib

import numpy as np
import concourse.bass as bass
from concourse import mybir

F32 = mybir.dt.float32
F32R = mybir.dt.float32r
I32 = mybir.dt.int32
U32 = mybir.dt.uint32
ACT = mybir.ActivationFunctionType
ALU = mybir.AluOpType
AX = mybir.AxisListType

P = 128
DEPTH, SEQ, D = 2, 512, 1024
NT = SEQ // P
KD = D // P
HD = 64
N_HEADS = D // HD
H_SB, H_MOBA, H_GMLP = 4, 8, 4
H_SOFT = H_SB + H_MOBA
ROT = HD // 4
THETA = 500000.0
EPS = 1e-6
SCALE = HD ** -0.5
NEG = -1e30

AT = {4: 0, 3: 4 * P, 1: 7 * P, 2: 8 * P}
SCORES = 10 * P

CHUNK = 2048
UNIT = CHUNK // 2
W_SLOTS = 4
TM_GROUPS = ((768, 512, 2), (256, 512, 2), (0, 256, 1))
TM_CHUNKS = 5
QK_CHUNKS = 6
OUT_CHUNKS = 4
MIX_CHUNKS = TM_CHUNKS + QK_CHUNKS + OUT_CHUNKS
MIX_UNITS = 2 * MIX_CHUNKS
QK_UNIT = 2 * TM_CHUNKS
OUT_UNIT = QK_UNIT + 2 * QK_CHUNKS
RAW_SLOTS = 6
OUT_ORDER = (6, 7, 0, 1, 2, 3, 4, 5)

NE, NG, EPG = 32, 4, 8
FE = D // 2
KF = FE // P
ROWS_T = 96
MORE = (2 * SEQ - 2) // ROWS_T
HALF = ROWS_T // 2
TILES = NE + MORE
OWN_CHUNKS = 6
OWN_UNITS = 2 * OWN_CHUNKS
XS_ROWS = -(-(TILES + 2) * ROWS_T // P) * P
MAX_R = -(-SEQ // ROWS_T)
assert NE % 2 == 0 and MORE % 2 == 0 and RAW_SLOTS == OWN_CHUNKS

C_IDENT, C_ROT, C_NEG, C_TRI8, C_ONE8, C_LOW, C_BEFORE, C_ONES = (P * n for n in range(8))
C_FREQ = 8 * P
C_IOTA = C_FREQ + 1
C_GROUP = C_IOTA + NE
C_LIMIT = C_GROUP + NE
C_COLS = C_LIMIT + MAX_R - 1
L_GMIX, L_GHEAD, L_GFFN, L_BS = 0, KD, 2 * KD, 3 * KD
L_WS = L_BS + H_GMLP
L_WR = L_WS + H_GMLP * P
NR = NG + NE
L_COLS = L_WR + KD * NR

TWO_PI = (6.28125, float(np.float32(1.9350051879882812e-3)), float(np.float32(3.0199157663725e-7)))
ROUND = 12582912.0


def build(nc, x_d, pos_d, mix_d, lay_d, gv_d, gffn_d, wg_d, wu_d, wd_d, gfin_d, const_d, out_d):
    xs_d = nc.dram_tensor("expert_rows_in", (XS_ROWS, D), F32).ap()
    ys_d = nc.dram_tensor("expert_rows_out", (XS_ROWS, D), F32).ap()
    wg_v = wg_d.rearrange("l e (p k) n -> (l e) p (k n)", k=KD)
    wu_v = wu_d.rearrange("l e (p k) n -> (l e) p (k n)", k=KD)
    wd_v = wd_d.rearrange("l e (p k) n -> (l e) p (k n)", k=KF)

    with contextlib.ExitStack() as ctx:
        def sb(name, shape, dt=F32):
            return ctx.enter_context(nc.sbuf_tensor(name, shape, dt))

        def sem(name):
            return ctx.enter_context(nc.semaphore(name))

        def same_place(name, cols, dt):
            return nc.alloc_sbuf_tensor_at(name, [P, cols], dt, offset=nc.sbuf_base - cols * 4)

        X = sb("X", [P, NT, D])
        ROWS = sb("ROWS", [P, NT, D])
        HT_HI = sb("HT_HI", [P, KD, SEQ], F32R)
        HT_HI_FREE = same_place("HT_HI_FREE", KD * SEQ, F32)
        HT_LO = sb("HT_LO", [P, KD, SEQ], F32R)
        HT_LO_FREE = same_place("HT_LO_FREE", KD * SEQ, F32)
        TM = sb("TM", [P, NT, TM_CHUNKS * 256])
        RAW = sb("RAW", [P, RAW_SLOTS, CHUNK])
        W_HI = sb("W_HI", [P, W_SLOTS, UNIT], F32R)
        W_LO = sb("W_LO", [P, W_SLOTS, UNIT], F32R)
        ROPE = sb("ROPE", [P, 2, SEQ])
        QK = sb("QK", [P, 2, SEQ])
        HEAD_A = sb("HEAD_A", [P, 2, SCORES])
        HEAD_B = sb("HEAD_B", [P, 2, SCORES])
        TILE_PARTS = same_place("TILE_PARTS", 2 * SCORES, F32R)
        LP = sb("LP", [P, L_COLS])
        GV = sb("GV", [P, H_GMLP * HD])
        GROW = sb("GROW", [P, D])
        C = sb("C", [P, C_COLS])
        WR_HI = sb("WR_HI", [P, KD, NR], F32R)
        WR_LO = sb("WR_LO", [P, KD, NR], F32R)
        ROOT = sb("ROOT", [P, 2, NT * H_GMLP])
        SS = sb("SS", [P, N_HEADS * NT])
        MINUS_HALF = sb("MINUS_HALF", [P, NT * H_GMLP])
        NMAX = sb("NMAX", [P, 4, NT])
        RSUM = sb("RSUM", [P, 4, NT])
        SLOT = sb("SLOT", [P, 2, NT], U32)
        GATE = sb("GATE", [P, 2, NT])
        TILE_TAB = sb("TILE_TAB", [1, MORE + 1], I32)
        FULL_TAB = sb("FULL_TAB", [1, NE + 2], I32)

        PS = ctx.enter_context(nc.psum_tensor("PS", [P, 8, 512], F32))

        A = HEAD_A[:].rearrange("p a n -> p (a n)")[:, 0:NT * SEQ].rearrange("p (i n) -> p i n", i=NT)
        B = HEAD_B[:].rearrange("p a n -> p (a n)")[:, 0:NT * SEQ].rearrange("p (i n) -> p i n", i=NT)
        DIAG = A[:, 3, :].rearrange("p (i n) -> p i n", i=NT)
        SET_BANKS = [PS[:, b:b + 3, :].rearrange("p b n -> p (b n)")[:, 0:SCORES] for b in (2, 5)]
        VALUES_OUT = [PS[:, 1, c:c + NT * HD].rearrange("p (i d) -> p i d", d=HD) for c in (0, 256)]

        QK_OF = [QK, TM[:, 0:2, 768:1280]]
        QK_RAW = TM[:, 2:4, 768:1280]
        TM_FLAT = TM[:].rearrange("p i n -> p (i n)")
        XS = [ROWS[0:ROWS_T, 2 + odd, :] for odd in range(2)]
        YB = [ROWS[0:ROWS_T, odd, :] for odd in range(2)]
        SIL = TM_FLAT[0:ROWS_T, 0:FE]
        ACTED = TM_FLAT[0:ROWS_T, FE:2 * FE]
        x_cols, a_cols = KD * ROWS_T, KF * ROWS_T
        XT_HI, XT_LO = (TILE_PARTS[:, c:c + x_cols].rearrange("p (k t) -> p k t", k=KD) for c in (0, x_cols))
        AT_HI, AT_LO = (TILE_PARTS[:, c:c + a_cols].rearrange("p (k t) -> p k t", k=KF)
                        for c in (2 * x_cols, 2 * x_cols + a_cols))
        ODD_RAW = [TM_FLAT[:, 2 * FE + CHUNK * n:2 * FE + CHUNK * (n + 1)] for n in range(2)]
        ODD_RAW += [(HT_HI_FREE, HT_LO_FREE)[n // 2][:, CHUNK * (n % 2):CHUNK * (n % 2 + 1)] for n in range(4)]
        GATHER = [(HT_HI_FREE, HT_LO_FREE)[n // 4][:, D * (n % 4):D * (n % 4 + 1)] for n in range(2 * NT)]
        IDENT = C[:, C_IDENT:C_IDENT + P]
        XT_PS = PS[:, 4:6, 0:KD * ROWS_T // 2].rearrange("p b (k t) -> p b k t", t=ROWS_T)
        AT_PS = PS[:, 6, 0:KF * ROWS_T].rearrange("p (k t) -> p k t", k=KF)
        LOGITS_T = A[0:NR, 2, :]

        def out_blocks(g):
            n = 2 * (g - (H_SOFT - 4))
            return [b for b in (n, n + 1) if 0 <= b < KD - 1]

        def slot_of(odd, j):
            return ODD_RAW[j] if odd else RAW[:, (MIX_CHUNKS + j) % RAW_SLOTS, :]

        def slot_in(odd, j):
            return odd_in[j] if odd else raw_in[(MIX_CHUNKS + j) % RAW_SLOTS]

        def slot_count(i, odd, j):
            return i + (1 if odd else (MIX_CHUNKS + j) // RAW_SLOTS)

        def raw_of(odd, u):
            return slot_of(odd, u // 2)[:, UNIT * (u % 2):UNIT * (u % 2 + 1)]

        def two(x):
            return x.rearrange("p (b k) t -> p b k t", b=2)

        first = sem("layer_sems_begin")
        odd_in = [sem(f"odd_in{j}") for j in range(OWN_CHUNKS)]
        raw_in = [sem(f"raw_in{s}") for s in range(RAW_SLOTS)]
        grow_in = sem("grow_in")
        hi_done, lo_done, mm_done = sem("hi_done"), sem("lo_done"), sem("mm_done")
        diag_done = sem("diag_done")
        v_ms = sem("v_ms")
        head_ms, head_rstd, head_normed = sem("head_ms"), sem("head_rstd"), sem("head_normed")
        ffn_ss, ffn_ms, ffn_rstd = sem("ffn_ss"), sem("ffn_ms"), sem("ffn_rstd")
        x_new, x_ss, x_ms, x_rstd = sem("x_new"), sem("x_ss"), sem("x_ms"), sem("x_rstd")
        root_done = sem("root_done")
        rows_done, tr_done, ht_hi, ht_lo = sem("rows_done"), sem("tr_done"), sem("ht_hi"), sem("ht_lo")
        tm_out = sem("tm_out")
        gelu_done, gv_ready, spatial_done, spatial_out = (
            sem("gelu_done"), sem("gv_ready"), sem("spatial_done"), sem("spatial_out"))
        qk_out, rot_done, qk_ready = sem("qk_out"), sem("rot_done"), sem("qk_ready")
        scores_done, rot_read = sem("scores_done"), sem("rot_read")
        sb_abs, sb_ln, sb_sum, sb_masked, sb_r, sb_w, sb_wm = (
            sem("sb_abs"), sem("sb_ln"), sem("sb_sum"), sem("sb_masked"), sem("sb_r"), sem("sb_w"), sem("sb_wm"))
        mo_low = sem("mo_low")
        mo_max, mo_p, mo_t, mo_pt = sem("mo_max"), sem("mo_p"), sem("mo_t"), sem("mo_pt")
        av_done, head_out = sem("av_done"), sem("head_out")
        x_added = sem("x_added")
        wr_hi, wr_lo, logits = sem("wr_hi"), sem("wr_lo"), sem("logits")
        logits_t, logits_sb = sem("logits_t"), sem("logits_sb")
        gexp_in, gexp, ranks_in, ranks, slots, table = (
            sem("gexp_in"), sem("gexp"), sem("ranks_in"), sem("ranks"), sem("slots"), sem("table"))
        xs_in = [sem("xs_in_even"), sem("xs_in_odd")]
        xs_t, xt_ready = sem("xs_t"), sem("xt_ready")
        sil_done, act_done, at_t, at_hi, at_lo, xt_hi = (
            sem("sil_done"), sem("act_done"), sem("at_t"), sem("at_hi"), sem("at_lo"), sem("xt_hi"))
        y_copied = sem("y_copied")
        y_stored = [sem("y_stored_even"), sem("y_stored_odd")]
        act_own, dve_own = sem("act_own"), sem("dve_own")
        last = sem("layer_sems_end")
        lay_in = sem("lay_in")
        pre_in = [sem(f"pre_in{s}") for s in range(RAW_SLOTS)]
        zeroed = sem("zeroed")
        scatter_in = sem("scatter_in")
        gather_in = [sem(f"gather_in{i}") for i in range(NT)]
        consts_in, setup, out_stored, gfin_in = sem("consts_in"), sem("setup"), sem("out_stored"), sem("gfin_in")
        fin_rows = sem("fin_rows")
        angles_in, first_ss, first_ms, first_rstd = sem("angles_in"), sem("first_ss"), sem("first_ms"), sem("first_rstd")

        exp_tables = "natural_log_exp_and_others"
        zero_count = []

        class Own:

            def __init__(self, eng, s):
                self.eng, self.s, self.n = eng, s, 0

            def __call__(self, ins):
                self.n += 1
                ins.then_inc(self.s, 1)
                self.eng.wait_ge(self.s, self.n)

        def product3(pe, out, a_hi, a_lo, b_hi, b_lo, start, stop):
            pe.matmul(out, a_hi, b_hi, start=start, stop=False)
            pe.matmul(out, a_hi, b_lo, start=False, stop=False)
            return pe.matmul(out, a_lo, b_hi, start=False, stop=stop)

        def load_layer(sp, layer, gathered=None):
            sp.dma_start(LP[:], lay_d[bass.ds(layer, 1), :, :].rearrange("l p n -> (l p) n")).then_inc(lay_in, 16)
            sp.dma_start(GV[:], gv_d[bass.ds(layer, 1), :].rearrange("l n -> (l n)").partition_broadcast(P)) \
              .then_inc(lay_in, 16)
            for c in range(RAW_SLOTS):
                if c == 1 and gathered is not None:
                    sp.wait_ge(gather_in[NT - 1], gathered)
                sp.dma_start(RAW[:, c, :],
                             mix_d[bass.ds(layer * MIX_CHUNKS + c, 1), :, :].rearrange("c p n -> (c p) n")) \
                  .then_inc(pre_in[c], 16)

        with nc.Block() as block:
            @block.sync
            def _(sp):
                sp.dma_start(A[:, 0, :].bitcast(I32), pos_d.partition_broadcast(P)).then_inc(angles_in, 16)
                sp.dma_start(C[:], const_d).then_inc(angles_in, 16)
                sp.dma_start(X[:], x_d.rearrange("(i p) d -> p i d", p=P)).then_inc(consts_in, 16)
                load_layer(sp, 0)

            @block.gpsimd
            def _(pool):
                pool.memset(MINUS_HALF[:], -0.5).then_inc(setup, 1)
                pool.memset(GROW[:], 0.0)
                pool.wait_ge(first_ms, 1)
                pool.wait_ge(setup, 1)
                pool.tensor_tensor(SS[:, 0:NT], SS[:, 0:NT], MINUS_HALF[:, 0:NT], ALU.pow).then_inc(first_rstd, 1)

            @block.vector
            def _(dve):
                n = [1]

                def own(ins):
                    n[0] += 1
                    ins.then_inc(setup, 1)
                    dve.wait_ge(setup, n[0])

                ang, turns, cosx = A[:, 1, :], A[:, 2, :], A[:, 3, :]
                dve.wait_ge(angles_in, 32)
                dve.wait_ge(setup, 1)
                own(dve.tensor_copy(B[:, 0, :], A[:, 0, :].bitcast(I32)))
                own(dve.tensor_scalar(ang, B[:, 0, :], C[:, C_FREQ:C_FREQ + 1], None, ALU.mult))
                own(dve.tensor_scalar(turns, ang, float(1 / (2 * np.pi)), ROUND, ALU.mult, ALU.add))
                own(dve.tensor_scalar(turns, turns, -ROUND, None, ALU.add))
                for part in TWO_PI:
                    own(dve.scalar_tensor_tensor(ang, turns, -part, ang, ALU.mult, ALU.add))
                own(dve.tensor_scalar(ang, ang, float(np.float32(3.1415925)), float(np.float32(-3.1415925)), ALU.min,
                                      ALU.max))
                own(dve.tensor_scalar(cosx, ang, -1.0, None, ALU.mult))
                own(dve.tensor_tensor(cosx, cosx, ang, ALU.max))
                own(dve.tensor_scalar(cosx, cosx, -1.0, float(np.pi / 2), ALU.mult, ALU.add))
                dve.wait_ge(consts_in, 16)
                for i in range(NT // 2, NT):
                    dve.tensor_tensor_reduce(out=ROWS[:, i, :], in0=X[:, i, :], in1=X[:, i, :], scale=1.0, scalar=0.0,
                                             op0=ALU.mult, op1=ALU.add, accum_out=SS[:, i:i + 1]).then_inc(first_ss, 1)
                dve.wait_ge(first_ss, NT)
                dve.tensor_scalar(SS[:, 0:NT], SS[:, 0:NT], 1.0 / D, EPS, ALU.mult, ALU.add).then_inc(first_ms, 1)

            @block.scalar
            def _(act):
                act.wait_ge(setup, 12)
                act.activation(ROPE[:, 0, :], A[:, 3, :], ACT.Sin)
                act.activation(ROPE[:, 1, :], A[:, 1, :], ACT.Sin)
                act.wait_ge(consts_in, 16)
                for i in range(NT // 2):
                    act.activation(ROWS[:, i, :], X[:, i, :], ACT.Square, accum_out=SS[:, i:i + 1]).then_inc(first_ss, 1)

        with nc.Fori(0, DEPTH) as l:
            with nc.Block() as block:
                @block.sync
                def _(sp):
                    fill = 4 * P
                    zeros = GROW[:].unsqueeze(1).broadcast_to([P, 4, D])
                    zero_rows = [xs_d[n:min(n + fill, XS_ROWS), :] for n in range(0, XS_ROWS, fill)]
                    zero_rows += [ys_d[n:min(n + fill, XS_ROWS), :] for n in range(0, XS_ROWS, fill)]

                    for c in range(RAW_SLOTS, MIX_CHUNKS):
                        sp.wait_ge(lo_done, 2 * (c - RAW_SLOTS) + 2)
                        sp.dma_start(RAW[:, c % RAW_SLOTS, :],
                                     mix_d[bass.ds(l * MIX_CHUNKS + c, 1), :, :].rearrange("c p n -> (c p) n")) \
                          .then_inc(raw_in[c % RAW_SLOTS], 16)
                        if zero_rows:
                            with sp.If(l < 1):
                                for rows in (zero_rows.pop() if zero_rows else None for _ in range(3)):
                                    if rows is not None:
                                        n = rows.shape[0] // P
                                        sp.dma_start(rows.rearrange("(n p) d -> p n d", p=P), zeros[:, 0:n, :]) \
                                          .then_inc(zeroed, 16)
                                        zero_count.append(1)
                    assert not zero_rows
                    sp.wait_ge(zeroed, 16 * len(zero_count))
                    sp.dma_start(GROW[:], gffn_d[bass.ds(l, 1), :].rearrange("l n -> (l n)").partition_broadcast(P)) \
                      .then_inc(grow_in, 16)

                    def load(w, n, e, odd, j):
                        sp.dma_start(slot_of(odd, j),
                                     w[bass.ds(e, 1), :, n * CHUNK:(n + 1) * CHUNK].rearrange("e p n -> (e p) n")) \
                          .then_inc(slot_in(odd, j), 16)

                    def tile(i, odd, experts, behind_scatter=False):
                        t = 2 * i + odd
                        for j in range(OWN_CHUNKS):
                            sp.wait_ge(lo_done, t * OWN_UNITS + (MIX_UNITS - 2 * OWN_UNITS + 2 * j + 2))
                            if behind_scatter and j == 0:
                                sp.wait_ge(scatter_in, l * (2 * NT * 16) + 2 * NT * 16)
                            load(experts[j // 2][0], j % 2, experts[j // 2][1], odd, j)

                    for j in range(OWN_CHUNKS):
                        sp.wait_ge(lo_done, 2 * (MIX_CHUNKS + j - RAW_SLOTS) + 2)
                        load((wg_v, wu_v, wg_v)[j // 2], j % 2, l * NE + j // 4, 0, j)

                    def load_1(j):
                        load((wu_v, wd_v, wg_v)[j // 2], j % 2, l * NE + (1, 0, 2)[j // 2], 1, j)

                    sp.wait_ge(av_done, H_SOFT)
                    load_1(0)
                    load_1(1)
                    sp.wait_ge(logits_t, 1)
                    for j in range(2, OWN_CHUNKS):
                        load_1(j)

                    def own_experts(i, odd):
                        e = l * NE + 2 * i + odd
                        return ((wu_v, e), (wd_v, e - 1), (wg_v, e + 1))

                    tile(1, 0, own_experts(1, 0), behind_scatter=True)
                    tile(1, 1, own_experts(1, 1))
                    with sp.Fori(2, NE // 2 - 1) as i:
                        for odd in range(2):
                            tile(i, odd, own_experts(i, odd))
                    tile(NE // 2 - 1, 0, own_experts(NE // 2 - 1, 0))
                    e = l * NE + NE - 1
                    tile(NE // 2 - 1, 1, ((wu_v, e), (wd_v, e - 1), (wd_v, e)))
                    n_more = sp.value_load(TILE_TAB[0:1, MORE:MORE + 1], min_val=0, max_val=MORE)
                    with sp.If(n_more > 0):
                        def expert_of(n):
                            return l * NE + sp.value_load(TILE_TAB[0:1, bass.ds(n, 1)] if not isinstance(n, int) else
                                                          TILE_TAB[0:1, n:n + 1], min_val=0, max_val=NE - 1)

                        def more_experts(i, odd):
                            n = 2 * i + (odd - NE)
                            return ((wu_v, expert_of(n)), (wd_v, expert_of(n - 1)), (wg_v, expert_of(n + 1)))

                        tile(NE // 2, 0, ((wg_v, expert_of(0)), (wu_v, expert_of(0)), (wg_v, expert_of(1))))
                        tile(NE // 2, 1, more_experts(NE // 2, 1))
                        with sp.Fori(NE // 2 + 1, TILES // 2 - 1) as i:
                            for odd in range(2):
                                tile(i, odd, more_experts(i, odd))
                        tile(TILES // 2 - 1, 0, more_experts(TILES // 2 - 1, 0))
                        e = expert_of(MORE - 1)
                        tile(TILES // 2 - 1, 1, ((wu_v, e), (wd_v, expert_of(MORE - 2)), (wd_v, e)))
                        sp.wait_ge(lo_done, MIX_UNITS + TILES * OWN_UNITS)
                    sp.wait_ge(lo_done, MIX_UNITS + NE * OWN_UNITS)
                    with sp.If(l < DEPTH - 1):
                        load_layer(sp, nc.s_assert_within(
                            l + 1, 1, DEPTH - 1, skip_runtime_bounds_check_because="the If admits no other layer"),
                            gathered=l * 32 + 32)

                @block.gpsimd
                def _(pool):
                    def root(means, count, col, cols, done):
                        pool.wait_ge(means, count)
                        pool.tensor_tensor(SS[:, col:col + cols], SS[:, col:col + cols], MINUS_HALF[:, 0:cols],
                                           ALU.pow).then_inc(done, 1)

                    def mask(x, done):
                        for n in range(1, NT + 1):
                            ins = pool.affine_select(out=x[:, AT[n]:AT[n] + P], in_=x[:, AT[n]:AT[n] + P],
                                                     compare_op=ALU.is_gt, fill=0.0, base=0, pattern=[[1, P]],
                                                     channel_multiplier=-1)
                        ins.then_inc(done, 1)

                    for g in range(H_SOFT + 1):
                        if 0 < g <= H_SB:
                            pool.wait_ge(sb_w, g)
                            mask(HEAD_B[:, (g - 1) % 2, :], sb_wm)
                        if g < H_SB:
                            pool.wait_ge(sb_sum, g + 1)
                            mask(HEAD_A[:, g % 2, :], sb_masked)
                        if g == 0:
                            root(head_ms, 1, NT * H_SOFT, NT * H_GMLP, head_rstd)
                        else:
                            root(head_ms, g + 1, NT * (g - 1), NT, head_rstd)
                    root(ffn_ms, 1, 0, NT, ffn_rstd)
                    pool.wait_ge(rows_done, NT)
                    pool.wait_ge(zeroed, 16 * len(zero_count))
                    pool.wait_ge(slots, 1)
                    for s in range(2):
                        for i in range(NT):
                            pool.indirect_dma_start(
                                out=xs_d, out_offset=bass.IndirectOffsetOnAxis(SLOT[:, s, i:i + 1], 0),
                                in_=ROWS[:, i, :], in_offset=None).then_inc(scatter_in, 16)
                    for odd in range(2):
                        pool.wait_ge(y_stored[odd], 32 * (NE // 2 + 1))
                    pool.wait_ge(table, 1)
                    n_more = pool.value_load(TILE_TAB[0:1, MORE:MORE + 1], min_val=0, max_val=MORE)
                    with pool.If(n_more > 0):
                        for odd in range(2):
                            pool.wait_ge(y_stored[odd], 32 * (TILES // 2 + 1))
                    for i in range(NT):
                        for s in range(2):
                            pool.indirect_dma_start(
                                out=GATHER[2 * i + s], out_offset=None, in_=ys_d,
                                in_offset=bass.IndirectOffsetOnAxis(SLOT[:, s, i:i + 1], 0)).then_inc(gather_in[i], 16)
                    root(x_ms, 1, 0, NT, x_rstd)

                @block.scalar
                def _(act):
                    own = Own(act, act_own)

                    def copy(out, in_, **kw):
                        return act.activation(out, in_, ACT.Copy, **kw)

                    def split_hi(u):
                        c = u // 2
                        if c < RAW_SLOTS:
                            act.wait_ge(pre_in[c], l * 16 + 16)
                        else:
                            act.wait_ge(raw_in[c % RAW_SLOTS], 16 * (c // RAW_SLOTS))
                        if u >= W_SLOTS:
                            act.wait_ge(mm_done, u - W_SLOTS + 1)
                        copy(W_HI[:, u % W_SLOTS, :], RAW[:, c % RAW_SLOTS, UNIT * (u % 2):UNIT * (u % 2 + 1)]) \
                            .then_inc(hi_done, 1)

                    def roots(cols):
                        act.wait_ge(v_ms, 1)
                        act.activation(ROOT[:, 0, 0:cols], SS[:, 0:cols], ACT.Sqrt).then_inc(root_done, 1)

                    def transposed_hi(n, k, bank, gains):
                        act.wait_ge(tr_done, n + 1)
                        copy(HT_HI[:, k, :], PS[:, bank, :], scale=LP[:, gains + k:gains + k + 1]).then_inc(ht_hi, 1)

                    act.preload_act_table_set(exp_tables)
                    act.wait_ge(lay_in, l * 32 + 32)
                    for k in range(KD):
                        if k % 2 == 0:
                            split_hi(k // 2)
                        transposed_hi(k, k, 4 + k % 4, L_GMIX)
                    u = 0
                    for g, (col, width, chunks) in enumerate(TM_GROUPS):
                        for _ in range(2 * chunks):
                            split_hi(u + W_SLOTS)
                            u += 1
                        b = 4 * (g % 2)
                        act.wait_ge(mm_done, u)
                        copy(TM[:, :, col:col + width], PS[:, b:b + NT, 0:width]).then_inc(tm_out, 1)
                        if g == 0:
                            act.wait_ge(tm_out, 1)
                            act.activation(TM[:, :, 768:1280], TM[:, :, 768:1280], ACT.Gelu_apprx_tanh) \
                                .then_inc(gelu_done, 1)
                            roots(NT * H_GMLP)
                            act.preload_act_table_set(exp_tables)

                    def projected(pair, q):
                        u = QK_UNIT + 2 * pair + q
                        act.wait_ge(mm_done, u + 1)
                        if pair == 1:
                            act.wait_ge(spatial_out, H_GMLP)
                            copy(QK_OF[1][:, q, :], PS[:, q, :]).then_inc(qk_out, 1)
                        else:
                            if pair > 2:
                                act.wait_ge(qk_ready, 2 * (pair - 3) + q + 1)
                            copy(QK_RAW[:, q, :], PS[:, 0, :]).then_inc(qk_out, 1)
                        split_hi(u + W_SLOTS)

                    def prepare(g):
                        z, b = SET_BANKS[g % 2], HEAD_B[:, g % 2, :]
                        if g < H_SB:
                            act.wait_ge(scores_done, g + 1)
                            act.activation(b, z, ACT.Abs, scale=SCALE).then_inc(sb_abs, 1)
                            act.wait_ge(sb_abs, g + 1)
                            own(act.activation(b, b, ACT.Exp, scale=-1.0))
                            act.activation(b, b, ACT.Ln, bias=1.0).then_inc(sb_ln, 1)
                        elif g < H_SOFT:
                            for n, i in enumerate((3, 1, 0, 2)):
                                act.wait_ge(mo_max, 3 * (g - H_SB) + min(n + 1, 3))
                                tile = slice(AT[i + 1], AT[i + 1] + P * (i + 1))
                                ins = act.activation(HEAD_A[:, g % 2, tile], z[:, tile], ACT.Exp,
                                                     bias=NMAX[:, 2 + g % 2, i:i + 1], scale=SCALE,
                                                     accum_out=RSUM[:, 2 + g % 2, i:i + 1])
                            ins.then_inc(mo_p, 1)

                    act.wait_ge(mm_done, QK_UNIT + 2)
                    copy(QK_OF[0][:], PS[:, 4:6, :]).then_inc(qk_out, 1)
                    for u in range(2):
                        split_hi(QK_UNIT + W_SLOTS + u)
                    act.wait_ge(gv_ready, 1)
                    prepare(0)
                    projected(1, 0)
                    projected(1, 1)
                    for g in range(H_SOFT):
                        if g < H_SB:
                            act.wait_ge(sb_r, g + 1)
                            act.activation(HEAD_B[:, g % 2, :], SET_BANKS[g % 2], ACT.Exp, scale=SCALE) \
                               .then_inc(sb_w, 1)
                        for n in out_blocks(g):
                            transposed_hi(KD + n, OUT_ORDER[n], 0, L_GHEAD)
                        prepare(g + 1)
                        if g // 2 + 2 < QK_CHUNKS:
                            projected(g // 2 + 2, g % 2)
                    for u in range(MIX_UNITS - W_SLOTS, MIX_UNITS):
                        if u == MIX_UNITS - W_SLOTS + 2:
                            transposed_hi(2 * KD - 1, OUT_ORDER[KD - 1], 0, L_GHEAD)
                        split_hi(u)
                    for half in range(2):
                        for i in range(NT):
                            act.wait_ge(x_added, 1 if half == 0 else 2 + i)
                            act.activation(ROWS[:, i, 512 * half:512 * (half + 1)], X[:, i, 512 * half:512 * (half + 1)],
                                           ACT.Square, accum_out=SS[:, NT * (half + 1) + i:NT * (half + 1) + i + 1]) \
                               .then_inc(ffn_ss, 1)
                    copy(WR_HI[:], LP[:, L_WR:L_COLS].rearrange("p (k n) -> p k n", n=NR)).then_inc(wr_hi, 1)

                    def split_own(i, odd, u):
                        act.wait_ge(slot_in(odd, u // 2), 16 * slot_count(i, odd, u // 2))
                        act.wait_ge(mm_done, (2 * i + odd) * OWN_UNITS + (MIX_UNITS + u - W_SLOTS + 1))
                        copy(W_HI[:, (MIX_UNITS + u) % W_SLOTS, :], raw_of(odd, u)).then_inc(hi_done, 1)

                    for k in range(KD):
                        transposed_hi(2 * KD + k, k, 4 + k % 4, L_GFFN)
                    act.wait_ge(logits_t, 1)
                    copy(LOGITS_T, PS[0:NR, 0, :]).then_inc(logits_sb, 1)
                    act.wait_ge(gexp_in, 1)
                    act.activation(A[:, 0, 0:NT * NG], A[:, 0, 0:NT * NG], ACT.Exp).then_inc(gexp, 1)
                    act.wait_ge(gexp_in, 2)
                    act.activation(GATE[:, 1, :], GATE[:, 1, :], ACT.Exp).then_inc(gexp, 1)

                    for odd in range(2):
                        act.sem_inc(y_stored[odd], 32)

                    def rows_hi(t):
                        act.wait_ge(xs_t, t + 1)
                        copy(two(XT_HI), XT_PS).then_inc(xt_hi, 1)

                    def second_half(t, further, move, done):
                        if further:
                            move()
                            return
                        at = FULL_TAB[0:1, t:t + 1] if isinstance(t, int) else FULL_TAB[0:1, bass.ds(t, 1)]
                        full = act.value_load(at, min_val=0, max_val=1)
                        with act.If(full > 0):
                            move()
                        with act.If(full < 1):
                            act.sem_inc(done, 16)

                    def load_rows(t, odd, further=False):
                        act.dma_start(XS[odd][0:HALF], xs_d[bass.ds(t * ROWS_T, HALF), :]).then_inc(xs_in[odd], 16)

                        def second():
                            act.dma_start(XS[odd][HALF:ROWS_T], xs_d[bass.ds(t * ROWS_T + HALF, HALF), :]) \
                               .then_inc(xs_in[odd], 16)

                        second_half(t, further, second, xs_in[odd])

                    def silu(t):
                        act.wait_ge(mm_done, t * OWN_UNITS + MIX_UNITS)
                        act.activation(SIL, PS[0:ROWS_T, 0, :], ACT.Silu).then_inc(sil_done, 1)

                    def store(i, odd, down, further=False):
                        t = 2 * i + odd
                        act.wait_ge(mm_done, down)
                        act.wait_ge(y_stored[odd], 32 * (i + 1))
                        copy(YB[odd], PS[0:ROWS_T, 2:4, :].rearrange("p a n -> p (a n)")).then_inc(y_copied, 1)
                        act.wait_ge(y_copied, t + 1)
                        act.dma_start(ys_d[bass.ds(t * ROWS_T, HALF), :], YB[odd][0:HALF]).then_inc(y_stored[odd], 16)

                        def second():
                            act.dma_start(ys_d[bass.ds(t * ROWS_T + HALF, HALF), :], YB[odd][HALF:ROWS_T]) \
                               .then_inc(y_stored[odd], 16)

                        second_half(t, further, second, y_stored[odd])

                    def act_hi(t):
                        act.wait_ge(at_t, t + 1)
                        copy(AT_HI, AT_PS).then_inc(at_hi, 1)

                    def tile(i, odd, more, further=False):
                        t = 2 * i + odd
                        silu(t)
                        for u in range(4, 8):
                            split_own(i, odd, u)
                        rows_hi(t + 1)
                        if more:
                            load_rows(t + 3, 1 - odd, further)
                        for u in range(8, 12):
                            split_own(i, odd, u)
                        store(i - 1 + odd, 1 - odd, t * OWN_UNITS + (MIX_UNITS + 8), further)
                        act_hi(t)
                        if more:
                            for u in range(4):
                                split_own(i + odd, 1 - odd, u)

                    def first_tile(i):
                        t, odd = 2 * i, 0
                        if t == 0:
                            rows_hi(t)
                        else:
                            for u in range(4):
                                split_own(i, odd, u)
                        load_rows(t + 2, 0, t > 0)
                        for u in range(4, 8):
                            split_own(i, odd, u)
                        act.wait_ge(mm_done, t * OWN_UNITS + MIX_UNITS + 4)
                        act.activation(SIL, PS[0:ROWS_T, 0, :], ACT.Silu).then_inc(sil_done, 1)
                        act.wait_ge(mm_done, t * OWN_UNITS + MIX_UNITS + 8)
                        rows_hi(t + 1)
                        load_rows(t + 3, 1, t > 0)
                        for u in range(8, 12):
                            split_own(i, odd, u)
                        act_hi(t)
                        for u in range(4):
                            split_own(i + odd, 1 - odd, u)

                    act.preload_act_table(ACT.Silu)
                    for u in range(4):
                        split_own(0, 0, u)
                    act.wait_ge(table, 1)
                    act.wait_ge(scatter_in, l * (2 * NT * 16) + 2 * NT * 16)
                    load_rows(0, 0)
                    load_rows(1, 1)
                    first_tile(0)
                    tile(0, 1, True)
                    with act.Fori(1, NE // 2 - 1) as i:
                        for odd in range(2):
                            tile(i, odd, True)
                    tile(NE // 2 - 1, 0, True)
                    tile(NE // 2 - 1, 1, False)
                    store(NE // 2 - 1, 1, MIX_UNITS + NE * OWN_UNITS)
                    act.wait_ge(table, 1)
                    n_more = act.value_load(TILE_TAB[0:1, MORE:MORE + 1], min_val=0, max_val=MORE)
                    with act.If(n_more > 0):
                        first_tile(NE // 2)
                        tile(NE // 2, 1, True, True)
                        with act.Fori(NE // 2 + 1, TILES // 2 - 1) as i:
                            for odd in range(2):
                                tile(i, odd, True, True)
                        tile(TILES // 2 - 1, 0, True, True)
                        tile(TILES // 2 - 1, 1, False, True)
                        store(TILES // 2 - 1, 1, MIX_UNITS + TILES * OWN_UNITS, True)
                        act.wait_ge(xs_in[1], 32 * (TILES // 2 + 1))
                    act.wait_ge(xs_in[1], 32 * (NE // 2 + 1))
                    for i in range(NT):
                        act.wait_ge(x_new, i + 1)
                        act.activation(ROWS[:, i, :], X[:, i, :], ACT.Square, accum_out=SS[:, i:i + 1]).then_inc(x_ss, 1)

                @block.vector
                def _(dve):
                    own = Own(dve, dve_own)
                    tt, ts, stt = dve.tensor_tensor, dve.tensor_scalar, dve.scalar_tensor_tensor

                    def split_lo(u):
                        dve.wait_ge(hi_done, u + 1)
                        tt(W_LO[:, u % W_SLOTS, :], RAW[:, u // 2 % RAW_SLOTS, UNIT * (u % 2):UNIT * (u % 2 + 1)],
                           W_HI[:, u % W_SLOTS, :].bitcast(F32), ALU.subtract).then_inc(lo_done, 1)

                    def mean(first_col, cols, count, done):
                        x = SS[:, first_col:first_col + cols]
                        ts(x, x, 1.0 / count, EPS, ALU.mult, ALU.add).then_inc(done, 1)

                    def inverse_root(cols):
                        x, y, z = SS[:, 0:cols], ROOT[:, 1, 0:cols], ROOT[:, 0, 0:cols]
                        dve.wait_ge(root_done, 1)
                        own(dve.reciprocal(y, z))
                        own(tt(z, y, y, ALU.mult))
                        own(tt(z, z, x, ALU.mult))
                        own(ts(z, z, -0.5, 1.5, ALU.mult, ALU.add))
                        own(tt(x, y, z, ALU.mult))

                    def diagonals():
                        for i in range(NT):
                            ts(DIAG[:, i, :], IDENT, SS[:, i:i + 1], None, ALU.mult).then_inc(diag_done, 1)

                    def transposed_lo(n, k, bank, gains):
                        dve.wait_ge(ht_hi, n + 1)
                        stt(HT_LO[:, k, :], PS[:, bank, :], LP[:, gains + k:gains + k + 1], HT_HI[:, k, :].bitcast(F32),
                            ALU.mult, ALU.subtract).then_inc(ht_lo, 1)

                    def heads_of(x):
                        return x.rearrange("p i (g d) -> p i g d", d=HD)

                    diagonals()
                    for k in range(KD):
                        if k % 2 == 0:
                            split_lo(k // 2)
                        transposed_lo(k, k, 4 + k % 4, L_GMIX)
                    for u in range(4, 8):
                        split_lo(u)
                    dve.wait_ge(gelu_done, 1)
                    V = heads_of(TM[:, :, 1024:1280])
                    sq = B[:, :, 0:256]
                    own(tt(sq, TM[:, :, 1024:1280], TM[:, :, 1024:1280], ALU.mult))
                    own(dve.tensor_reduce(SS[:, 0:NT * H_GMLP].rearrange("p (i g) -> p i g", i=NT), heads_of(sq), AX.X,
                                          ALU.add))
                    mean(0, NT * H_GMLP, HD, v_ms)
                    inverse_root(NT * H_GMLP)
                    own(tt(V, V, SS[:, 0:NT * H_GMLP].rearrange("p (i g) -> p i g", i=NT).unsqueeze(3)
                           .broadcast_to([P, NT, H_GMLP, HD]), ALU.mult))
                    own(tt(TM[:, :, 1024:1280], TM[:, :, 1024:1280], GV[:].unsqueeze(1).broadcast_to([P, NT, 256]),
                           ALU.mult))
                    WS = LP[:, L_WS:L_WR].rearrange("p (g t) -> p g t", g=H_GMLP)
                    tt(WS, WS, C[:, C_LOW:C_LOW + P].unsqueeze(1).broadcast_to([P, H_GMLP, P]), ALU.mult) \
                        .then_inc(gv_ready, 1)
                    for u in range(8, QK_UNIT + W_SLOTS):
                        split_lo(u)
                    for g in range(H_GMLP):
                        dve.wait_ge(spatial_done, g + 1)
                        stt(ROWS[:, :, HD * (12 + g):HD * (13 + g)],
                            PS[:, 6 + g % 2, 0:NT * HD].rearrange("p (i d) -> p i d", d=HD),
                            LP[:, L_BS + g:L_BS + g + 1], TM[:, :, 768 + HD * g:768 + HD * (g + 1)], ALU.add,
                            ALU.mult).then_inc(spatial_out, 1)
                    for u in range(QK_UNIT + W_SLOTS, QK_UNIT + W_SLOTS + 2):
                        split_lo(u)

                    def rotate(pair, q):
                        x, y = QK_RAW[:, q, :], QK_OF[pair % 2][:, q, :]
                        dve.wait_ge(rot_done, 2 * (pair - 2) + q + 1)
                        own(tt(x, x, ROPE[:, 0, :], ALU.mult))
                        tt(y, PS[:, 0, :], ROPE[:, 1, :], ALU.mult).then_inc(rot_read, 1)
                        dve.wait_ge(rot_read, 2 * (pair - 2) + q + 1)
                        tt(y, y, x, ALU.add).then_inc(qk_ready, 1)

                    def prepare(g):
                        z, a, b = SET_BANKS[g % 2], HEAD_A[:, g % 2, :], HEAD_B[:, g % 2, :]
                        if g == H_SOFT:
                            return
                        if g < H_SB:
                            dve.wait_ge(sb_abs, g + 1)
                            own(ts(a, z, SCALE, 0.0, ALU.mult, ALU.max))
                            dve.wait_ge(sb_ln, g + 1)
                            tt(a, a, b, ALU.add).then_inc(sb_sum, 1)
                        else:
                            h = g - H_SB
                            low, scaled = NMAX[:, g % 2, :], NMAX[:, 2 + g % 2, :]

                            def row_max(i):
                                dve.tensor_reduce(low[:, i:i + 1], z[:, AT[i + 1]:AT[i + 1] + P * (i + 1)], AX.X, ALU.max,
                                                  negate=True).then_inc(mo_low, 1)

                            def scale(tiles, count):
                                dve.wait_ge(mo_low, NT * h + count)
                                ts(scaled[:, tiles], low[:, tiles], SCALE, None, ALU.mult).then_inc(mo_max, 1)

                            dve.wait_ge(scores_done, g + 1)
                            row_max(3)
                            row_max(1)
                            scale(slice(3, 4), 1)
                            row_max(0)
                            row_max(2)
                            scale(slice(1, 2), 2)
                            scale(slice(0, 3, 2), 4)

                    def square_sums(y, heads, scratch, col):
                        sq = scratch[:, 0:NT * heads * HD].rearrange("p (i n) -> p i n", i=NT)
                        own(tt(sq, y, y, ALU.mult))
                        own(dve.tensor_reduce(SS[:, col:col + NT * heads].rearrange("p (g i) -> p i g", i=NT),
                                              heads_of(sq), AX.X, ALU.add))
                        mean(col, NT * heads, HD, head_ms)

                    def norm_heads(count, first_head, heads):
                        dve.wait_ge(head_rstd, count)
                        y = heads_of(ROWS[:, :, HD * first_head:HD * (first_head + heads)])
                        r = SS[:, NT * first_head:NT * (first_head + heads)].rearrange("p (g i) -> p i g", i=NT)
                        tt(y, y, r.unsqueeze(3).broadcast_to([P, NT, heads, HD]), ALU.mult).then_inc(head_normed, 1)

                    prepare(0)
                    dve.wait_ge(spatial_out, H_GMLP)
                    square_sums(ROWS[:, :, HD * H_SOFT:D], H_GMLP, HEAD_A[:, 1, :], NT * H_SOFT)
                    for u in range(2):
                        split_lo(QK_UNIT + W_SLOTS + 2 + u)
                    for g in range(H_SOFT):
                        if g >= 1 and (g - 1) // 2 + 2 < QK_CHUNKS:
                            rotate((g - 1) // 2 + 2, (g - 1) % 2)
                        if g >= H_SB:
                            dve.wait_ge(mo_t, g - H_SB + 1)
                            dve.tensor_copy(HEAD_B[:, g % 2, :], SET_BANKS[g % 2]).then_inc(mo_pt, 1)
                        blocks = out_blocks(g)
                        for n in blocks[:1]:
                            transposed_lo(KD + n, OUT_ORDER[n], 0, L_GHEAD)
                        prepare(g + 1)
                        for n in blocks[1:]:
                            transposed_lo(KD + n, OUT_ORDER[n], 0, L_GHEAD)
                        if g // 2 + 2 < QK_CHUNKS:
                            split_lo(QK_UNIT + 4 + g + W_SLOTS)
                        if g == 1:
                            norm_heads(1, H_SOFT, H_GMLP)
                        if g:
                            norm_heads(g + 1, g - 1, 1)
                        heads_out = ROWS[:, :, HD * g:HD * (g + 1)]
                        if g >= H_SB:
                            own(dve.reciprocal(RSUM[:, g % 2, :], RSUM[:, 2 + g % 2, :]))
                        dve.wait_ge(av_done, g + 1)
                        if g < H_SB:
                            dve.tensor_copy(heads_out, VALUES_OUT[g % 2]).then_inc(head_out, 1)
                        else:
                            tt(heads_out, VALUES_OUT[g % 2], RSUM[:, g % 2, :].unsqueeze(2).broadcast_to([P, NT, HD]),
                               ALU.mult).then_inc(head_out, 1)
                        dve.wait_ge(head_out, g + 1)
                        square_sums(heads_out, 1, HEAD_A[:, g % 2, :], NT * g)
                    norm_heads(H_SOFT + 1, H_SOFT - 1, 1)
                    for u in range(MIX_UNITS - W_SLOTS, MIX_UNITS):
                        if u == MIX_UNITS - W_SLOTS + 2:
                            transposed_lo(2 * KD - 1, OUT_ORDER[KD - 1], 0, L_GHEAD)
                        split_lo(u)
                    dve.wait_ge(mm_done, OUT_UNIT + 4)
                    xq = X[:, :, 0:512]
                    tt(xq, xq, PS[:, 4:4 + NT, :], ALU.add).then_inc(x_added, 1)
                    dve.wait_ge(mm_done, OUT_UNIT + 8)
                    for i in range(NT):
                        xq = X[:, i, 512:D]
                        tt(xq, xq, PS[:, i, :], ALU.add).then_inc(x_added, 1)
                    dve.wait_ge(ffn_ss, 2 * NT)
                    own(tt(SS[:, 0:NT], SS[:, NT:2 * NT], SS[:, 2 * NT:3 * NT], ALU.add))
                    mean(0, NT, D, ffn_ms)
                    dve.wait_ge(wr_hi, 1)
                    tt(WR_LO[:], LP[:, L_WR:L_COLS].rearrange("p (k n) -> p k n", n=NR), WR_HI[:].bitcast(F32),
                       ALU.subtract).then_inc(wr_lo, 1)
                    dve.wait_ge(ffn_rstd, 1)
                    diagonals()
                    dve.wait_ge(grow_in, 16)
                    for k in range(KD):
                        transposed_lo(2 * KD + k, k, 4 + k % 4, L_GFFN)
                        if k % 2 == 0:
                            i = k // 2
                            stt(ROWS[:, i, :], X[:, i, :], SS[:, i:i + 1], GROW[:], ALU.mult, ALU.mult) \
                                .then_inc(rows_done, 1)
                    def bc(x, n):
                        return x.unsqueeze(2).broadcast_to([P, NT, n])

                    def area(a, b, cols):
                        return B[:, a, b * 128:b * 128 + NT * cols].rearrange("p (i n) -> p i n", n=cols)

                    def over(col, n):
                        return C[:, col:col + n].unsqueeze(1).broadcast_to([P, NT, n])

                    GE = A[:, 0, 0:NT * NG].rearrange("p (i n) -> p i n", n=NG)
                    G4, L, M1, M2 = area(0, 0, NG), area(0, 1, NE), area(0, 2, NE), area(0, 3, NE)
                    T1, T2, MB, POS = area(1, 0, NE), area(1, 1, NE), area(1, 2, NE), area(1, 3, NE)
                    SM = A[:, 1, 0:64].rearrange("p (a i) -> p a i", i=NT)
                    MAXG, SUMG, GSEL, TOP1, IDX1, TOP2, IDX2 = (SM[:, a, :] for a in range(7))
                    dve.wait_ge(logits, 1)
                    LG = PS[:, 1, 0:NT * 64].rearrange("p (i n) -> p i n", n=64)
                    own(dve.tensor_copy(G4, LG[:, :, 0:NG]))
                    own(dve.tensor_reduce(MAXG, G4, AX.X, ALU.max))
                    tt(GE, G4, bc(MAXG, NG), ALU.subtract).then_inc(gexp_in, 1)

                    def argmax(x, top, idx, n, tmp):
                        own(tt(tmp, x, bc(top, n), ALU.is_lt))
                        own(stt(tmp, tmp, 64.0, over(C_IOTA, n), ALU.mult, ALU.add))
                        own(dve.tensor_reduce(idx, tmp, AX.X, ALU.min))

                    argmax(G4, MAXG, GSEL, NG, area(2, 0, NG))
                    own(tt(T1, over(C_GROUP, NE), bc(GSEL, NE), ALU.is_equal))
                    own(ts(T1, T1, -1.0, -NEG, ALU.add, ALU.mult))
                    own(tt(L, LG[:, :, NG:NR], T1, ALU.add))
                    own(dve.tensor_reduce(TOP1, L, AX.X, ALU.max))
                    argmax(L, TOP1, IDX1, NE, T2)
                    own(tt(M1, over(C_IOTA, NE), bc(IDX1, NE), ALU.is_equal))
                    own(stt(L, M1, 2 * NEG, L, ALU.mult, ALU.add))
                    own(dve.tensor_reduce(TOP2, L, AX.X, ALU.max))
                    argmax(L, TOP2, IDX2, NE, T2)
                    own(tt(M2, over(C_IOTA, NE), bc(IDX2, NE), ALU.is_equal))
                    tt(MB, M1, M2, ALU.add).then_inc(ranks_in, 1)
                    tt(GATE[:, 1, :], TOP2, TOP1, ALU.subtract).then_inc(gexp_in, 1)
                    dve.wait_ge(ranks, 1)
                    RANK = PS[:, 3, 0:NT * NE].rearrange("p (i n) -> p i n", n=NE)
                    CNT = area(3, 0, NE)[:, 0, :]
                    NV, INC, DIF, ONES = (area(3, 0, NE)[:, 1, :], area(3, 0, NE)[:, 2, :], area(3, 0, NE)[:, 3, :],
                                          C[:, C_ONES:C_ONES + NE])
                    own(dve.tensor_copy(CNT, PS[:, 3, NT * NE:NT * NE + NE]))
                    TH = A[:, 2, 0:NE * (MAX_R - 1)].rearrange("p (n r) -> p n r", r=MAX_R - 1)
                    own(tt(TH, CNT.unsqueeze(2).broadcast_to([P, NE, MAX_R - 1]),
                           C[:, C_LIMIT:C_LIMIT + MAX_R - 1].unsqueeze(1).broadcast_to([P, NE, MAX_R - 1]), ALU.is_gt))
                    own(dve.tensor_reduce(NV, TH, AX.X, ALU.add))
                    own(dve.tensor_tensor_scan(INC, ONES, NV, 0.0, ALU.mult, ALU.add))
                    own(tt(DIF, INC, NV, ALU.subtract))
                    own(ts(DIF, DIF, float(NE - 1), None, ALU.add))
                    own(tt(DIF, DIF, C[:, C_IOTA:C_IOTA + NE], ALU.subtract))
                    own(ts(T2, RANK, float(ROWS_T), None, ALU.is_ge))
                    own(tt(T2, T2, DIF.unsqueeze(1).broadcast_to([P, NT, NE]), ALU.mult))
                    own(tt(T2, T2, over(C_IOTA, NE), ALU.add))
                    own(stt(POS, T2, float(ROWS_T), RANK, ALU.mult, ALU.add))
                    own(tt(T2, POS, M1, ALU.mult))
                    own(dve.tensor_reduce(IDX1, T2, AX.X, ALU.add))
                    own(tt(T2, POS, M2, ALU.mult))
                    own(dve.tensor_reduce(IDX2, T2, AX.X, ALU.add))
                    own(dve.tensor_copy(SLOT[:, 0, :], IDX1))
                    dve.tensor_copy(SLOT[:, 1, :], IDX2).then_inc(slots, 1)
                    dve.wait_ge(gexp, 2)
                    own(dve.tensor_reduce(SUMG, GE, AX.X, ALU.add))
                    own(ts(T1[:, 0:1, 0:NT].rearrange("p a i -> p (a i)"), GATE[:, 1, :], 1.0, None, ALU.add))
                    own(tt(SUMG, SUMG, T1[:, 0:1, 0:NT].rearrange("p a i -> p (a i)"), ALU.mult))
                    own(dve.reciprocal(GATE[:, 0, :], SUMG))
                    own(tt(GATE[:, 1, :], GATE[:, 1, :], GATE[:, 0, :], ALU.mult))
                    TJ = A[0:1, 3, 0:MORE * NE].rearrange("p (j n) -> p j n", n=NE)
                    EJ = A[0:1, 1, 64:64 + MORE + 1]
                    own(tt(TJ, INC[0:1, :].unsqueeze(1).broadcast_to([1, MORE, NE]),
                           C[0:1, C_IOTA:C_IOTA + MORE].unsqueeze(2).broadcast_to([1, MORE, NE]), ALU.is_le))
                    own(dve.tensor_reduce(EJ[:, 0:MORE], TJ, AX.X, ALU.add))
                    own(ts(EJ[:, 0:MORE], EJ[:, 0:MORE], float(NE - 1), None, ALU.min))
                    own(dve.tensor_copy(EJ[:, MORE:MORE + 1], INC[0:1, NE - 1:NE]))
                    FULL = A[0:1, 1, 128:128 + NE + 2]
                    own(ts(FULL, C[0:1, C_ONES:C_ONES + NE + 2], 1.0, None, ALU.mult))
                    own(ts(FULL[:, 0:NE], CNT[0:1, :], float(HALF), None, ALU.is_gt))
                    own(dve.tensor_copy(FULL_TAB[:], FULL))
                    dve.tensor_copy(TILE_TAB[:], EJ).then_inc(table, 1)

                    def lo_own(i, odd, u):
                        t = 2 * i + odd
                        slot = (MIX_UNITS + u) % W_SLOTS
                        dve.wait_ge(hi_done, t * OWN_UNITS + (MIX_UNITS + u + 1))
                        tt(W_LO[:, slot, :], raw_of(odd, u), W_HI[:, slot, :].bitcast(F32), ALU.subtract).then_inc(lo_done, 1)

                    def rows_lo(t):
                        dve.wait_ge(xt_hi, t + 1)
                        tt(two(XT_LO), XT_PS, two(XT_HI).bitcast(F32), ALU.subtract) \
                            .then_inc(xt_ready, 1)

                    def acted(t, up):
                        dve.wait_ge(mm_done, up)
                        dve.wait_ge(sil_done, t + 1)
                        tt(ACTED, SIL, PS[0:ROWS_T, 1, :], ALU.mult).then_inc(act_done, 1)

                    def acted_lo(t):
                        dve.wait_ge(at_hi, t + 1)
                        tt(AT_LO, AT_PS, AT_HI.bitcast(F32), ALU.subtract).then_inc(at_lo, 1)

                    def tile(i, odd, more):
                        t = 2 * i + odd
                        for u in range(4, 8):
                            lo_own(i, odd, u)
                        acted(t, t * OWN_UNITS + (MIX_UNITS + 4))
                        rows_lo(t + 1)
                        for u in range(8, 12):
                            lo_own(i, odd, u)
                        acted_lo(t)
                        if more:
                            for u in range(4):
                                lo_own(i + odd, 1 - odd, u)

                    def first_tile(i):
                        t, odd = 2 * i, 0
                        for u in range(4):
                            lo_own(i, odd, u)
                        if t == 0:
                            rows_lo(t)
                        for u in range(4, 8):
                            lo_own(i, odd, u)
                        acted(t, t * OWN_UNITS + (MIX_UNITS + 8))
                        rows_lo(t + 1)
                        for u in range(8, 12):
                            lo_own(i, odd, u)
                        acted_lo(t)
                        for u in range(4):
                            lo_own(i + odd, 1 - odd, u)

                    first_tile(0)
                    tile(0, 1, True)
                    with dve.Fori(1, NE // 2 - 1) as i:
                        for odd in range(2):
                            tile(i, odd, True)
                    tile(NE // 2 - 1, 0, True)
                    tile(NE // 2 - 1, 1, False)
                    n_more = dve.value_load(TILE_TAB[0:1, MORE:MORE + 1], min_val=0, max_val=MORE)
                    with dve.If(n_more > 0):
                        first_tile(NE // 2)
                        tile(NE // 2, 1, True)
                        with dve.Fori(NE // 2 + 1, TILES // 2 - 1) as i:
                            for odd in range(2):
                                tile(i, odd, True)
                        tile(TILES // 2 - 1, 0, True)
                        tile(TILES // 2 - 1, 1, False)
                    for i in range(NT):
                        dve.wait_ge(gather_in[i], l * 32 + 32)
                        for s in range(2):
                            ins = stt(X[:, i, :], GATHER[2 * i + s], GATE[:, s, i:i + 1], X[:, i, :], ALU.mult,
                                      ALU.add)
                            if s == 0:
                                own(ins)
                        ins.then_inc(x_new, 1)
                    dve.wait_ge(x_ss, NT)
                    mean(0, NT, D, x_ms)

                @block.tensor
                def _(pe):
                    def norm_block(n, k):
                        if n % KD >= 4:
                            pe.wait_ge(ht_lo, n - 3)
                        for i in range(NT):
                            if n % KD == 0:
                                pe.wait_ge(diag_done, (1 if n == 0 else 1 + NT) + i)
                            ins = pe.matmul(PS[:, 4 + k % 4, P * i:P * (i + 1)],
                                            X[:, i, :].rearrange("p (m k) -> p m k", k=KD)[:, :, k], DIAG[:, i, :],
                                            start=True, stop=True)
                        ins.then_inc(tr_done, 1)

                    def out_block(n):
                        k = OUT_ORDER[n]
                        if n:
                            pe.wait_ge(ht_lo, KD + n)
                        else:
                            pe.wait_ge(rot_read, 2 * (QK_CHUNKS - 2))
                        pe.wait_ge(head_normed, 1 if k >= H_SOFT // 2 else 2 * k + 3)
                        for i in range(NT):
                            ins = pe.transpose(PS[:, 0, P * i:P * (i + 1)], ROWS[:, i, P * k:P * (k + 1)], IDENT)
                        ins.then_inc(tr_done, 1)

                    def by_tokens(u, width, bank, ks, order, rows_ready):
                        slot = u % W_SLOTS
                        pe.wait_ge(ht_lo, rows_ready)
                        pe.wait_ge(lo_done, u + 1)
                        w_hi = W_HI[:, slot, :].rearrange("p (k n) -> p k n", n=width)
                        w_lo = W_LO[:, slot, :].rearrange("p (k n) -> p k n", n=width)
                        for i in range(NT):
                            tokens = slice(P * i, P * (i + 1))
                            for kk, n in enumerate(ks):
                                k = order[n]
                                ins = product3(pe, PS[:, bank + i, 0:width], HT_HI[:, k, tokens], HT_LO[:, k, tokens],
                                               w_hi[:, kk, :], w_lo[:, kk, :], n == 0, n == KD - 1)
                        ins.then_inc(mm_done, 1)

                    def project(pair, q):
                        u = QK_UNIT + 2 * pair + q
                        if pair == 0:
                            pe.wait_ge(tm_out, 2)
                        elif pair == 1:
                            pe.wait_ge(tm_out, len(TM_GROUPS))
                        elif pair == 2 and q == 0:
                            pe.wait_ge(qk_out, 2)
                        elif pair >= 2:
                            pe.wait_ge(rot_read, 2 * (pair - 2) + q)
                        pe.wait_ge(lo_done, u + 1)
                        w_hi = W_HI[:, u % W_SLOTS, :].rearrange("p (k n) -> p k n", k=KD)
                        w_lo = W_LO[:, u % W_SLOTS, :].rearrange("p (k n) -> p k n", k=KD)
                        for k in range(KD):
                            ins = product3(pe, PS[:, (4 + q, q, 0)[min(pair, 2)], :], w_hi[:, k, :], w_lo[:, k, :],
                                           HT_HI[:, k, :], HT_LO[:, k, :], k == 0, k == KD - 1)
                        ins.then_inc(mm_done, 1)

                    def rotated(pair, q):
                        pe.wait_ge(qk_out, 2 * pair + q)
                        pe.matmul(PS[:, 0, :], C[:, C_ROT:C_ROT + P], QK_RAW[:, q, :], start=True, stop=True) \
                            .then_inc(rot_done, 1)

                    for k in range(4):
                        norm_block(k, k)
                    u = 0
                    for g, (_, width, chunks) in enumerate(TM_GROUPS):
                        if g == 2:
                            pe.wait_ge(tm_out, 1)
                        per_unit = KD // (2 * chunks)
                        for n in range(2 * chunks):
                            by_tokens(u, width, 4 * (g % 2), range(per_unit * n, per_unit * (n + 1)), range(KD),
                                      per_unit * (n + 1) if g == 0 else KD)
                            if g == 0 and n < 2:
                                norm_block(4 + 2 * n, 4 + 2 * n)
                                norm_block(5 + 2 * n, 5 + 2 * n)
                            u += 1
                    project(0, 0)
                    project(0, 1)
                    pe.wait_ge(gv_ready, 1)
                    for g in range(H_GMLP):
                        if g >= 2:
                            pe.wait_ge(spatial_out, g - 1)
                        pe.matmul(PS[:, 6 + g % 2, 0:NT * HD], LP[:, L_WS + P * g:L_WS + P * (g + 1)],
                                  TM[:, :, 1024 + HD * g:1024 + HD * (g + 1)], start=True, stop=True) \
                            .then_inc(spatial_done, 1)
                    def scores(g):
                        pair, z = g // 2, SET_BANKS[g % 2]
                        part = slice(HD * (g % 2), HD * (g % 2 + 1))
                        q_t, k_t = QK_OF[pair % 2][part, 0, :], QK_OF[pair % 2][part, 1, :]
                        if pair < 2:
                            pe.wait_ge(qk_out, (1, 3)[pair])
                        else:
                            pe.wait_ge(qk_ready, 2 * (pair - 1))
                        for n in range(1, NT + 1):
                            if g < H_SB:
                                j = NT - n
                                ins = pe.matmul(z[:, AT[n]:AT[n] + P * n], k_t[:, P * j:P * (j + 1)], q_t[:, P * j:SEQ],
                                                start=(n != 3), stop=True, skip_group_check=(n == 3))
                            else:
                                i = n - 1
                                q, own_keys = q_t[:, P * i:P * (i + 1)], z[:, AT[n] + P * i:AT[n] + P * (i + 1)]
                                if i:
                                    pe.matmul(z[:, AT[n]:AT[n] + P * i], q, k_t[:, 0:P * i], start=True, stop=True)
                                pe.matmul(own_keys, q, k_t[:, P * i:P * (i + 1)], start=True, stop=False)
                                ins = pe.matmul(own_keys, IDENT, C[:, C_NEG:C_NEG + P], start=False, stop=True)
                        ins.then_inc(scores_done, 1)

                    pe.wait_ge(tm_out, len(TM_GROUPS))
                    scores(0)
                    project(1, 0)
                    project(1, 1)
                    for g in range(H_SOFT):
                        z, a, b = SET_BANKS[g % 2], HEAD_A[:, g % 2, :], HEAD_B[:, g % 2, :]
                        if g < H_SB:
                            pe.wait_ge(sb_masked, g + 1)
                            for n in range(1, NT + 1):
                                for m in range(1, n):
                                    pe.matmul(z[:, AT[n] + P * (n - m):AT[n] + P * n], C[:, C_ONE8:C_ONE8 + P],
                                              a[:, AT[m]:AT[m] + P * m], start=False, stop=False, skip_group_check=True)
                                ins = pe.matmul(z[:, AT[n]:AT[n] + P * n], C[:, C_TRI8:C_TRI8 + P],
                                                a[:, AT[n]:AT[n] + P * n], start=False, stop=True, skip_group_check=True)
                            ins.then_inc(sb_r, 1)
                        else:
                            pe.wait_ge(mo_p, g - H_SB + 1)
                            for n in range(1, NT + 1):
                                for c in range(AT[n], AT[n] + P * n, P):
                                    ins = pe.transpose(z[:, c:c + P], a[:, c:c + P], IDENT)
                            ins.then_inc(mo_t, 1)
                        blocks = out_blocks(g)
                        for n in blocks[:1]:
                            out_block(n)
                        if g == 0:
                            pe.wait_ge(spatial_out, H_GMLP)
                        if g + 1 < H_SOFT:
                            scores(g + 1)
                        if g // 2 + 2 < QK_CHUNKS:
                            project(g // 2 + 2, g % 2)
                        for n in blocks[1:]:
                            out_block(n)
                        if g:
                            pe.wait_ge(head_out, g)
                        else:
                            pe.wait_ge(qk_out, 3)
                        pe.wait_ge(*((sb_wm, g + 1) if g < H_SB else (mo_pt, g - H_SB + 1)))
                        for i in range(NT):
                            for j in range(i + 1):
                                c = AT[NT - j] + P * (i - j) if g < H_SB else AT[i + 1] + P * j
                                ins = pe.matmul(VALUES_OUT[g % 2][:, i, :], b[:, c:c + P],
                                                TM[:, j, HD * g:HD * (g + 1)], start=(j == 0), stop=(j == i))
                        ins.then_inc(av_done, 1)
                        if g // 2 + 2 < QK_CHUNKS:
                            rotated(g // 2 + 2, g % 2)
                    for half in range(2):
                        if half:
                            pe.wait_ge(head_out, H_SOFT)
                        for n in range(4):
                            by_tokens(OUT_UNIT + 4 * half + n, 512, 4 - 4 * half, (2 * n, 2 * n + 1), OUT_ORDER,
                                      KD + 2 * n + 2)
                            if half == 0 and n == 1:
                                out_block(KD - 1)
                    def router(k):
                        pe.wait_ge(ht_lo, 2 * KD + k + 1)
                        return product3(pe, PS[0:NR, 0, :], WR_HI[:, k, :], WR_LO[:, k, :], HT_HI[:, k, :],
                                        HT_LO[:, k, :], k == 0, k == KD - 1)

                    pe.wait_ge(wr_lo, 1)
                    pe.wait_ge(x_added, 1 + NT)
                    for k in range(KD):
                        norm_block(2 * KD + k, k)
                        if k >= 2:
                            router(k - 2)
                    router(KD - 2)
                    router(KD - 1).then_inc(logits_t, 1)
                    pe.wait_ge(logits_sb, 1)
                    for i in range(NT):
                        ins = pe.transpose(PS[:, 1, 64 * i:64 * i + NR], LOGITS_T[:, P * i:P * (i + 1)], IDENT[0:NR, 0:NR])
                    ins.then_inc(logits, 1)
                    pe.wait_ge(ranks_in, 1)
                    chosen = B[:, 1, 256:256 + NE * NT]
                    pe.matmul(PS[:, 3, 0:NE * NT], C[:, C_BEFORE:C_BEFORE + P], chosen, start=True, stop=True)
                    for b in range(NT):
                        after = NT - b
                        ins = pe.matmul(PS[:, 3, NE * (b + 1):NE * (NT + 1)].rearrange("p (a n) -> p a n", n=NE),
                                        C[:, C_ONES:C_ONES + P],
                                        chosen[:, NE * b:NE * (b + 1)].unsqueeze(1).broadcast_to([P, after, NE]),
                                        start=False, stop=True, skip_group_check=True)
                    ins.then_inc(ranks, 1)

                    def transpose_tile(i, odd):
                        pe.wait_ge(xs_in[odd], 32 * (i + 1))
                        pe.wait_ge(xt_ready, 2 * i + odd)
                        for k in range(KD):
                            ins = pe.transpose(XT_PS[:, k // 4, k % 4, :],
                                               XS[odd].rearrange("p (m k) -> p m k", k=KD)[:, :, k],
                                               C[0:ROWS_T, C_IDENT:C_IDENT + ROWS_T])
                        ins.then_inc(xs_t, 1)

                    def parts(t, u, n):
                        pe.wait_ge(lo_done, t * OWN_UNITS + (MIX_UNITS + u + 1))
                        slot = (MIX_UNITS + u) % W_SLOTS
                        return (W_HI[:, slot, :].rearrange("p (k n) -> p k n", n=n),
                                W_LO[:, slot, :].rearrange("p (k n) -> p k n", n=n))

                    def gate_or_up(t, u0, bank):
                        for u in range(4):
                            w_hi, w_lo = parts(t, u0 + u, FE)
                            for kk in range(2):
                                k = 2 * u + kk
                                ins = product3(pe, PS[0:ROWS_T, bank, :], XT_HI[:, k, :], XT_LO[:, k, :],
                                               w_hi[:, kk, :], w_lo[:, kk, :], k == 0, k == KD - 1)
                            ins.then_inc(mm_done, 1)

                    def down(t, u0, n):
                        pe.wait_ge(at_lo, n + 1)
                        for k in range(KF):
                            w_hi, w_lo = parts(t, u0 + k, D)
                            for half in range(2):
                                cols = slice(512 * half, 512 * (half + 1))
                                ins = product3(pe, PS[0:ROWS_T, 2 + half, :], AT_HI[:, k, :], AT_LO[:, k, :],
                                               w_hi[:, 0, cols], w_lo[:, 0, cols], k == 0, k == KF - 1)
                            ins.then_inc(mm_done, 1)

                    def transpose_acted(t):
                        pe.wait_ge(act_done, t + 1)
                        for k in range(KF):
                            ins = pe.transpose(AT_PS[:, k, :], ACTED.rearrange("p (m k) -> p m k", k=KF)[:, :, k],
                                               C[0:ROWS_T, C_IDENT:C_IDENT + ROWS_T])
                        ins.then_inc(at_t, 1)

                    def first_tile(i):
                        t = 2 * i
                        pe.wait_ge(xt_ready, t + 1)
                        gate_or_up(t, 0, 0)
                        transpose_tile(i, 1)
                        gate_or_up(t, 4, 1)
                        transpose_acted(t)
                        pe.wait_ge(xt_ready, t + 2)
                        gate_or_up(t, 8, 0)

                    def tile(i, odd, more):
                        t = 2 * i + odd
                        transpose_tile(i + odd, 1 - odd)
                        gate_or_up(t, 0, 1)
                        down(t, 4, t - 1)
                        transpose_acted(t)
                        pe.wait_ge(xt_ready, t + 2)
                        if more:
                            gate_or_up(t, 8, 0)
                        else:
                            down(t, 8, t)

                    transpose_tile(0, 0)
                    first_tile(0)
                    tile(0, 1, True)
                    with pe.Fori(1, NE // 2 - 1) as i:
                        for odd in range(2):
                            tile(i, odd, True)
                    tile(NE // 2 - 1, 0, True)
                    tile(NE // 2 - 1, 1, False)
                    pe.wait_ge(table, 1)
                    n_more = pe.value_load(TILE_TAB[0:1, MORE:MORE + 1], min_val=0, max_val=MORE)
                    with pe.If(n_more > 0):
                        first_tile(NE // 2)
                        tile(NE // 2, 1, True)
                        with pe.Fori(NE // 2 + 1, TILES // 2 - 1) as i:
                            for odd in range(2):
                                tile(i, odd, True)
                        tile(TILES // 2 - 1, 0, True)
                        tile(TILES // 2 - 1, 1, False)

            nc.all_engine_barrier(sems_to_clear=range(first.num, last.num + 1))

        with nc.Block() as block:
            @block.vector
            def _(dve):
                dve.wait_ge(gfin_in, 16)
                for i in range(NT):
                    dve.scalar_tensor_tensor(ROWS[:, i, :], X[:, i, :], SS[:, i:i + 1], GROW[:], ALU.mult, ALU.mult) \
                       .then_inc(fin_rows, 1)

            @block.sync
            def _(sp):
                sp.dma_start(GROW[:], gfin_d.partition_broadcast(P)).then_inc(gfin_in, 16)
                for i in range(NT):
                    sp.wait_ge(fin_rows, i + 1)
                    sp.dma_start(out_d[i * P:(i + 1) * P, :], ROWS[:, i, :]).then_inc(out_stored, 16)
                sp.wait_ge(out_stored, 16 * NT)


def constants():
    c = np.zeros((P, C_COLS), np.float32)
    row, col = np.arange(P)[:, None], np.arange(P)[None, :]
    c[:, C_IDENT:C_IDENT + P] = row == col
    half = ROT // 2
    d_in, d_out, same = row % HD, col % HD, row // HD == col // HD
    c[:, C_ROT:C_ROT + P] = np.where(same & (d_out < half) & (d_in == d_out + half), -1.0, 0.0) + np.where(
        same & (d_out >= half) & (d_out < ROT) & (d_in == d_out - half), 1.0, 0.0)
    c[:, C_NEG:C_NEG + P] = np.where(col > row, NEG, 0.0)
    c[:, C_TRI8:C_TRI8 + P] = np.where(row >= col, -1.0 / SCALE, 0.0)
    c[:, C_ONE8:C_ONE8 + P] = -1.0 / SCALE
    c[:, C_LOW:C_LOW + P] = col >= row
    c[:, C_BEFORE:C_BEFORE + P] = row < col
    c[:, C_ONES:C_ONES + P] = 1.0
    freq = np.power(np.float32(THETA), -np.arange(half, dtype=np.float32) / np.float32(half)).astype(np.float32)
    d = np.arange(P) % HD
    c[:, C_FREQ] = np.where(d < ROT, freq[d % half], 0.0)
    c[:, C_IOTA:C_IOTA + NE] = np.arange(NE)
    c[:, C_GROUP:C_GROUP + NE] = np.arange(NE) // EPG
    c[:, C_LIMIT:C_LIMIT + MAX_R - 1] = ROWS_T * np.arange(1, MAX_R)
    return c


def kernel(x, positions, w_in, w_out, g_mix_norm, g_head_norm, g_gmlp_vnorm, w_spatial, b_spatial, g_ffn_norm,
           w_router_group, w_router_expert, w_expert_gate, w_expert_up, w_expert_down, g_final):
    import concourse.bacc as bacc
    from concourse.bass_utils import run_bass_kernel_spmd

    w_in, w_out = np.asarray(w_in), np.asarray(w_out)
    wsb, wmo = H_SB * HD, H_MOBA * HD
    rows = w_in.reshape(DEPTH, P, KD, -1)
    qa, ka, va, qb, kb, vb, uv = np.split(rows, np.cumsum([wsb] * 3 + [wmo] * 3), axis=-1)
    chunks = []
    for w in (uv, vb, va):
        n = w.shape[-1] * KD // CHUNK
        chunks += [w[:, :, c * (KD // n):(c + 1) * (KD // n)].reshape(DEPTH, P, CHUNK) for c in range(n)]
    for q, k in ((qa, ka), (qb, kb)):
        for c in range(q.shape[-1] // P):
            pair = np.stack([q[..., P * c:P * (c + 1)], k[..., P * c:P * (c + 1)]], axis=2)
            chunks.append(pair.reshape(DEPTH, P, CHUNK))
    out_rows = w_out.reshape(DEPTH, KD, P, D)[:, list(OUT_ORDER)].transpose(0, 2, 1, 3)
    for cols in (slice(0, 512), slice(512, D)):
        chunks += [out_rows[:, :, k:k + KD // 2, cols].reshape(DEPTH, P, CHUNK) for k in (0, KD // 2)]
    mix = np.ascontiguousarray(np.stack(chunks, axis=1)).reshape(DEPTH * MIX_CHUNKS, P, CHUNK)

    router = np.concatenate([np.asarray(w_router_group), np.asarray(w_router_expert)], axis=-1)
    lay = np.concatenate([
        np.asarray(g_mix_norm).reshape(DEPTH, P, KD),
        np.asarray(g_head_norm).reshape(DEPTH, KD, P).transpose(0, 2, 1),
        np.asarray(g_ffn_norm).reshape(DEPTH, P, KD),
        np.asarray(b_spatial).transpose(0, 2, 1),
        np.asarray(w_spatial).transpose(0, 3, 1, 2).reshape(DEPTH, P, H_GMLP * P),
        router.reshape(DEPTH, P, KD * NR),
    ], axis=-1)
    arrays = {
        "x": np.asarray(x).reshape(SEQ, D),
        "positions": np.asarray(positions).reshape(SEQ),
        "mix": mix,
        "lay": np.ascontiguousarray(lay),
        "g_vnorm": np.asarray(g_gmlp_vnorm).reshape(DEPTH, H_GMLP * HD),
        "g_ffn": np.asarray(g_ffn_norm),
        "w_gate": np.asarray(w_expert_gate),
        "w_up": np.asarray(w_expert_up),
        "w_down": np.asarray(w_expert_down),
        "g_final": np.asarray(g_final),
        "constants": constants(),
    }
    nc = bacc.Bacc("TRN2", target_bir_lowering=False, num_devices=1)
    ins = [nc.dram_tensor(n, a.shape, mybir.dt.from_np(a.dtype), kind="ExternalInput").ap() for n, a in arrays.items()]
    out = nc.dram_tensor("out", (SEQ, D), F32, kind="ExternalOutput").ap()
    build(nc, *ins, out)
    r = run_bass_kernel_spmd(nc, [arrays], core_ids=[0])
    return r.results[0]["out"].reshape(1, SEQ, D)
```
